# Optimizing a Trainium2 kernel written in Bass

```python
import math
import jax, jax.numpy as jnp
from jax import lax
import numpy as np

D_MODEL = 1024
BATCH = 1
SEQ = 256
DEPTH = 2

N_META = 16
BLOCK = 128
PAD = BLOCK - N_META
HEAD_DIM = 64
A_HEADS = 8
A_KV_HEADS = 2
WINDOW = 128
B_HEADS = 4
B_QK_DIM = 32
B_V_DIM = 64
C_GROUPS = 4
C_GROUP_DIM = 64
POOL_WINDOWS = (2, 4, 8, 16)
N_BUCKETS = 32
MAX_DISTANCE = 128
N_BIAS_HEADS = A_HEADS + B_HEADS
D_FF = 2816
N_EXPERTS = 8
TOP_K = 2
D_FF_EXPERT = 3584
EPS = 1e-6
NEG = -1e30

A_Q = A_HEADS * HEAD_DIM
A_KV = A_KV_HEADS * HEAD_DIM
B_QK = B_HEADS * 2 * B_QK_DIM
B_V = B_HEADS * B_V_DIM
C_W = C_GROUPS * C_GROUP_DIM
D_IN = A_Q + 2 * A_KV + 2 * B_QK + B_V + C_W
D_MIX = A_Q + B_V + C_W
N_DENSE = (DEPTH + 1) // 2
N_MOE = DEPTH // 2

kernel_name = "hybrid_swa_diffattn_pool_moe"

def rmsnorm(x, g):
    xf = x.astype(jnp.float32)
    y = xf * lax.rsqrt(jnp.mean(xf * xf, axis=-1, keepdims=True) + EPS)
    return (y * g.astype(jnp.float32)).astype(x.dtype)

def t5_bucket(n):
    max_exact = N_BUCKETS // 2
    nf = jnp.maximum(n, 1).astype(jnp.float32)
    large = max_exact + (jnp.log(nf / max_exact) / math.log(MAX_DISTANCE / max_exact)
                         * (N_BUCKETS - max_exact)).astype(jnp.int32)
    large = jnp.minimum(large, N_BUCKETS - 1)
    return jnp.where(n < max_exact, n, large)

def pad_front(t):
    return jnp.pad(t, ((0, 0), (PAD, 0)) + ((0, 0),) * (t.ndim - 2))

def sliding_window_attention(q, k, v, sinks, table_a):
    B, Lp = q.shape[:2]
    nb = Lp // BLOCK
    g = A_HEADS // A_KV_HEADS
    qb = q.reshape(B, nb, BLOCK, A_KV_HEADS, g, HEAD_DIM)

    def band(t):
        tp = jnp.pad(t, ((0, 0), (BLOCK, 0), (0, 0), (0, 0)))
        tp = tp.reshape(B, nb + 1, BLOCK, A_KV_HEADS, HEAD_DIM)
        return jnp.concatenate([tp[:, :-1], tp[:, 1:]], axis=2)

    kb, vb = band(k), band(v)
    a_idx = jnp.arange(BLOCK)[:, None]
    b_idx = jnp.arange(2 * BLOCK)[None, :]
    n = BLOCK + a_idx - b_idx
    in_win = (n >= 0) & (n < WINDOW)
    blk = jnp.arange(nb)[:, None, None]
    key_ok = (blk - 1) * BLOCK + b_idx[None] >= PAD
    mask = in_win[None] & key_ok
    bias = table_a[t5_bucket(jnp.maximum(n, 0))]
    bias = jnp.transpose(bias, (2, 0, 1)).reshape(A_KV_HEADS, g, BLOCK, 2 * BLOCK)

    s = jnp.einsum('bnqhgd,bnkhd->bnhgqk', qb, kb).astype(jnp.float32) * (HEAD_DIM ** -0.5)
    s = s + bias[None, None].astype(jnp.float32)
    s = jnp.where(mask[None, :, None, None], s, NEG)
    sink = jnp.broadcast_to(sinks.astype(jnp.float32).reshape(1, 1, A_KV_HEADS, g, 1, 1),
                            s.shape[:-1] + (1,))
    p = jax.nn.softmax(jnp.concatenate([s, sink], axis=-1), axis=-1)[..., :-1]
    o = jnp.einsum('bnhgqk,bnkhd->bnqhgd', p.astype(v.dtype), vb)
    return o.reshape(B, Lp, A_Q)

def diff_attention(q, k, v, table_b, lam, g_out, lam_init):
    B, Lp = q.shape[:2]
    nb = Lp // BLOCK
    scale = B_QK_DIM ** -0.5
    outs = []
    for i in range(nb):
        q0, kend = i * BLOCK, (i + 1) * BLOCK
        qi, kk, vv = q[:, q0:kend], k[:, :kend], v[:, :kend]
        s = jnp.einsum('bqhcd,bkhcd->bhcqk', qi, kk).astype(jnp.float32) * scale
        qpos = q0 + jnp.arange(BLOCK)
        kpos = jnp.arange(kend)
        n = qpos[:, None] - kpos[None, :]
        bias = table_b[t5_bucket(jnp.maximum(n, 0))]
        s = s + jnp.transpose(bias, (2, 0, 1))[None, :, None].astype(jnp.float32)
        mask = (n >= 0) & (kpos[None, :] >= PAD)
        s = jnp.where(mask, s, NEG)
        p = jax.nn.softmax(s, axis=-1)
        a = p[:, :, 0] - lam * p[:, :, 1]
        outs.append(jnp.einsum('bhqk,bkhd->bqhd', a.astype(v.dtype), vv))
    o = jnp.concatenate(outs, axis=1)
    o = rmsnorm(o, g_out) * (1.0 - lam_init)
    return o.reshape(B, Lp, B_V)

def multiscale_pool(u, w_pool, pool_scale):
    B, L, _ = u.shape
    ug = u.reshape(B, L, C_GROUPS, C_GROUP_DIM)
    t = jnp.arange(L)
    pooled = []
    for gi, w in enumerate(POOL_WINDOWS):
        xg = ug[:, :, gi].astype(jnp.float32)
        cs = jnp.concatenate([jnp.zeros((B, 1, C_GROUP_DIM), jnp.float32),
                              jnp.cumsum(xg, axis=1)], axis=1)
        lo = jnp.maximum(t + 1 - w, 0)
        cnt = jnp.minimum(t + 1, w).astype(jnp.float32)
        mean = (cs[:, 1:] - cs[:, lo]) / cnt[None, :, None]
        pooled.append(mean - xg)
    d = jnp.stack(pooled, axis=2).astype(u.dtype)
    y = jnp.einsum('blgc,gcd->blgd', d, w_pool).reshape(B, L, C_W)
    return y * pool_scale

def swiglu(h, wg, wu, wd):
    return (jax.nn.silu(h @ wg) * (h @ wu)) @ wd

def moe_swiglu(h, w_router, w_gate, w_up, w_down):
    B, L, D = h.shape
    t = h.reshape(-1, D)
    logits = (t @ w_router).astype(jnp.float32)
    top_v, top_i = lax.top_k(logits, TOP_K)
    gates = jax.nn.softmax(top_v, axis=-1)
    combine = jnp.sum(jax.nn.one_hot(top_i, N_EXPERTS, dtype=jnp.float32) * gates[..., None], axis=1)
    out = jnp.zeros_like(t)
    for e in range(N_EXPERTS):
        ye = swiglu(t, w_gate[e], w_up[e], w_down[e])
        out = out + combine[:, e:e + 1].astype(t.dtype) * ye
    return out.reshape(B, L, D)

def setup_inputs(seed: int = 0) -> dict:
    key = jax.random.key(seed)
    ks = jax.random.split(key, 24)
    f32 = jnp.float32
    nrm = lambda k, s, sc: jax.random.normal(k, s, f32) * sc
    return {
        "x": nrm(ks[0], (BATCH, SEQ, D_MODEL), 1.0),
        "meta_tokens": nrm(ks[1], (N_META, D_MODEL), 1.0),
        "rel_bias_table": nrm(ks[2], (N_BUCKETS, N_BIAS_HEADS), 0.5),
        "g_mix": 1.0 + nrm(ks[3], (DEPTH, D_MODEL), 0.05),
        "w_in": nrm(ks[4], (DEPTH, D_MODEL, D_IN), D_MODEL ** -0.5),
        "qk_gain_a": 1.0 + nrm(ks[5], (DEPTH, 2, HEAD_DIM), 0.05),
        "sinks": nrm(ks[6], (DEPTH, A_HEADS), 0.5),
        "qk_gain_b": 1.0 + nrm(ks[7], (DEPTH, 2, B_QK_DIM), 0.05),
        "diff_lambda": nrm(ks[8], (DEPTH, 4, B_QK_DIM), 0.1),
        "g_diff_out": 1.0 + nrm(ks[9], (DEPTH, B_V_DIM), 0.05),
        "w_pool": nrm(ks[10], (DEPTH, C_GROUPS, C_GROUP_DIM, C_GROUP_DIM), C_GROUP_DIM ** -0.5),
        "pool_scale": 1.0 + nrm(ks[11], (DEPTH, C_W), 0.1),
        "w_out": nrm(ks[12], (DEPTH, D_MIX, D_MODEL), D_MIX ** -0.5),
        "g_ffn": 1.0 + nrm(ks[13], (DEPTH, D_MODEL), 0.05),
        "w_ffn_gate": nrm(ks[14], (N_DENSE, D_MODEL, D_FF), D_MODEL ** -0.5),
        "w_ffn_up": nrm(ks[15], (N_DENSE, D_MODEL, D_FF), D_MODEL ** -0.5),
        "w_ffn_down": nrm(ks[16], (N_DENSE, D_FF, D_MODEL), D_FF ** -0.5),
        "w_router": nrm(ks[17], (N_MOE, D_MODEL, N_EXPERTS), D_MODEL ** -0.5),
        "w_exp_gate": nrm(ks[18], (N_MOE, N_EXPERTS, D_MODEL, D_FF_EXPERT), D_MODEL ** -0.5),
        "w_exp_up": nrm(ks[19], (N_MOE, N_EXPERTS, D_MODEL, D_FF_EXPERT), D_MODEL ** -0.5),
        "w_exp_down": nrm(ks[20], (N_MOE, N_EXPERTS, D_FF_EXPERT, D_MODEL), D_FF_EXPERT ** -0.5),
    }

def reference(x, meta_tokens, rel_bias_table, g_mix, w_in, qk_gain_a, sinks, qk_gain_b,
              diff_lambda, g_diff_out, w_pool, pool_scale, w_out, g_ffn, w_ffn_gate,
              w_ffn_up, w_ffn_down, w_router, w_exp_gate, w_exp_up, w_exp_down):
    B = x.shape[0]
    meta = jnp.broadcast_to(meta_tokens[None].astype(x.dtype), (B, N_META, D_MODEL))
    h_res = jnp.concatenate([meta, x], axis=1)
    L = h_res.shape[1]
    table_a = rel_bias_table[:, :A_HEADS]
    table_b = rel_bias_table[:, A_HEADS:]
    splits = list(np.cumsum([A_Q, A_KV, A_KV, B_QK, B_QK, B_V]))
    for l in range(DEPTH):
        h = rmsnorm(h_res, g_mix[l])
        z = h @ w_in[l]
        qa, ka, va, qb, kb, vb, uc = jnp.split(z, splits, axis=-1)
        qa = rmsnorm(qa.reshape(B, L, A_HEADS, HEAD_DIM), qk_gain_a[l, 0])
        ka = rmsnorm(ka.reshape(B, L, A_KV_HEADS, HEAD_DIM), qk_gain_a[l, 1])
        va = va.reshape(B, L, A_KV_HEADS, HEAD_DIM)
        o_a = sliding_window_attention(pad_front(qa), pad_front(ka), pad_front(va),
                                       sinks[l], table_a)[:, PAD:]
        qb = rmsnorm(qb.reshape(B, L, B_HEADS, 2, B_QK_DIM), qk_gain_b[l, 0])
        kb = rmsnorm(kb.reshape(B, L, B_HEADS, 2, B_QK_DIM), qk_gain_b[l, 1])
        vb = vb.reshape(B, L, B_HEADS, B_V_DIM)
        lam_init = 0.8 - 0.6 * math.exp(-0.3 * l)
        dl = diff_lambda[l].astype(jnp.float32)
        lam = jnp.exp(jnp.sum(dl[0] * dl[1])) - jnp.exp(jnp.sum(dl[2] * dl[3])) + lam_init
        o_b = diff_attention(pad_front(qb), pad_front(kb), pad_front(vb), table_b, lam,
                             g_diff_out[l], lam_init)[:, PAD:]
        o_c = multiscale_pool(uc, w_pool[l], pool_scale[l])
        mix = jnp.concatenate([o_a.astype(h.dtype), o_b.astype(h.dtype), o_c.astype(h.dtype)], axis=-1)
        h_res = h_res + mix @ w_out[l]
        h = rmsnorm(h_res, g_ffn[l])
        if l % 2 == 0:
            j = l // 2
            f = swiglu(h, w_ffn_gate[j], w_ffn_up[j], w_ffn_down[j])
        else:
            j = l // 2
            f = moe_swiglu(h, w_router[j], w_exp_gate[j], w_exp_up[j], w_exp_down[j])
        h_res = h_res + f
    return h_res[:, N_META:]


_drawn_inputs = setup_inputs


def setup_inputs(seed=0):
    import zlib

    import numpy as np

    out = dict(_drawn_inputs(seed))
    spreads = {}
    factors = {'qk_gain_a': 3.845, 'sinks': 17.196}
    for name, (base, spread) in spreads.items():
        noise = np.random.default_rng([zlib.crc32(name.encode()), seed]).standard_normal(out[name].shape)
        drawn = base * np.exp(spread * noise) if base else spread * noise
        out[name] = __import__('jax').numpy.asarray(drawn.astype(out[name].dtype))
    for name, factor in factors.items():
        out[name] = (out[name] * factor).astype(out[name].dtype)
    return out
```

```python
import math
from contextlib import ExitStack

import concourse.bass as bass
import numpy as np
from concourse import mybir

ALU = mybir.AluOpType
ACT = mybir.ActivationFunctionType
AX = mybir.AxisListType
F32 = mybir.dt.float32
I32 = mybir.dt.int32
U32 = mybir.dt.uint32

P = 128
D = 1024
KT = D // P
N_META = 16
SEQ = 256
T = N_META + SEQ
DEPTH = 2
HD = 64
A_HEADS, A_KV = 8, 2
B_HEADS, B_QK, B_V = 4, 32, 64
WINDOW = 128
POOL_WINDOWS = (2, 4, 8, 16)
N_BUCKETS, MAX_DISTANCE = 32, 128
N_BIAS = A_HEADS + B_HEADS
D_FF = 2816
N_EXPERTS = 8
D_FF_EXPERT = 3584
EPS = 1e-6
MASKED = 1e30

META, REAL0, REAL1 = 0, 1, 2
TOKENS = [(0, 16), (16, 144), (144, 272)]
N_DIST = T + P - 1

CHUNK = 2048
CW = 256
RING = 14
FF_STEPS = D_FF // CW
FF_TILES = D_FF // P
DOWN_PIECES = [(0, 8), (8, 16), (16, FF_TILES)]
EXP_STEPS = D_FF_EXPERT // CW
IN_CHUNKS = 7
OUT_CHUNKS = D // CW

CAP = 96
PASSES = -(-SEQ // CAP)

CONST_COLS = {}
PARAM_COLS = {}


def _columns(table, items):
    at = 0
    for name, n in items:
        table[name] = (at, n)
        at += n
    return at


N_CONST = _columns(CONST_COLS, [
    ("ident", P), ("mean_d", P), ("mean64", P), ("mean32", P), ("flip", P), ("before", P), ("ones", P),
    ("dup", 2 * P), ("iota", CAP), ("iota8", N_EXPERTS), ("inv_count", 2 * T), ("eps", 1)])
N_PARAM = _columns(PARAM_COLS, [
    ("g_mix", DEPTH * KT), ("g_ffn", DEPTH * KT), ("gain_a", DEPTH * 2), ("gain_b", DEPTH * 2),
    ("pool_scale", DEPTH * 2), ("sinks", DEPTH * A_HEADS), ("lam", DEPTH * 4 * B_QK),
    ("g_out", DEPTH * B_V), ("w_pool", DEPTH * 2 * P), ("router", KT * N_EXPERTS)])


def lam_init(l):
    return 0.8 - 0.6 * math.exp(-0.3 * l)


def query_tiles(l):
    return [META, REAL0, REAL1] if l < DEPTH - 1 else [REAL0, REAL1]


def key_tiles(group, qt):
    if qt == META:
        return [META]
    if qt == REAL0:
        return [META, REAL0]
    return [REAL0, REAL1] if group == "A" else [META, REAL0, REAL1]


def bias_column(qt):
    return TOKENS[REAL1][0] - TOKENS[qt][0]


def units(l):
    return [(g, qt, h) for g, n in (("A", A_HEADS), ("B", B_HEADS)) for qt in query_tiles(l) for h in range(n)]


LAG = 2
PROJECTIONS = ["qa0", "qa1", "qa2", "qa3", "ka0", "va0", "qb0", "qb1", "kb0", "kb1", "vb0", "vb1", "uc0", "uc1"]


def normed(name):
    return name[0] in "qk"


NORMED = [x for x in PROJECTIONS if normed(x)]


def first_token(l):
    return 0 if l < DEPTH - 1 else N_META


def unit_steps(l):
    u = units(l)

    def at(n):
        return u[n] if 0 <= n < len(u) else None

    def closed(n):
        x = at(n)
        return x[:2] if x and (n == len(u) - 1 or u[n + 1][:2] != x[:2]) else None

    for n in range(len(u) + LAG + 2):
        yield n, at(n), at(n - 1), at(n - LAG), closed(n - LAG - 1), closed(n - LAG - 2)


def groups(l):
    return [(g, qt) for g in "AB" for qt in query_tiles(l)]


SCORE_NO, B_NO, A_GROUP_NO, B_GROUP_NO = {}, {}, {}, {}
SCORE_OWNER = []
for _l in range(DEPTH):
    for _u in units(_l):
        for _i in range(1 + (_u[0] == "B")):
            SCORE_NO[_l, _u, _i] = len(SCORE_OWNER)
            SCORE_OWNER.append((_l, _u))
        if _u[0] == "B":
            B_NO[_l, _u] = len(B_NO)
    for _g in groups(_l):
        _no = A_GROUP_NO if _g[0] == "A" else B_GROUP_NO
        _no[_l, _g] = len(_no)
SCORE_SLOTS = 3
PROB_SLOTS = 8


def plan_banks():
    of, used, turn = {}, [0] * 8, [0, 0]

    def add(key):
        held = key[0] == "o"
        b = 6 + turn[1] % 2 if held else turn[0] % 6
        turn[held] += 1
        used[b] += 1
        of[key] = (b, used[b])

    for k in range(KT):
        add(("xt", k))
    add(("dist",))
    for l in range(DEPTH):
        add(("ms", l, 0))
        waiting = None
        for name in PROJECTIONS:
            add(("z", l, name))
            if waiting:
                add(("st", l, waiting))
            waiting = name if normed(name) else None
        add(("kd", l, 0))
        add(("kd", l, 1))
        if l == 0:
            for h in range(N_BIAS):
                add(("bias", h))
        for n, s, c, o, fin, tr in unit_steps(l):
            if s:
                for i in range(1 + (s[0] == "B")):
                    add(("s", l, s, i))
            if o:
                if o[2] == 0:
                    add(("o", l, o[:2]))
                add(("pt", l, o))
            if tr:
                add(("ot", l, tr))
        for j in range(2):
            add(("pool", l, j))
        for d in range(KT):
            add(("mix", l, d))
        add(("ms", l, 1))
        if l < DEPTH - 1:
            for f in range(FF_TILES):
                add(("g", f))
                add(("u", f))
            for d in range(KT):
                add(("down", d))
    for i in range(4):
        add(("ht", i))
    add(("logits",))
    add(("rank",))
    for i in range(4):
        add(("acc", i))
    return of, used


def plan_chunks():
    out = []
    for l in range(DEPTH):
        out += [("in", l, c) for c in range(IN_CHUNKS)]
        out += [("out", l, c) for c in range(OUT_CHUNKS)]
        if l < DEPTH - 1:
            out += [x for s in range(FF_STEPS) for x in (("gate", s), ("up", s))]
            out += [("down", c, p) for c in range(OUT_CHUNKS) for p in range(len(DOWN_PIECES))]
    return out


EXPERT_CHUNKS = []
for _s in range(EXP_STEPS):
    EXPERT_CHUNKS += [("gate", _s), ("up", _s)] + ([("down", _s - 1)] if _s else [])
EXPERT_CHUNKS.append(("down", EXP_STEPS - 1))


def build(nc, x, meta_tokens, bias_table, onehot, mask_row, consts, params, w_in, w_out, w_gate, w_up, w_down,
          e_gate, e_up, e_down, out, dist_dram):
    bank_of, bank_uses = plan_banks()
    chunks = plan_chunks()
    chunk_at = {c: n for n, c in enumerate(chunks)}
    assert len(chunks) % RING == 0 and len(EXPERT_CHUNKS) % RING == 0
    ring_base = len(chunks) // RING
    ring_per = len(EXPERT_CHUNKS) // RING

    with ExitStack() as ctx:
        def sb(name, shape, dt=F32):
            return ctx.enter_context(nc.sbuf_tensor(name, shape, dt))

        def sem(name):
            return ctx.enter_context(nc.semaphore(name))

        ring = sb("ring", [P, RING, CHUNK])
        X = sb("X", [P, KT, T])
        H = sb("H", [P, KT, T])
        cst = sb("cst", [P, N_CONST])
        par = sb("par", [P, N_PARAM])
        bias = sb("bias", [P, N_BIAS, T])
        work = sb("work", [P, (SCORE_SLOTS + PROB_SLOTS) * T + 2 * 3 * P])
        scores = work[:, 0:SCORE_SLOTS * T].rearrange("p (s t) -> p s t", s=SCORE_SLOTS)
        probs = work[:, SCORE_SLOTS * T:(SCORE_SLOTS + PROB_SLOTS) * T].rearrange("p (s t) -> p s t", s=PROB_SLOTS)
        probs_t = work[:, (SCORE_SLOTS + PROB_SLOTS) * T:].rearrange("p (s t) -> p s t", s=2)
        bias_rev = work[:, 0:N_BIAS * T].rearrange("p (h t) -> p h t", h=N_BIAS)
        rstd = sb("rstd", [P, 2, T])
        low = sb("low", [P, 6, 8])
        total = sb("total", [P, 6, 8])
        gap = sb("gap", [P, 6, 8])
        share = sb("share", [P, 6, 8])
        mean_o = sb("mean_o", [P, 6, 4])
        std_o = sb("std_o", [P, 6, 4])
        factor = sb("factor", [P, 2, B_HEADS])
        neg_sink = sb("neg_sink", [P, DEPTH * A_HEADS])
        gains = sb("gains", [P, DEPTH, 4])
        g_out = sb("g_out", [P, DEPTH, B_V])
        lam_t = sb("lam_t", [P, DEPTH, 2, B_QK])
        lam_s = sb("lam_s", [P, DEPTH * 4])
        ARENA = 8960
        arena = sb("arena", [P, ARENA])
        arena_at = [0]

        def part(shape):
            n = int(np.prod(shape[1:]))
            at = arena_at[0]
            arena_at[0] += n
            assert arena_at[0] <= ARENA, arena_at
            v = arena[:, at:at + n]
            if len(shape) == 3:
                v = v.rearrange("p (a b) -> p a b", a=shape[1])
            return v

        q_a = part([P, 4, T])
        k_a = part([P, T])
        k_dup = part([P, 2, T])
        q_b = part([P, 2, T])
        k_b = part([P, 2, T])
        v_all = part([P, 3, 2 * HD + B_HEADS * B_V])
        mix = part([P, KT, T])
        square = part([P, 2, T])
        PADDED = N_META + T
        pool_u = part([P, 2, PADDED])
        attention_end = arena_at[0]
        arena_at[0] = 0
        x_rows = part([P, 2, D])
        x_meta = part([P, D])
        arena_at[0] = attention_end
        hot = part([P, N_DIST])
        mrow = part([P, N_DIST])
        dist = part([P, N_DIST])
        tab = part([P, N_BIAS])
        arena_at[0] = 0
        hidden = part([P, FF_TILES, T])
        arena_at[0] = 0
        h_rows = part([P, 2, D])
        acc = part([P, 2, D])
        te = part([P, KT, CAP])
        pick = part([P, 2, CAP])
        gated_pick = part([P, 2, CAP])
        gate_t = part([P, SEQ])
        silu = part([P, 2, 2 * CAP])
        hid_t = part([P, 2, 2 * CAP])
        y_t = part([P, KT, CAP])
        y = part([P, D])
        route = part([P, 3, 2 * N_EXPERTS])
        cur = part([P, 3, 2])
        lg = part([P, 2, N_EXPERTS])
        top = part([P, 2, N_EXPERTS])
        idx = part([P, 2, N_EXPERTS])
        one = part([P, 2, N_EXPERTS])
        two = part([P, 2, N_EXPERTS])
        rt = part([P, 16])
        h_flat = H[:, :, :].rearrange("p k t -> p (k t)")
        pool_a = h_flat[:, 0:PADDED]
        pool_b = h_flat[:, PADDED:2 * PADDED]
        pool_d = h_flat[:, 2 * PADDED:2 * PADDED + 2 * T].rearrange("p (j t) -> p j t", j=2)
        heads = h_flat[:, 2 * PADDED + 2 * T:2 * PADDED + 2 * T + 2 * A_HEADS * HD].rearrange("p (m n) -> p m n", m=2)
        idx_u = sb("idx_u", [P, 2, N_EXPERTS], U32)
        most = sb("most", [P, 2], I32)

        ps = [ctx.enter_context(nc.psum_tensor(f"bank{b}", [P, 512], F32)) for b in range(8)]

        bank_full = [sem(f"bank_full{b}") for b in range(8)]
        bank_drained = [sem(f"bank_drained{b}") for b in range(8)]
        ring_full = [sem(f"ring_full{r}") for r in range(RING)]
        x_loaded = sem("x_loaded")
        consts_loaded = sem("consts_loaded")
        params_loaded = sem("params_loaded")
        dist_loaded = sem("dist_loaded")
        dist_stored = sem("dist_stored")
        bias_loaded = sem("bias_loaded")
        squares_act = sem("squares_act")
        squares_dve = sem("squares_dve")
        head_squares = sem("head_squares")
        dve_step = sem("dve_step")
        pool_step = sem("pool_step")
        h_ready = sem("h_ready")
        exp_ready = sem("exp_ready")
        sink_gap = sem("sink_gap")
        sink_exp = sem("sink_exp")
        probs_mixed = sem("probs_mixed")
        out_mean = sem("out_mean")
        out_std = sem("out_std")
        heads_ready = sem("heads_ready")
        pool_ready = sem("pool_ready")
        down_read = sem("down_read")
        lam_dot = sem("lam_dot")
        lam_exp = sem("lam_exp")
        gap_ready = sem("gap_ready")
        gap_exp = sem("gap_exp")
        mask_ready = sem("mask_ready")
        count_ready = sem("count_ready")
        rank_moved = sem("rank_moved")
        pick_ready = sem("pick_ready")
        e_down_read = sem("e_down_read")
        out_stored = sem("out_stored")

        def const(name, a=0, n=None):
            at, size = CONST_COLS[name]
            return cst[:, at + a:at + (size if n is None else a + n)]

        def param(name, a=0, n=None):
            at, size = PARAM_COLS[name]
            return par[:, at + a:at + (size if n is None else a + n)]

        def full(eng, key):
            b, n = bank_of[key]
            eng.wait_ge(bank_full[b], n)
            return ps[b]

        def drained(eng, key):
            b, n = bank_of[key]
            eng.wait_ge(bank_drained[b], n)

        def drain(ins, key):
            ins.then_inc(bank_drained[bank_of[key][0]], 1)

        def copy_probs(eng, copy, l, u, n):
            g, qt, h = u
            nq = TOKENS[qt][1] - TOKENS[qt][0]
            kts = key_tiles(g, qt)
            o = full(eng, ("pt", l, u))
            slot = probs_t[:, n % 2, :]
            ins = None
            if META in kts:
                ins = copy(slot[0:N_META, 0:nq], o[0:N_META, 0:nq])
            if kts[-1] != META:
                first = max(kts[0], REAL0)
                ins = copy(slot[:, first * P:(kts[-1] + 1) * P], o[:, first * P:(kts[-1] + 1) * P])
            drain(ins, ("pt", l, u))

        MISC = ["te0", "te1", "gt", "yt0", "yt1", "sc00", "sc01", "sc10", "sc11"]
        MISC_AT = {m: (6 + n % 2, n // 2) for n, m in enumerate(MISC)}
        MISC_USES = {6: (len(MISC) + 1) // 2, 7: len(MISC) // 2}
        moe_uses = [EXP_STEPS // 2] * 4 + [1, 1, MISC_USES[6], MISC_USES[7]]

        def moe_count(b, j, i):
            return i * moe_uses[b] + (bank_uses[b] + j + 1)

        def acc_done(i):
            b, j = MISC_AT["sc11"]
            return bank_drained[b], moe_count(b, j, i)

        block = ctx.enter_context(nc.Block())

        @block.sync
        def _(sp):
            sp.dma_start(x_meta[0:N_META, :], meta_tokens).then_inc(x_loaded, 16)
            sp.dma_start(x_rows, x[0].rearrange("(t p) d -> p t d", p=P)).then_inc(x_loaded, 16)

            def source(chunk):
                kind = chunk[0]
                if kind in ("in", "out", "gate", "up"):
                    w = {"in": w_in, "out": w_out, "gate": w_gate, "up": w_up}[kind]
                    l, c = chunk[1:] if len(chunk) == 3 else (0, chunk[1])
                    return w[l, :, c * CW:(c + 1) * CW].rearrange("(k p) n -> p k n", p=P)
                c, (k0, k1) = chunk[1], DOWN_PIECES[chunk[2]]
                return w_down[0, k0 * P:k1 * P, c * CW:(c + 1) * CW].rearrange("(k p) n -> p k n", p=P)

            def last_reader(chunk):
                kind = chunk[0]
                if kind == "in":
                    key = ("z", chunk[1], ["qa1", "qa3", "va0", "qb1", "kb1", "vb1", "uc1"][chunk[2]])
                elif kind == "out":
                    key = ("mix", chunk[1], 2 * chunk[2] + 1)
                elif kind in ("gate", "up"):
                    key = (kind[0], 2 * chunk[1] + 1)
                elif chunk[2] < 2:
                    return down_read, 2 * chunk[1] + chunk[2] + 1
                else:
                    key = ("down", 2 * chunk[1] + 1)
                b, n = bank_of[key]
                return bank_full[b], n

            for n, chunk in enumerate(chunks):
                if n >= RING:
                    sp.wait_ge(*last_reader(chunks[n - RING]))
                src = source(chunk)
                k = src.shape[1]
                dst = ring[:, n % RING, 0:k * CW].rearrange("p (k n) -> p k n", k=k)
                sp.dma_start(dst, src).then_inc(ring_full[n % RING], 16)

            def expert_source(kind, s, e):
                if kind == "down":
                    return e_down[0, e, s * CW:(s + 1) * CW, :].rearrange("(k p) n -> p k n", p=P)
                w = e_gate if kind == "gate" else e_up
                return w[0, e, :, s * CW:(s + 1) * CW].rearrange("(k p) n -> p k n", p=P)

            def expert_reader(n, i):
                kind, s = EXPERT_CHUNKS[n]
                if kind == "down" and s < EXP_STEPS - 1:
                    return e_down_read, i * (EXP_STEPS - 1) + (s + 1)
                if kind == "down":
                    return bank_full[5], moe_count(5, 0, i)
                b = s % 2 + (0 if kind == "gate" else 2)
                return bank_full[b], moe_count(b, s // 2, i)

            def stream_expert(i, e, first):
                for n, (kind, s) in enumerate(EXPERT_CHUNKS):
                    if n >= RING:
                        sp.wait_ge(*expert_reader(n - RING, i))
                    elif first:
                        sp.wait_ge(*last_reader(chunks[len(chunks) - RING + n]))
                    else:
                        sp.wait_ge(*expert_reader(len(EXPERT_CHUNKS) + n - RING, i - 1))
                    src = expert_source(kind, s, e)
                    dst = ring[:, n % RING, :].rearrange("p (k n) -> p k n", k=src.shape[1])
                    sp.dma_start(dst, src).then_inc(ring_full[n % RING], 16)

            stream_expert(0, 0, True)
            with sp.Fori(1, N_EXPERTS) as e:
                stream_expert(e, e, False)
            sp.wait_ge(count_ready, 1)
            count = sp.value_load(most[0:1, 0:1])
            with sp.If(count > CAP):
                with sp.Fori(1, PASSES) as p:
                    with sp.Fori(0, N_EXPERTS) as e:
                        stream_expert(p * N_EXPERTS + e, e, False)
                sp.wait_ge(*acc_done(PASSES * N_EXPERTS - 1))
            sp.wait_ge(*acc_done(N_EXPERTS - 1))
            for t in range(2):
                sp.dma_start(out[0, t * P:(t + 1) * P, :], acc[:, t, :]).then_inc(out_stored, 16)
            sp.wait_ge(out_stored, 32)

        @block.tensor
        def _(pe):
            def open_job(key):
                b, n = bank_of[key]
                if n > 1:
                    pe.wait_ge(bank_drained[b], n - 1)
                return ps[b]

            def close(ins, key):
                ins.then_inc(bank_full[bank_of[key][0]], 1)

            def weights(chunk, n=CW):
                at = chunk_at[chunk]
                pe.wait_ge(ring_full[at % RING], 16 * (at // RING + 1))
                return ring[:, at % RING, :].rearrange("p (k n) -> p k n", n=n)

            ident = const("ident")
            pe.wait_ge(x_loaded, 32)
            pe.wait_ge(consts_loaded, 16)
            for k in range(KT):
                key = ("xt", k)
                o = open_job(key)
                cols = slice(k * P, (k + 1) * P)
                pe.transpose(o[:, 0:16], x_meta[0:N_META, cols], ident[0:N_META, 0:N_META])
                pe.transpose(o[:, 16:144], x_rows[:, 0, cols], ident)
                close(pe.transpose(o[:, 144:272], x_rows[:, 1, cols], ident), key)
            pe.wait_ge(dist_loaded, 48)
            key = ("dist",)
            o = open_job(key)
            close(pe.matmul(o[0:N_BIAS, 0:N_DIST], tab[0:N_BUCKETS, :], hot[0:N_BUCKETS, :], start=True, stop=True),
                  key)

            def mean_square(l, which):
                t0 = first_token(l) if which else 0
                key = ("ms", l, which)
                o = open_job(key)
                pe.wait_ge(squares_act, 2 * l + which + 1)
                for k in range(KT):
                    if k == KT // 2:
                        pe.wait_ge(squares_dve, 2 * l + which + 1)
                    ins = pe.matmul(o[:, t0:T], const("mean_d"), H[:, k, t0:T], start=k == 0, stop=k == KT - 1)
                close(ins, key)

            def h_ready_value(l, which, k):
                return (2 * l + which) * KT + k + 1

            def project(l, name):
                key = ("z", l, name)
                kind, j = name[:2], int(name[2])
                o = open_job(key)
                if kind in ("va", "vb"):
                    w = weights(("in", l, 2 if kind == "va" else 5))
                    if kind == "va":
                        places = [(META, 0), (REAL0, 128), (REAL1, 256)]
                        cols = slice(128, 256)
                    else:
                        places = [(META, 0), (REAL0, 256)] if j == 0 else [(REAL1, 0)]
                        cols = slice(0, 256)
                    for tile, at in places:
                        t0, t1 = TOKENS[tile]
                        for k in range(KT):
                            ins = pe.matmul(o[0:t1 - t0, at:at + cols.stop - cols.start], H[:, k, t0:t1],
                                            w[:, k, cols], start=k == 0, stop=k == KT - 1)
                else:
                    chunk, at = {"qa": (j // 2, j % 2), "ka": (2, 0), "qb": (3, j), "kb": (4, j), "uc": (6, j)}[kind]
                    w = weights(("in", l, chunk))
                    t0 = first_token(l) if kind[0] == "q" else 0
                    for k in range(KT):
                        if name == "qa0":
                            pe.wait_ge(h_ready, h_ready_value(l, 0, k))
                        ins = pe.matmul(o[:, t0:T], w[:, k, at * P:(at + 1) * P], H[:, k, t0:T],
                                        start=k == 0, stop=k == KT - 1)
                close(ins, key)

            def head_square(l, name):
                key = ("st", l, name)
                o = open_job(key)
                t0 = first_token(l) if name[0] == "q" else 0
                n = NORMED.index(name)
                pe.wait_ge(head_squares, l * len(NORMED) + n + 1)
                mean = const("mean64" if name[1] == "a" else "mean32")
                close(pe.matmul(o[:, t0:T], mean, square[:, n % 2, t0:T], start=True, stop=True), key)

            def scores_of(l, u):
                g, qt, h = u
                t0, t1 = TOKENS[qt]
                kts = key_tiles(g, qt)
                k0, k1 = TOKENS[kts[0]][0], TOKENS[kts[-1]][1]
                for i in range(1 + (g == "B")):
                    key = ("s", l, u, i)
                    o = open_job(key)
                    if g == "A":
                        r = slice(HD * (h % 2), HD * (h % 2) + HD)
                        ql, kr = q_a[r, h // 2, t0:t1], k_dup[r, h // 4, k0:k1]
                    else:
                        at = B_QK * (2 * (h % 2) + i)
                        r = slice(at, at + B_QK)
                        ql, kr = q_b[r, h // 2, t0:t1], k_b[r, h // 2, k0:k1]
                    close(pe.matmul(o[0:t1 - t0, 0:k1 - k0], ql, kr, start=True, stop=True), key)

            def output_of(l, u, n):
                g, qt, h = u
                nq = TOKENS[qt][1] - TOKENS[qt][0]
                kts = key_tiles(g, qt)
                key = ("pt", l, u)
                o = open_job(key)
                if g == "A":
                    pe.wait_ge(exp_ready, SCORE_NO[l, u, 0] + 1)
                else:
                    pe.wait_ge(probs_mixed, B_NO[l, u] + 1)
                pr = probs[:, SCORE_NO[l, u, 0] % PROB_SLOTS, :]
                at = 0
                for kt in kts:
                    k0, k1 = TOKENS[kt]
                    ins = pe.transpose(o[0:k1 - k0, kt * P:kt * P + nq], pr[0:nq, at:at + k1 - k0],
                                       ident[0:nq, 0:nq])
                    at += k1 - k0
                close(ins, key)

            def values_of(l, u, n):
                g, qt, h = u
                nq = TOKENS[qt][1] - TOKENS[qt][0]
                kts = key_tiles(g, qt)
                okey = ("o", l, u[:2])
                ob = ps[bank_of[okey][0]]
                if h == 0:
                    open_job(okey)
                drained(pe, ("pt", l, u))
                vcol = HD * (h // 4) if g == "A" else 2 * HD + B_V * h
                for m, kt in enumerate(kts):
                    rows = TOKENS[kt][1] - TOKENS[kt][0]
                    ins = pe.matmul(ob[0:nq, h * HD:(h + 1) * HD], probs_t[0:rows, n % 2, kt * P:kt * P + nq],
                                    v_all[0:rows, kt, vcol:vcol + HD], start=m == 0, stop=m == len(kts) - 1)
                if h == (A_HEADS if g == "A" else B_HEADS) - 1:
                    close(ins, okey)

            def transpose_heads(l, group):
                g, qt = group
                key = ("ot", l, group)
                nq = TOKENS[qt][1] - TOKENS[qt][0]
                o = open_job(key)
                m = groups(l).index(group)
                if g == "A":
                    drained(pe, ("o", l, group))
                else:
                    pe.wait_ge(heads_ready, B_GROUP_NO[l, group] + 1)
                for j in range(4 if g == "A" else 2):
                    ins = pe.transpose(o[:, j * P:j * P + nq], heads[0:nq, m % 2, j * P:(j + 1) * P],
                                       ident[0:nq, 0:nq])
                close(ins, key)

            for l in range(DEPTH):
                mean_square(l, 0)
                waiting = None
                for name in PROJECTIONS:
                    project(l, name)
                    if waiting:
                        head_square(l, waiting)
                    waiting = name if normed(name) else None
                drained(pe, ("z", l, "ka0"))
                for i in range(2):
                    key = ("kd", l, i)
                    o = open_job(key)
                    close(pe.matmul(o[:, 0:T], const("dup", i * P, P), k_a, start=True, stop=True), key)
                if l == 0:
                    pe.wait_ge(bias_loaded, 16)
                    for h in range(N_BIAS):
                        key = ("bias", h)
                        o = open_job(key)
                        close(pe.matmul(o[:, 0:T], const("flip"), bias_rev[:, h, :], start=True, stop=True), key)
                drained(pe, ("z", l, "kb1"))
                drained(pe, ("kd", l, 0))
                drained(pe, ("kd", l, 1))
                for name in ("va0", "vb0", "vb1"):
                    drained(pe, ("z", l, name))
                for n, s, c, o, fin, tr in unit_steps(l):
                    if s:
                        scores_of(l, s)
                    if o:
                        output_of(l, o, n)
                        values_of(l, o, n)
                    if tr:
                        transpose_heads(l, tr)
                for j in range(2):
                    key = ("pool", l, j)
                    o = open_job(key)
                    pe.wait_ge(pool_ready, 2 * l + j + 1)
                    close(pe.matmul(o[:, 0:T], param("w_pool", (2 * l + j) * P, P), pool_d[:, j, :],
                                    start=True, stop=True), key)
                for group in groups(l):
                    drained(pe, ("ot", l, group))
                for j in range(2):
                    drained(pe, ("pool", l, j))
                t0 = first_token(l)
                for d in range(KT):
                    key = ("mix", l, d)
                    o = open_job(key)
                    w = weights(("out", l, d // 2))
                    for k in range(KT):
                        ins = pe.matmul(o[:, t0:T], w[:, k, (d % 2) * P:(d % 2 + 1) * P], mix[:, k, t0:T],
                                        start=k == 0, stop=k == KT - 1)
                    close(ins, key)
                mean_square(l, 1)
                if l < DEPTH - 1:
                    for f in range(FF_TILES):
                        for which in ("gate", "up"):
                            key = (which[0], f)
                            o = open_job(key)
                            w = weights((which, f // 2))
                            for k in range(KT):
                                if f == 0 and which == "gate":
                                    pe.wait_ge(h_ready, h_ready_value(l, 1, k))
                                ins = pe.matmul(o[:, 0:T], w[:, k, (f % 2) * P:(f % 2 + 1) * P], H[:, k, :],
                                                start=k == 0, stop=k == KT - 1)
                            close(ins, key)
                    for c in range(OUT_CHUNKS):
                        keys = [("down", 2 * c), ("down", 2 * c + 1)]
                        o = [open_job(key) for key in keys]
                        for p, (k0, k1) in enumerate(DOWN_PIECES):
                            w = weights(("down", c, p))
                            for j in range(2):
                                for k in range(k0, k1):
                                    if c == 0 and j == 0:
                                        drained(pe, ("u", k))
                                    ins = pe.matmul(o[j][:, 0:T], w[:, k - k0, j * P:(j + 1) * P], hidden[:, k, :],
                                                    start=k == 0, stop=k == FF_TILES - 1)
                                if p == len(DOWN_PIECES) - 1:
                                    close(ins, keys[j])
                            if p < len(DOWN_PIECES) - 1:
                                ins.then_inc(down_read, 1)

            pe.wait_ge(h_ready, h_ready_value(DEPTH - 1, 1, KT - 1))

            def rows_of(src, name):
                for i in range(4):
                    key = (name, i)
                    o = open_job(key)
                    for j in range(4):
                        k = 4 * (i % 2) + j
                        t0, t1 = TOKENS[1 + i // 2]
                        ins = pe.transpose(o[:, j * P:(j + 1) * P], src[:, k, t0:t1], ident)
                    close(ins, key)

            rows_of(H, "ht")
            key = ("logits",)
            o = open_job(key)
            for t in range(2):
                t0, t1 = TOKENS[1 + t]
                for k in range(KT):
                    ins = pe.matmul(o[:, t * N_EXPERTS:(t + 1) * N_EXPERTS], H[:, k, t0:t1],
                                    param("router", k * N_EXPERTS, N_EXPERTS), start=k == 0, stop=k == KT - 1)
            close(ins, key)
            key = ("rank",)
            o = open_job(key)
            pe.wait_ge(mask_ready, 1)
            mask = [route[:, 0, t * N_EXPERTS:(t + 1) * N_EXPERTS] for t in range(2)]
            pe.matmul(o[:, 0:8], const("before"), mask[0], start=True, stop=True)
            pe.matmul(o[:, 8:16], const("ones"), mask[0], start=True, stop=False)
            pe.matmul(o[:, 8:16], const("before"), mask[1], start=False, stop=True)
            pe.matmul(o[:, 16:24], const("ones"), mask[0], start=True, stop=False)
            close(pe.matmul(o[:, 16:24], const("ones"), mask[1], start=False, stop=True), key)
            rows_of(X, "acc")
            for i in range(4):
                drained(pe, ("ht", i))

            def expert(i):
                def reopen(b, j):
                    pe.wait_ge(bank_drained[b], moe_count(b, j - 1, i))
                    return ps[b]

                def chunk(n):
                    pe.wait_ge(ring_full[n % RING], (i * ring_per + (ring_base + n // RING + 1)) * 16)
                    return ring[:, n % RING, :]

                at = [0]

                def next_chunk():
                    at[0] += 1
                    return chunk(at[0] - 1)

                pe.wait_ge(pick_ready, i * 2 + 1)
                for half in range(2):
                    b, j = MISC_AT[f"te{half}"]
                    o = reopen(b, j)
                    for m in range(4):
                        d = 4 * half + m
                        for t in range(2):
                            ins = pe.matmul(o[:, m * CAP:(m + 1) * CAP], h_rows[:, t, d * P:(d + 1) * P],
                                            pick[:, t, :], start=t == 0, stop=t == 1)
                    ins.then_inc(bank_full[b], 1)
                b, j = MISC_AT["gt"]
                o = reopen(b, j)
                pe.wait_ge(pick_ready, i * 2 + 2)
                for t in range(2):
                    ins = pe.transpose(o[0:CAP, t * P:(t + 1) * P], gated_pick[:, t, :], ident)
                ins.then_inc(bank_full[b], 1)
                for half in range(2):
                    b, j = MISC_AT[f"te{half}"]
                    pe.wait_ge(bank_drained[b], moe_count(b, j, i))

                def down(s):
                    w = next_chunk().rearrange("p (k n) -> p k n", n=D)
                    if s == 0:
                        reopen(4, 0)
                        reopen(5, 0)
                    pe.wait_ge(bank_drained[2 + s % 2], moe_count(2 + s % 2, s // 2, i))
                    for m in range(2):
                        for d in range(KT):
                            ins = pe.matmul(ps[4 + d // 4][:, (d % 4) * CAP:(d % 4 + 1) * CAP],
                                            w[:, m, d * P:(d + 1) * P], hid_t[:, s % 2, m * CAP:(m + 1) * CAP],
                                            start=(s == 0 and m == 0 and d % 4 == 0),
                                            stop=(s == EXP_STEPS - 1 and m == 1), skip_group_check=True)
                            if s == EXP_STEPS - 1 and m == 1 and d == 3:
                                ins.then_inc(bank_full[4], 1)
                    ins.then_inc(e_down_read if s < EXP_STEPS - 1 else bank_full[5], 1)

                for s in range(EXP_STEPS):
                    for which in range(2):
                        w = next_chunk().rearrange("p (k n) -> p k n", n=CW)
                        b = 2 * which + s % 2
                        o = reopen(b, s // 2)
                        for m in range(2):
                            for k in range(KT):
                                ins = pe.matmul(o[:, m * CAP:(m + 1) * CAP], w[:, k, m * P:(m + 1) * P], te[:, k, :],
                                                start=k == 0, stop=k == KT - 1)
                        ins.then_inc(bank_full[b], 1)
                    if s:
                        down(s - 1)
                down(EXP_STEPS - 1)
                for half in range(2):
                    b, j = MISC_AT[f"yt{half}"]
                    o = reopen(b, j)
                    pe.wait_ge(bank_drained[4 + half], moe_count(4 + half, 0, i))
                    for m in range(4):
                        ins = pe.transpose(o[0:CAP, m * P:(m + 1) * P], y_t[:, 4 * half + m, :], ident)
                    ins.then_inc(bank_full[b], 1)
                b, j = MISC_AT["gt"]
                pe.wait_ge(bank_drained[b], moe_count(b, j, i))
                for half in range(2):
                    b, j = MISC_AT[f"yt{half}"]
                    pe.wait_ge(bank_drained[b], moe_count(b, j, i))
                for t in range(2):
                    for half in range(2):
                        b, j = MISC_AT[f"sc{t}{half}"]
                        o = reopen(b, j)
                        pe.matmul(o[:, :], gate_t[0:CAP, t * P:(t + 1) * P], y[0:CAP, half * 512:(half + 1) * 512],
                                  start=True, stop=True).then_inc(bank_full[b], 1)

            with pe.Fori(0, N_EXPERTS) as e:
                expert(e)
            pe.wait_ge(count_ready, 1)
            count = pe.value_load(most[0:1, 0:1])
            with pe.If(count > CAP):
                with pe.Fori(N_EXPERTS, PASSES * N_EXPERTS) as i:
                    expert(i)

        @block.scalar
        def _(act):
            act.dma_start(cst[:, :], consts).then_inc(consts_loaded, 16)
            act.dma_start(tab[0:N_BUCKETS, :], bias_table).then_inc(dist_loaded, 16)
            act.dma_start(hot[0:N_BUCKETS, :], onehot).then_inc(dist_loaded, 16)
            act.dma_start(mrow[0:N_BIAS, :], mask_row).then_inc(dist_loaded, 16)
            act.dma_start(par[:, :], params).then_inc(params_loaded, 16)
            eps = const("eps")

            for k in range(KT // 2):
                o = full(act, ("xt", k))
                drain(nc.scalar.copy(X[:, k, :], o[:, 0:T]), ("xt", k))

            def norm(l, which):
                t0 = first_token(l) if which else 0
                if which:
                    drained(act, ("mix", l, KT // 2 - 1))
                elif l:
                    drained(act, ("down", KT // 2 - 1))
                else:
                    drained(act, ("xt", KT // 2 - 1))
                nc.scalar.activation(H[:, 0:KT // 2, t0:T], X[:, 0:KT // 2, t0:T], ACT.Square).then_inc(squares_act, 1)
                o = full(act, ("ms", l, which))
                drain(nc.scalar.activation(rstd[:, 0, t0:T], o[:, t0:T], ACT.Sqrt, bias=eps), ("ms", l, which))

            def head_std(l, name):
                n = NORMED.index(name)
                t0 = first_token(l) if name[0] == "q" else 0
                o = full(act, ("st", l, name))
                if n >= 2:
                    drained(act, ("z", l, NORMED[n - 2]))
                drain(nc.scalar.activation(rstd[:, n % 2, t0:T], o[:, t0:T], ACT.Sqrt, bias=eps),
                      ("st", l, name))

            for l in range(DEPTH):
                norm(l, 0)
                if l == 0:
                    act.wait_ge(lam_dot, 1)
                    nc.scalar.activation(lam_s[:, 0:2 * DEPTH], lam_s[:, 0:2 * DEPTH], ACT.Exp).then_inc(lam_exp, 1)
                waiting = None
                for name in PROJECTIONS:
                    key = ("z", l, name)
                    o = full(act, key)
                    if normed(name):
                        n = NORMED.index(name)
                        t0 = first_token(l) if name[0] == "q" else 0
                        if n >= 2:
                            full(act, ("st", l, NORMED[n - 2]))
                        nc.scalar.activation(square[:, n % 2, t0:T], o[:, t0:T], ACT.Square).then_inc(head_squares, 1)
                    elif name == "va0":
                        nc.scalar.copy(v_all[0:N_META, META, 0:128], o[0:N_META, 0:128])
                        drain(nc.scalar.copy(v_all[:, REAL0:REAL1 + 1, 0:128],
                                                    o[:, 128:384].rearrange("p (t n) -> p t n", t=2)), key)
                    elif name == "vb0":
                        nc.scalar.copy(v_all[0:N_META, META, 128:384], o[0:N_META, 0:256])
                        drain(nc.scalar.copy(v_all[:, REAL0, 128:384], o[:, 256:512]), key)
                    elif name == "vb1":
                        drain(nc.scalar.copy(v_all[:, REAL1, 128:384], o[:, 0:256]), key)
                    else:
                        drain(nc.scalar.copy(pool_u[:, int(name[2]), N_META:PADDED], o[:, 0:T]), key)
                    if waiting:
                        head_std(l, waiting)
                    waiting = name if normed(name) else None
                for i in range(2):
                    o = full(act, ("kd", l, i))
                    drain(nc.scalar.copy(k_dup[:, i, :], o[:, 0:T]), ("kd", l, i))
                if l == 0:
                    for h in range(0, N_BIAS, 2):
                        o = full(act, ("bias", h))
                        drain(nc.scalar.copy(bias[:, h, :], o[:, 0:T]), ("bias", h))
                gs = groups(l)
                for n, s, c, o_unit, fin, tr in unit_steps(l):
                    if s:
                        g, qt, h = s
                        nq = TOKENS[qt][1] - TOKENS[qt][0]
                        kts = key_tiles(g, qt)
                        nk = TOKENS[kts[-1]][1] - TOKENS[kts[0]][0]
                        m = gs.index(s[:2])
                        for i in range(1 + (g == "B")):
                            no = SCORE_NO[l, s, i]
                            col = h if g == "A" else 2 * h + i
                            drained(act, ("s", l, s, i))
                            if no >= PROB_SLOTS:
                                ol, ou = SCORE_OWNER[no - PROB_SLOTS]
                                full(act, ("pt", ol, ou))
                            nc.scalar.activation(probs[0:nq, no % PROB_SLOTS, 0:nk], scores[0:nq, no % SCORE_SLOTS, 0:nk],
                                                 ACT.Exp, bias=low[0:nq, m, col:col + 1], scale=-1.0,
                                                 accum_out=total[0:nq, m, col:col + 1]).then_inc(exp_ready, 1)
                        if g == "A" and h == A_HEADS - 1:
                            act.wait_ge(sink_gap, A_GROUP_NO[l, s[:2]] + 1)
                            nc.scalar.activation(gap[0:nq, m, :], gap[0:nq, m, :], ACT.Exp).then_inc(sink_exp, 1)
                    if o_unit and o_unit[0] == "B":
                        copy_probs(act, nc.scalar.copy, l, o_unit, n)
                    if fin and fin[0] == "B":
                        nq = TOKENS[fin[1]][1] - TOKENS[fin[1]][0]
                        m = gs.index(fin)
                        act.wait_ge(out_mean, B_GROUP_NO[l, fin] + 1)
                        nc.scalar.activation(std_o[0:nq, m, :], mean_o[0:nq, m, :], ACT.Sqrt, bias=eps[0:nq],
                                             scale=1.0 / B_V).then_inc(out_std, 1)
                    if tr:
                        g, qt = tr
                        t0, t1 = TOKENS[qt]
                        o = full(act, ("ot", l, tr))
                        j0, nj = (0, 4) if g == "A" else (4, 2)
                        drain(nc.scalar.copy(
                            mix[:, j0:j0 + nj, t0:t1],
                            o[:, 0:nj * P].rearrange("p (j t) -> p j t", j=nj)[:, :, 0:t1 - t0]), ("ot", l, tr))
                for j in range(2):
                    o = full(act, ("pool", l, j))
                    drain(nc.scalar.activation(mix[:, 6 + j, :], o[:, 0:T], ACT.Copy,
                                                      scale=param("pool_scale", 2 * l + j, 1)), ("pool", l, j))
                norm(l, 1)
                if l < DEPTH - 1:
                    for f in range(FF_TILES):
                        o = full(act, ("g", f))
                        if f >= 2:
                            drained(act, ("u", f - 2))
                        drain(nc.scalar.activation(probs[:, f % 2, :], o[:, 0:T], ACT.Silu), ("g", f))

            for i in (0, 2):
                o = full(act, ("ht", i))
                drain(nc.scalar.copy(h_rows[:, i // 2, 0:512], o[:, :]), ("ht", i))
            act.wait_ge(gap_ready, 1)
            nc.scalar.activation(rt[:, 2:4], rt[:, 0:2], ACT.Exp).then_inc(gap_exp, 1)
            for i in (0, 2):
                o = full(act, ("acc", i))
                drain(nc.scalar.copy(acc[:, i // 2, 0:512], o[:, :]), ("acc", i))

            def expert(i):
                def taken(b, j):
                    act.wait_ge(bank_full[b], moe_count(b, j, i))
                    return ps[b]

                for s in range(EXP_STEPS):
                    o = taken(s % 2, s // 2)
                    if s >= 2:
                        act.wait_ge(bank_drained[2 + s % 2], moe_count(2 + s % 2, s // 2 - 1, i))
                    nc.scalar.activation(silu[:, s % 2, :], o[:, 0:2 * CAP], ACT.Silu).then_inc(bank_drained[s % 2], 1)
                o = taken(4, 0)
                nc.scalar.copy(y_t[:, 0:4, :], o[:, 0:4 * CAP].rearrange("p (d c) -> p d c", d=4)).then_inc(
                    bank_drained[4], 1)
                b, j = MISC_AT["yt0"]
                o = taken(b, j)
                nc.scalar.copy(y[0:CAP, 0:512], o[0:CAP, :]).then_inc(bank_drained[b], 1)

            with act.Fori(0, N_EXPERTS) as e:
                expert(e)
            act.wait_ge(count_ready, 1)
            count = act.value_load(most[0:1, 0:1])
            with act.If(count > CAP):
                with act.Fori(N_EXPERTS, PASSES * N_EXPERTS) as i:
                    expert(i)

        @block.vector
        def _(dve):
            V = nc.vector
            dve_steps = [0]

            def step(ins):
                dve_steps[0] += 1
                ins.then_inc(dve_step, 1)
                dve.wait_ge(dve_step, dve_steps[0])

            for k in range(KT // 2, KT):
                o = full(dve, ("xt", k))
                drain(V.tensor_copy(X[:, k, :], o[:, 0:T]), ("xt", k))
            drained(dve, ("xt", KT - 1))

            def squares(l, which):
                t0 = first_token(l) if which else 0
                V.tensor_tensor(H[:, KT // 2:KT, t0:T], X[:, KT // 2:KT, t0:T], X[:, KT // 2:KT, t0:T],
                                ALU.mult).then_inc(squares_dve, 1)

            def norm(l, which):
                t0 = first_token(l) if which else 0
                drained(dve, ("ms", l, which))
                step(V.reciprocal(rstd[:, 0, t0:T], rstd[:, 0, t0:T]))
                gain = param("g_ffn" if which else "g_mix", l * KT, KT)
                for k in range(KT):
                    V.scalar_tensor_tensor(H[:, k, t0:T], X[:, k, t0:T], gain[:, k:k + 1], rstd[:, 0, t0:T],
                                           ALU.mult, ALU.mult).then_inc(h_ready, 1)

            def normalise(l, name):
                n = NORMED.index(name)
                t0 = first_token(l) if name[0] == "q" else 0
                gain = gains[:, l, ["qa", "ka", "qb", "kb"].index(name[:2]):][:, 0:1]
                dst = {"qa": q_a[:, int(name[2]), t0:T], "ka": k_a[:, t0:T], "qb": q_b[:, int(name[2]) % 2, t0:T],
                       "kb": k_b[:, int(name[2]) % 2, t0:T]}[name[:2]]
                drained(dve, ("st", l, name))
                step(V.reciprocal(rstd[:, n % 2, t0:T], rstd[:, n % 2, t0:T]))
                o = full(dve, ("z", l, name))
                drain(V.scalar_tensor_tensor(dst, o[:, t0:T], gain, rstd[:, n % 2, t0:T], ALU.mult, ALU.mult),
                      ("z", l, name))

            squares(0, 0)
            dve.wait_ge(params_loaded, 16)
            lam_p = param("lam").rearrange("p (l a b n) -> p l a b n", l=DEPTH, a=2, b=2)
            for l in range(DEPTH):
                ins = V.tensor_tensor(lam_t[:, l, :, :], lam_p[:, l, :, 0, :], lam_p[:, l, :, 1, :], ALU.mult)
            step(ins)
            V.tensor_reduce(lam_s[:, 0:2 * DEPTH], lam_t[:, :, :, :], AX.X, ALU.add).then_inc(lam_dot, 1)
            V.tensor_scalar(neg_sink[:, :], param("sinks"), -1.0, None, ALU.mult)
            for l in range(DEPTH):
                V.tensor_scalar(gains[:, l, 0:1], param("gain_a", 2 * l, 1), -(HD ** -0.5), None, ALU.mult)
                V.tensor_copy(gains[:, l, 1:2], param("gain_a", 2 * l + 1, 1))
                V.tensor_scalar(gains[:, l, 2:3], param("gain_b", 2 * l, 1), -(B_QK ** -0.5), None, ALU.mult)
                V.tensor_copy(gains[:, l, 3:4], param("gain_b", 2 * l + 1, 1))
                step(V.tensor_scalar(g_out[:, l, :], param("g_out", l * B_V, B_V), 1.0 - lam_init(l), None, ALU.mult))
            o = full(dve, ("dist",))
            drain(V.tensor_tensor(dist[0:N_BIAS, :], mrow[0:N_BIAS, :], o[0:N_BIAS, 0:N_DIST], ALU.subtract),
                  ("dist",))

            for l in range(DEPTH):
                norm(l, 0)
                if l == 0:
                    dve.wait_ge(lam_exp, 1)
                    for m in range(DEPTH):
                        step(V.tensor_tensor(lam_s[:, 2 * m + 1:2 * m + 2], lam_s[:, 2 * m + 1:2 * m + 2],
                                             lam_s[:, 2 * m:2 * m + 1], ALU.subtract))
                        step(V.tensor_scalar(lam_s[:, 4 + m:5 + m], lam_s[:, 2 * m + 1:2 * m + 2], -lam_init(m), None,
                                             ALU.add))
                for name in NORMED:
                    normalise(l, name)
                if l == 0:
                    for h in range(1, N_BIAS, 2):
                        o = full(dve, ("bias", h))
                        drain(V.tensor_copy(bias[:, h, :], o[:, 0:T]), ("bias", h))
                    for h in range(N_BIAS):
                        drained(dve, ("bias", h))
                gs = groups(l)
                for n, s, c, o_unit, fin, tr in unit_steps(l):
                    if s:
                        g, qt, h = s
                        nq = TOKENS[qt][1] - TOKENS[qt][0]
                        kts = key_tiles(g, qt)
                        k0, k1 = TOKENS[kts[0]][0], TOKENS[kts[-1]][1]
                        m = gs.index(s[:2])
                        j0 = bias_column(qt) + k0
                        head = h if g == "A" else A_HEADS + h
                        for i in range(1 + (g == "B")):
                            no = SCORE_NO[l, s, i]
                            col = h if g == "A" else 2 * h + i
                            o = full(dve, ("s", l, s, i))
                            if no >= SCORE_SLOTS:
                                dve.wait_ge(exp_ready, no - SCORE_SLOTS + 1)
                            start = neg_sink[0:nq, l * A_HEADS + h:l * A_HEADS + h + 1] if g == "A" else 3.0e38
                            drain(V.tensor_tensor_reduce(
                                scores[0:nq, no % SCORE_SLOTS, 0:k1 - k0], o[0:nq, 0:k1 - k0],
                                bias[0:nq, head, j0:j0 + k1 - k0], 1.0, start, ALU.add, ALU.min,
                                low[0:nq, m, col:col + 1]), ("s", l, s, i))
                        if g == "A" and h == A_HEADS - 1:
                            drained(dve, ("s", l, s, 0))
                            V.tensor_tensor(gap[0:nq, m, :], low[0:nq, m, :],
                                            neg_sink[0:nq, l * A_HEADS:(l + 1) * A_HEADS],
                                            ALU.subtract).then_inc(sink_gap, 1)
                    if c and c[0] == "B":
                        g, qt, h = c
                        nq = TOKENS[qt][1] - TOKENS[qt][0]
                        kts = key_tiles(g, qt)
                        nk = TOKENS[kts[-1]][1] - TOKENS[kts[0]][0]
                        m = gs.index(c[:2])
                        dve.wait_ge(exp_ready, SCORE_NO[l, c, 1] + 1)
                        step(V.reciprocal(share[0:nq, m, 2 * h:2 * h + 2], total[0:nq, m, 2 * h:2 * h + 2]))
                        f = factor[0:nq, l, h:h + 1]
                        step(V.scalar_tensor_tensor(f, share[0:nq, m, 2 * h + 1:2 * h + 2], lam_s[0:nq, 4 + l:5 + l],
                                                    total[0:nq, m, 2 * h:2 * h + 1], ALU.mult, ALU.mult))
                        p0 = probs[0:nq, SCORE_NO[l, c, 0] % PROB_SLOTS, 0:nk]
                        p1 = probs[0:nq, SCORE_NO[l, c, 1] % PROB_SLOTS, 0:nk]
                        V.scalar_tensor_tensor(p0, p1, f, p0, ALU.mult, ALU.add).then_inc(probs_mixed, 1)
                    if o_unit and o_unit[0] == "A":
                        copy_probs(dve, V.tensor_copy, l, o_unit, n)
                    if fin:
                        g, qt = fin
                        nq = TOKENS[qt][1] - TOKENS[qt][0]
                        m = gs.index(fin)
                        nh = A_HEADS if g == "A" else B_HEADS
                        hv = heads[0:nq, m % 2, 0:nh * HD].rearrange("p (h d) -> p h d", h=nh)
                        if m >= 2:
                            full(dve, ("ot", l, gs[m - 2]))
                        if g == "A":
                            dve.wait_ge(sink_exp, A_GROUP_NO[l, fin] + 1)
                            step(V.tensor_tensor(share[0:nq, m, :], total[0:nq, m, :], gap[0:nq, m, :], ALU.add))
                            step(V.reciprocal(share[0:nq, m, :], share[0:nq, m, :]))
                            sh = share[0:nq, m, :]
                        else:
                            sh = share[0:nq, m, :].rearrange("p (h c) -> p h c", c=2)[:, :, 0]
                        o = full(dve, ("o", l, fin))
                        ov = o[0:nq, 0:nh * HD].rearrange("p (h d) -> p h d", h=nh)
                        drain(V.tensor_tensor(hv, ov, sh.unsqueeze(2).to_broadcast([nq, nh, HD]), ALU.mult),
                              ("o", l, fin))
                        if g == "B":
                            drained(dve, ("o", l, fin))
                            tmp = square[0:nq, 0, 0:nh * HD].rearrange("p (h d) -> p h d", h=nh)
                            step(V.tensor_tensor(tmp, hv, hv, ALU.mult))
                            V.tensor_reduce(mean_o[0:nq, m, :], tmp, AX.X, ALU.add).then_inc(out_mean, 1)
                            dve.wait_ge(out_std, B_GROUP_NO[l, fin] + 1)
                            step(V.reciprocal(std_o[0:nq, m, :], std_o[0:nq, m, :]))
                            step(V.tensor_tensor(hv, hv, std_o[0:nq, m, :].unsqueeze(2).to_broadcast([nq, nh, HD]),
                                                 ALU.mult))
                            V.tensor_tensor(hv, hv, g_out[0:nq, l, :].unsqueeze(1).to_broadcast([nq, nh, HD]),
                                            ALU.mult).then_inc(heads_ready, 1)

                t0 = first_token(l)

                def residual(name, d):
                    key = (name, l, d) if name == "mix" else (name, d)
                    o = full(dve, key)
                    drain(V.tensor_tensor(X[:, d, t0:T], X[:, d, t0:T], o[:, t0:T], ALU.add), key)

                for d in range(KT):
                    residual("mix", d)
                drained(dve, ("mix", l, KT - 1))
                squares(l, 1)
                norm(l, 1)
                if l < DEPTH - 1:
                    for f in range(FF_TILES):
                        drained(dve, ("g", f))
                        o = full(dve, ("u", f))
                        drain(V.tensor_tensor(hidden[:, f, :], probs[:, f % 2, :], o[:, 0:T], ALU.mult),
                              ("u", f))
                    for d in range(KT):
                        residual("down", d)
                    drained(dve, ("down", KT - 1))
                    squares(l + 1, 0)

            for i in (1, 3):
                o = full(dve, ("ht", i))
                drain(V.tensor_copy(h_rows[:, i // 2, 512:1024], o[:, :]), ("ht", i))
            o = full(dve, ("logits",))
            drain(V.tensor_copy(lg[:, :, :], o[:, 0:2 * N_EXPERTS].rearrange("p (t e) -> p t e", t=2)),
                  ("logits",))
            drained(dve, ("logits",))
            for t in range(2):
                step(V.max(top[:, t, :], lg[:, t, :]))
            V.tensor_tensor(rt[:, 0:2], top[:, :, 1], top[:, :, 0], ALU.subtract).then_inc(gap_ready, 1)
            for t in range(2):
                step(V.max_index(idx_u[:, t, :], top[:, t, :], lg[:, t, :]))
            step(V.tensor_copy(idx[:, :, :], idx_u[:, :, :]))
            for t in range(2):
                V.tensor_scalar(one[:, t, :], const("iota8"), idx[:, t, 0:1], None, ALU.is_equal)
                step(V.tensor_scalar(two[:, t, :], const("iota8"), idx[:, t, 1:2], None, ALU.is_equal))
            rv = route.rearrange("p a (t e) -> p a t e", t=2)
            V.tensor_tensor(rv[:, 0], one[:, :, :], two[:, :, :], ALU.add).then_inc(mask_ready, 1)
            dve.wait_ge(gap_exp, 1)
            step(V.tensor_scalar(rt[:, 4:6], rt[:, 2:4], 1.0, None, ALU.add))
            step(V.reciprocal(rt[:, 6:8], rt[:, 4:6]))
            step(V.tensor_tensor(rt[:, 8:10], rt[:, 6:8], rt[:, 2:4], ALU.mult))
            for t in range(2):
                step(V.tensor_scalar(rv[:, 2, t, :], one[:, t, :], rt[:, 6 + t:7 + t], None, ALU.mult))
                step(V.scalar_tensor_tensor(rv[:, 2, t, :], two[:, t, :], rt[:, 8 + t:9 + t], rv[:, 2, t, :],
                                            ALU.mult, ALU.add))
            o = full(dve, ("rank",))
            step(V.tensor_reduce(rt[:, 10:11], o[:, 16:24], AX.X, ALU.max))
            step(V.tensor_copy(most[:, 0:1], rt[:, 10:11]))
            drain(V.tensor_copy(rv[:, 1], o[:, 0:16].rearrange("p (t e) -> p t e", t=2)), ("rank",))
            drained(dve, ("rank",))
            for i in (1, 3):
                o = full(dve, ("acc", i))
                drain(V.tensor_copy(acc[:, i // 2, 512:1024], o[:, :]), ("acc", i))
            V.tensor_copy(rt[:, 11:12], rt[:, 10:11]).then_inc(count_ready, 1)
            for i in (0, 2):
                drained(dve, ("acc", i))

            steps_before = dve_steps[0]

            def expert(i, e):
                def taken(b, j):
                    dve.wait_ge(bank_full[b], moe_count(b, j, i))
                    return ps[b]

                V.tensor_copy(cur[:, :, :], rv[:, :, :, bass.ds(e, 1)].squeeze(3)).then_inc(dve_step, 1)
                dve.wait_ge(dve_step, i + (steps_before + 1))
                for which, dst in ((0, pick), (2, gated_pick)):
                    for t in range(2):
                        ins = V.tensor_scalar(dst[:, t, :], const("iota"), cur[:, 1, t:t + 1],
                                              cur[:, which, t:t + 1], ALU.is_equal, ALU.mult)
                    ins.then_inc(pick_ready, 1)
                for half in range(2):
                    b, j = MISC_AT[f"te{half}"]
                    o = taken(b, j)
                    V.tensor_copy(te[:, 4 * half:4 * half + 4, :],
                                  o[:, 0:4 * CAP].rearrange("p (d c) -> p d c", d=4)).then_inc(bank_drained[b], 1)
                b, j = MISC_AT["gt"]
                o = taken(b, j)
                V.tensor_copy(gate_t[0:CAP, :], o[0:CAP, 0:SEQ]).then_inc(bank_drained[b], 1)
                for s in range(EXP_STEPS):
                    b = 2 + s % 2
                    o = taken(b, s // 2)
                    dve.wait_ge(bank_drained[s % 2], moe_count(s % 2, s // 2, i))
                    V.tensor_tensor(hid_t[:, s % 2, :], silu[:, s % 2, :], o[:, 0:2 * CAP],
                                    ALU.mult).then_inc(bank_drained[b], 1)
                o = taken(5, 0)
                V.tensor_copy(y_t[:, 4:8, :], o[:, 0:4 * CAP].rearrange("p (d c) -> p d c", d=4)).then_inc(
                    bank_drained[5], 1)
                b, j = MISC_AT["yt1"]
                o = taken(b, j)
                V.tensor_copy(y[0:CAP, 512:1024], o[0:CAP, :]).then_inc(bank_drained[b], 1)
                for t in range(2):
                    for half in range(2):
                        b, j = MISC_AT[f"sc{t}{half}"]
                        o = taken(b, j)
                        a = acc[:, t, half * 512:(half + 1) * 512]
                        V.tensor_tensor(a, a, o[:, :], ALU.add).then_inc(bank_drained[b], 1)

            with dve.Fori(0, N_EXPERTS) as e:
                expert(e, e)
            count = dve.value_load(most[0:1, 0:1])
            with dve.If(count > CAP):
                with dve.Fori(1, PASSES) as p:
                    V.tensor_scalar(rv[:, 1], rv[:, 1], -float(CAP), None, ALU.add).then_inc(rank_moved, 1)
                    with dve.Fori(0, N_EXPERTS) as e:
                        dve.wait_ge(rank_moved, p)
                        expert(p * N_EXPERTS + e, e)

        @block.gpsimd
        def _(pool):
            G = nc.gpsimd
            pool_steps = [0]
            drained(pool, ("dist",))
            pool.dma_start(dist_dram, dist[0:N_BIAS, :]).then_inc(dist_stored, 16)
            pool.wait_ge(dist_stored, 16)
            pool.dma_start(bias_rev, bass.AP(tensor=dist_dram.tensor, offset=0,
                                             ap=[[1, P], [N_DIST, N_BIAS], [1, T]])).then_inc(bias_loaded, 16)
            pool.wait_ge(bias_loaded, 16)

            def step(ins):
                pool_steps[0] += 1
                ins.then_inc(pool_step, 1)
                pool.wait_ge(pool_step, pool_steps[0])

            def later(dst, src, shift, rows=slice(0, P)):
                step(G.tensor_tensor(dst[rows, N_META:PADDED], src[rows, N_META:PADDED],
                                     src[rows, N_META - shift:PADDED - shift], ALU.add))

            low_half, high_half = slice(0, P // 2), slice(P // 2, P)
            for l in range(DEPTH):
                drained(pool, ("z", l, "uc1"))
                for buf in (pool_a, pool_b, pool_u[:, 0], pool_u[:, 1]):
                    ins = G.memset(buf[:, 0:N_META], 0.0)
                step(ins)
                for j in range(2):
                    u = pool_u[:, j, :]
                    inv = const("inv_count", j * T, T)
                    later(pool_a, u, 1)
                    if j == 0:
                        later(pool_b, pool_a, 2, high_half)
                    else:
                        later(pool_b, pool_a, 2)
                        later(pool_a, pool_b, 4)
                        later(pool_b, pool_a, 8, high_half)
                    G.tensor_tensor(pool_d[low_half, j, :], pool_a[low_half, N_META:PADDED], inv[low_half], ALU.mult)
                    step(G.tensor_tensor(pool_d[high_half, j, :], pool_b[high_half, N_META:PADDED], inv[high_half],
                                         ALU.mult))
                    G.tensor_tensor(pool_d[:, j, :], pool_d[:, j, :], u[:, N_META:PADDED],
                                    ALU.subtract).then_inc(pool_ready, 1)


def bucket(n):
    exact = N_BUCKETS // 2
    if n < exact:
        return n
    large = exact + int(np.log(np.float32(n) / exact) / math.log(MAX_DISTANCE / exact) * (N_BUCKETS - exact))
    return min(large, N_BUCKETS - 1)


def shape_constants():
    c = np.zeros((P, N_CONST), np.float32)

    def put(name, v):
        at, n = CONST_COLS[name]
        c[:, at:at + n] = v

    i = np.arange(P)
    put("ident", np.eye(P))
    put("mean_d", np.full((P, P), 1.0 / D))
    put("mean64", (i[:, None] // HD == i[None] // HD) / HD)
    put("mean32", (i[:, None] // B_QK == i[None] // B_QK) / B_QK)
    put("flip", np.eye(P)[::-1])
    put("before", i[:, None] < i[None])
    put("ones", np.ones((P, P)))
    put("dup", np.concatenate([i[:, None] == HD * j + i[None] % HD for j in range(2)], 1))
    put("iota", np.arange(CAP)[None])
    put("iota8", np.arange(N_EXPERTS)[None])
    t = np.arange(T)
    w = np.array(POOL_WINDOWS)[np.arange(2 * P) // 64].reshape(2, P).T
    put("inv_count", (np.float32(1) / np.minimum(t[None, None] + 1, w[:, :, None]).astype(np.float32)).reshape(P, -1))
    put("eps", EPS)
    n = T - 1 - np.arange(N_DIST)
    b = np.array([bucket(max(x, 0)) for x in n])
    hot = (np.arange(N_BUCKETS)[:, None] == b[None]).astype(np.float32)
    seen = np.stack([(n >= 0) & (n < WINDOW)] * A_HEADS + [n >= 0] * B_HEADS)
    return c, hot, np.where(seen, 0.0, MASKED).astype(np.float32)


def pack_params(v):
    p = np.zeros((P, N_PARAM), np.float32)

    def put(name, a):
        at, n = PARAM_COLS[name]
        p[:, at:at + n] = a

    put("g_mix", v["g_mix"].reshape(DEPTH * KT, P).T)
    put("g_ffn", v["g_ffn"].reshape(DEPTH * KT, P).T)
    put("gain_a", np.tile(v["qk_gain_a"].reshape(DEPTH * 2, HD), (1, P // HD)).T)
    put("gain_b", np.tile(v["qk_gain_b"].reshape(DEPTH * 2, B_QK), (1, P // B_QK)).T)
    put("pool_scale", v["pool_scale"].reshape(DEPTH * 2, P).T)
    put("sinks", v["sinks"].reshape(1, -1))
    put("lam", v["diff_lambda"].reshape(1, -1))
    put("g_out", v["g_diff_out"].reshape(1, -1))
    w = np.zeros((2, HD, DEPTH, 2, 2, HD), np.float32)
    for g in range(2):
        w[g, :, :, :, g, :] = v["w_pool"].reshape(DEPTH, 2, 2, HD, HD)[:, :, g].transpose(2, 0, 1, 3)
    put("w_pool", w.reshape(P, -1))
    put("router", v["w_router"][0].reshape(KT, P, N_EXPERTS).transpose(1, 0, 2).reshape(P, -1))
    return p


def kernel(**inputs):
    import concourse.bacc as bacc
    from concourse.bass_utils import run_bass_kernel_spmd

    nc = bacc.Bacc("TRN2", target_bir_lowering=False, num_devices=1)
    v = {name: np.ascontiguousarray(a) for name, a in inputs.items()}
    consts, hot, mask_row = shape_constants()
    arrays, args = {}, []
    for name, a in (("x", v["x"]), ("meta_tokens", v["meta_tokens"]), ("rel_bias_table", v["rel_bias_table"]),
                    ("onehot", hot), ("mask_row", mask_row), ("consts", consts), ("params", pack_params(v)),
                    ("w_in", v["w_in"]), ("w_out", v["w_out"]), ("w_ffn_gate", v["w_ffn_gate"]),
                    ("w_ffn_up", v["w_ffn_up"]), ("w_ffn_down", v["w_ffn_down"]), ("w_exp_gate", v["w_exp_gate"]),
                    ("w_exp_up", v["w_exp_up"]), ("w_exp_down", v["w_exp_down"])):
        arrays[f"in_{name}"] = a
        args.append(nc.dram_tensor(f"in_{name}", a.shape, mybir.dt.from_np(a.dtype), kind="ExternalInput").ap())
    out = nc.dram_tensor("out_0", (1, SEQ, D), F32, kind="ExternalOutput").ap()
    dist_dram = nc.dram_tensor("dist_scratch", (N_BIAS, N_DIST), F32, kind="Internal").ap()
    build(nc, *args, out, dist_dram)
    r = run_bass_kernel_spmd(nc, [arrays], core_ids=[0])
    return r.results[0]["out_0"]
```

```python
import math
from contextlib import ExitStack

import concourse.bass as bass
import numpy as np
from concourse import mybir

ALU = mybir.AluOpType
ACT = mybir.ActivationFunctionType
AX = mybir.AxisListType
F32 = mybir.dt.float32
F32R = mybir.dt.float32r
I32 = mybir.dt.int32
U32 = mybir.dt.uint32

P = 128
D = 1024
KT = D // P
N_META = 16
SEQ = 256
T = N_META + SEQ
DEPTH = 2
HD = 64
A_HEADS, A_KV = 8, 2
B_HEADS, B_QK, B_V = 4, 32, 64
WINDOW = 128
POOL_WINDOWS = (2, 4, 8, 16)
N_BUCKETS, MAX_DISTANCE = 32, 128
N_BIAS = A_HEADS + B_HEADS
D_FF = 2816
N_EXPERTS = 8
D_FF_EXPERT = 3584
EPS = 1e-6
MASKED = 1e30

META, REAL0, REAL1 = 0, 1, 2
TOKENS = [(0, 16), (16, 144), (144, 272)]
N_DIST = T + P - 1

CHUNK = 2048
CW = 256
RING = 14
FF_STEPS = D_FF // CW
FF_TILES = D_FF // P
DOWN_PIECES = [(0, 8), (8, 16), (16, FF_TILES)]
IN_CHUNKS = 7
OUT_CHUNKS = D // CW

CAP = 128
PASSES = -(-SEQ // CAP)
UNIT = CHUNK // 2
WIDE = 512
EXP_STEPS = D_FF_EXPERT // WIDE
FF_PER_STEP = WIDE // P
SLOTS = 4

CONST_COLS = {}
PARAM_COLS = {}


def _columns(table, items):
    at = 0
    for name, n in items:
        table[name] = (at, n)
        at += n
    return at


N_CONST = _columns(CONST_COLS, [
    ("ident", P), ("mean_d", P), ("mean64", P), ("mean32", P), ("flip", P), ("before", P), ("ones", P),
    ("dup", 2 * P), ("iota", CAP), ("iota8", N_EXPERTS), ("inv_count", 2 * T), ("eps", 1)])
N_PARAM = _columns(PARAM_COLS, [
    ("g_mix", DEPTH * KT), ("g_ffn", DEPTH * KT), ("gain_a", DEPTH * 2), ("gain_b", DEPTH * 2),
    ("pool_scale", DEPTH * 2), ("sinks", DEPTH * A_HEADS), ("lam", DEPTH * 4 * B_QK),
    ("g_out", DEPTH * B_V), ("w_pool", DEPTH * 2 * P), ("router", KT * N_EXPERTS)])


def lam_init(l):
    return 0.8 - 0.6 * math.exp(-0.3 * l)


def query_tiles(l):
    return [META, REAL0, REAL1] if l < DEPTH - 1 else [REAL0, REAL1]


def key_tiles(group, qt):
    if qt == META:
        return [META]
    if qt == REAL0:
        return [META, REAL0]
    return [REAL0, REAL1] if group == "A" else [META, REAL0, REAL1]


def bias_column(qt):
    return TOKENS[REAL1][0] - TOKENS[qt][0]


def units(l):
    return [(g, qt, h) for g, n in (("A", A_HEADS), ("B", B_HEADS)) for qt in query_tiles(l) for h in range(n)]


LAG = 3
PROJECTIONS = ["qa0", "qa1", "qa2", "qa3", "ka0", "va0", "qb0", "qb1", "kb0", "kb1", "vb0", "vb1", "uc0", "uc1"]


def normed(name):
    return name[0] in "qk"


NORMED = [x for x in PROJECTIONS if normed(x)]


def first_token(l):
    return 0 if l < DEPTH - 1 else N_META


def unit_steps(l):
    u = units(l)

    def at(n):
        return u[n] if 0 <= n < len(u) else None

    def closed(n):
        x = at(n)
        return x[:2] if x and (n == len(u) - 1 or u[n + 1][:2] != x[:2]) else None

    for n in range(len(u) + LAG + 4):
        yield n, at(n), at(n - 2), at(n - LAG), at(n - LAG - 1), closed(n - LAG - 2), closed(n - LAG - 4)


def groups(l):
    return [(g, qt) for g in "AB" for qt in query_tiles(l)]


SCORE_NO, B_NO, A_GROUP_NO, B_GROUP_NO = {}, {}, {}, {}
SCORE_OWNER = []
for _l in range(DEPTH):
    for _u in units(_l):
        for _i in range(1 + (_u[0] == "B")):
            SCORE_NO[_l, _u, _i] = len(SCORE_OWNER)
            SCORE_OWNER.append((_l, _u))
        if _u[0] == "B":
            B_NO[_l, _u] = len(B_NO)
    for _g in groups(_l):
        _no = A_GROUP_NO if _g[0] == "A" else B_GROUP_NO
        _no[_l, _g] = len(_no)
SCORE_SLOTS = 4
PROB_SLOTS = 8


def plan_banks():
    of, used, turn = {}, [0] * 8, [0, 0]

    def add(key):
        held = key[0] == "o"
        b = 6 + turn[1] % 2 if held else turn[0] % 6
        turn[held] += 1
        used[b] += 1
        of[key] = (b, used[b])

    for k in range(KT):
        add(("xt", k))
    add(("dist",))
    for l in range(DEPTH):
        add(("ms", l, 0))
        waiting = None
        for name in PROJECTIONS:
            add(("z", l, name))
            if waiting:
                add(("st", l, waiting))
            waiting = name if normed(name) else None
        add(("kd", l, 0))
        add(("kd", l, 1))
        if l == 0:
            for h in range(N_BIAS):
                add(("bias", h))
        for n, s, c, o, v, fin, tr in unit_steps(l):
            if s:
                for i in range(1 + (s[0] == "B")):
                    add(("s", l, s, i))
            if o:
                add(("pt", l, o))
            if v and v[2] == 0:
                add(("o", l, v[:2]))
            if tr:
                add(("ot", l, tr))
        for j in range(2):
            add(("pool", l, j))
        for d in range(KT):
            add(("mix", l, d))
        add(("ms", l, 1))
        if l < DEPTH - 1:
            for f in range(FF_TILES):
                add(("g", f))
                add(("u", f))
            for d in range(KT):
                add(("down", d))
    for i in range(4):
        add(("ht", i))
    add(("logits",))
    add(("rank",))
    for i in range(4):
        add(("acc", i))
    add(("te", 0))
    add(("te", 1))
    return of, used


def plan_chunks():
    out = []
    for l in range(DEPTH):
        out += [("in", l, c) for c in range(IN_CHUNKS)]
        out += [("out", l, c) for c in range(OUT_CHUNKS)]
        if l < DEPTH - 1:
            out += [x for s in range(FF_STEPS) for x in (("gate", s), ("up", s))]
            out += [("down", c, p) for c in range(OUT_CHUNKS) for p in range(len(DOWN_PIECES))]
    return out


EXPERT_UNITS = []
for _s in range(EXP_STEPS):
    EXPERT_UNITS += [("gate", _s, _q) for _q in range(4)] + [("up", _s, _q) for _q in range(4)]
    if _s:
        EXPERT_UNITS += [("down", _s - 1, _q) for _q in range(4)]
EXPERT_UNITS += [("down", EXP_STEPS - 1, _q) for _q in range(4)]
N_UNITS = len(EXPERT_UNITS)
UNIT_AT = {u: n for n, u in enumerate(EXPERT_UNITS)}
N_CHUNKS = N_UNITS // 2
LAST_UNITS = [("down", EXP_STEPS - 1, 3)] + [(w, _s, 3) for w in ("gate", "up") for _s in range(EXP_STEPS)]
READ_COUNT = [sum(u not in LAST_UNITS for u in EXPERT_UNITS[:n + 1]) for n in range(N_UNITS)]

_last = EXP_STEPS - 1
EXPERT_JOBS = []
for _s in range(EXP_STEPS):
    EXPERT_JOBS.append((f"gate{_s}", _s % 2))
    if _s:
        EXPERT_JOBS.append((f"tr{_s - 1}", 6))
    EXPERT_JOBS.append((f"up{_s}", 2 + _s % 2))
    if _s == 1:
        EXPERT_JOBS += [("gt", 7), ("y0", 4), ("y1", 5)]
EXPERT_JOBS += [("te0", 7), ("te1", 6), (f"tr{_last}", 7), ("sc00", 1), ("sc01", 3), ("sc10", 0), ("sc11", 2)]
EXPERT_USES = [sum(b == x for _, x in EXPERT_JOBS) for b in range(8)]
EXPERT_JOB = {name: (b, sum(x == b for _, x in EXPERT_JOBS[:n])) for n, (name, b) in enumerate(EXPERT_JOBS)}
ROUNDS = PASSES * N_EXPERTS


def build(nc, x, meta_tokens, bias_table, onehot, mask_row, consts, params, w_in, w_out, w_gate, w_up, w_down,
          e_gate, e_up, e_down, out, dist_dram):
    bank_of, bank_uses = plan_banks()
    chunks = plan_chunks()
    chunk_at = {c: n for n, c in enumerate(chunks)}
    assert len(chunks) % RING == 0 and N_CHUNKS % RING == 0 and N_UNITS % SLOTS == 0
    ring_base = len(chunks) // RING
    ring_per = N_CHUNKS // RING

    with ExitStack() as ctx:
        def sb(name, shape, dt=F32):
            return ctx.enter_context(nc.sbuf_tensor(name, shape, dt))

        def sem(name):
            return ctx.enter_context(nc.semaphore(name))

        ring = sb("ring", [P, RING, CHUNK])
        cst = sb("cst", [P, N_CONST])
        par = sb("par", [P, N_PARAM])

        WORK = (SCORE_SLOTS + PROB_SLOTS) * T + 2 * 3 * P
        ARENA = 9184
        sizes = [N_BIAS * T, WORK, KT * T, KT * T, ARENA]
        region = -(-nc.sbuf_base // 32) * 32
        sb("region", [P, sum(sizes)])

        def place(name, shape, at, dt=F32):
            return nc.alloc_sbuf_tensor_at(name, shape, dt, offset=region + 4 * at)

        bias = place("bias", [P, N_BIAS, T], 0)
        work = place("work", [P, WORK], sizes[0])
        X = place("X", [P, KT, T], sum(sizes[:2]))
        H = place("H", [P, KT, T], sum(sizes[:3]))
        arena = place("arena", [P, ARENA], sum(sizes[:4]))
        w_hi = place("w_hi", [P, SLOTS, UNIT], 0, F32R)
        w_lo = place("w_lo", [P, SLOTS, UNIT], SLOTS * UNIT, F32R)
        te_hi = place("te_hi", [P, KT, CAP], sum(sizes[:3]), F32R)
        te_lo = place("te_lo", [P, KT, CAP], sum(sizes[:3]) + KT * CAP, F32R)
        hid_end = sum(sizes) - 4 * FF_PER_STEP * CAP
        hid_hi = place("hid_hi", [P, 2, FF_PER_STEP, CAP], hid_end, F32R)
        hid_lo = place("hid_lo", [P, 2, FF_PER_STEP, CAP], hid_end + 2 * FF_PER_STEP * CAP, F32R)
        scores = work[:, 0:SCORE_SLOTS * T].rearrange("p (s t) -> p s t", s=SCORE_SLOTS)
        probs = work[:, SCORE_SLOTS * T:(SCORE_SLOTS + PROB_SLOTS) * T].rearrange("p (s t) -> p s t", s=PROB_SLOTS)
        probs_t = work[:, (SCORE_SLOTS + PROB_SLOTS) * T:].rearrange("p (s t) -> p s t", s=2)
        bias_rev = work[:, 0:N_BIAS * T].rearrange("p (h t) -> p h t", h=N_BIAS)
        rstd = sb("rstd", [P, 2, T])
        neg_sink = sb("neg_sink", [P, DEPTH * A_HEADS])
        gains = sb("gains", [P, DEPTH, 4])
        g_out = sb("g_out", [P, DEPTH, B_V])
        lam_s = sb("lam_s", [P, DEPTH * 4])
        arena_at = [0]

        def part(shape):
            n = int(np.prod(shape[1:]))
            at = arena_at[0]
            arena_at[0] += n
            assert arena_at[0] <= ARENA, arena_at
            v = arena[:, at:at + n]
            if len(shape) == 3:
                v = v.rearrange("p (a b) -> p a b", a=shape[1])
            return v

        q_a = part([P, 4, T])
        k_a = part([P, T])
        k_dup = part([P, 2, T])
        q_b = part([P, 2, T])
        k_b = part([P, 2, T])
        v_all = part([P, 3, 2 * HD + B_HEADS * B_V])
        mix = part([P, KT, T])
        square = part([P, 2, T])
        PADDED = N_META + T
        pool_u = part([P, 2, PADDED])
        attention_end = arena_at[0]
        arena_at[0] = 0
        x_rows = part([P, 2, D])
        x_meta = part([P, D])
        arena_at[0] = attention_end
        hot = part([P, N_DIST])
        mrow = part([P, N_DIST])
        dist = part([P, N_DIST])
        tab = part([P, N_BIAS])
        prologue_end = arena_at[0]
        arena_at[0] = ARENA - 6 * 4 * 8 - 2 * 6 * 4 - DEPTH * B_HEADS - DEPTH * 2 * B_QK
        assert arena_at[0] >= prologue_end
        low = part([P, 6, 8])
        total = part([P, 6, 8])
        gap = part([P, 6, 8])
        share = part([P, 6, 8])
        mean_o = part([P, 6, 4])
        std_o = part([P, 6, 4])
        factor = part([P, DEPTH, B_HEADS])
        lam_t = part([P, DEPTH * 2, B_QK])
        arena_at[0] = 0
        hidden = part([P, FF_TILES, T])
        arena_at[0] = 0
        h_rows = part([P, 2, D])
        acc = part([P, 2, D])
        pick = part([P, 2, CAP])
        gated_pick = part([P, 2, CAP])
        gate_t = part([P, SEQ])
        silu = part([P, WIDE])
        hid = part([P, WIDE])
        y = part([P, D])
        route = part([P, 3, 2 * (ROUNDS + 1)])
        cur = part([P, 3, 2])
        lg = part([P, 2, N_EXPERTS])
        top = part([P, 2, N_EXPERTS])
        idx = part([P, 2, N_EXPERTS])
        one = part([P, 2, N_EXPERTS])
        two = part([P, 2, N_EXPERTS])
        rt = part([P, 16])
        assert sum(sizes[:4]) + arena_at[0] <= hid_end
        h_flat = H[:, :, :].rearrange("p k t -> p (k t)")
        pool_a = h_flat[:, 0:PADDED]
        pool_b = h_flat[:, PADDED:2 * PADDED]
        pool_d = h_flat[:, 2 * PADDED:2 * PADDED + 2 * T].rearrange("p (j t) -> p j t", j=2)
        heads = h_flat[:, 2 * PADDED + 2 * T:2 * PADDED + 2 * T + 2 * A_HEADS * HD].rearrange("p (m n) -> p m n", m=2)
        idx_u = sb("idx_u", [P, 2, N_EXPERTS], U32)
        most = sb("most", [P, 2], I32)

        ps = [ctx.enter_context(nc.psum_tensor(f"bank{b}", [P, 512], F32)) for b in range(8)]

        bank_full = [sem(f"bank_full{b}") for b in range(8)]
        bank_drained = [sem(f"bank_drained{b}") for b in range(8)]
        ring_full = [sem(f"ring_full{r}") for r in range(RING)]
        x_loaded = sem("x_loaded")
        consts_loaded = sem("consts_loaded")
        params_loaded = sem("params_loaded")
        dist_loaded = sem("dist_loaded")
        dist_stored = sem("dist_stored")
        bias_loaded = sem("bias_loaded")
        squares_act = sem("squares_act")
        squares_dve = sem("squares_dve")
        head_squares = sem("head_squares")
        dve_step = sem("dve_step")
        pool_step = sem("pool_step")
        h_ready = sem("h_ready")
        exp_ready = sem("exp_ready")
        sink_gap = sem("sink_gap")
        sink_exp = sem("sink_exp")
        probs_mixed = sem("probs_mixed")
        out_mean = sem("out_mean")
        out_std = sem("out_std")
        heads_ready = sem("heads_ready")
        pool_ready = sem("pool_ready")
        down_read = sem("down_read")
        lam_dot = sem("lam_dot")
        lam_exp = sem("lam_exp")
        gap_ready = sem("gap_ready")
        gap_exp = sem("gap_exp")
        mask_ready = sem("mask_ready")
        count_ready = sem("count_ready")
        pick_ready = sem("pick_ready")
        gates_picked = sem("gates_picked")
        unit_rounded = sem("unit_rounded")
        unit_split = sem("unit_split")
        unit_read = sem("unit_read")
        te_rounded = sem("te_rounded")
        hid_rounded = sem("hid_rounded")
        out_stored = sem("out_stored")

        def const(name, a=0, n=None):
            at, size = CONST_COLS[name]
            return cst[:, at + a:at + (size if n is None else a + n)]

        def param(name, a=0, n=None):
            at, size = PARAM_COLS[name]
            return par[:, at + a:at + (size if n is None else a + n)]

        def full(eng, key):
            b, n = bank_of[key]
            eng.wait_ge(bank_full[b], n)
            return ps[b]

        def drained(eng, key):
            b, n = bank_of[key]
            eng.wait_ge(bank_drained[b], n)

        def drain(ins, key):
            ins.then_inc(bank_drained[bank_of[key][0]], 1)

        def copy_probs(eng, copy, l, u, n):
            g, qt, h = u
            nq = TOKENS[qt][1] - TOKENS[qt][0]
            kts = key_tiles(g, qt)
            o = full(eng, ("pt", l, u))
            slot = probs_t[:, n % 2, :]
            ins = None
            if META in kts:
                ins = copy(slot[0:N_META, 0:nq], o[0:N_META, 0:nq])
            if kts[-1] != META:
                first = max(kts[0], REAL0)
                ins = copy(slot[:, first * P:(kts[-1] + 1) * P], o[:, first * P:(kts[-1] + 1) * P])
            drain(ins, ("pt", l, u))

        def expert_job(name, i, before=0):
            b, j = EXPERT_JOB[name]
            return b, i * EXPERT_USES[b] + (bank_uses[b] + j + 1 - before)

        def unit_weights(n):
            return ring[:, (n // 2) % RING, (n % 2) * UNIT:(n % 2 + 1) * UNIT]

        def acc_done(i):
            b, n = expert_job("sc11", i)
            return bank_drained[b], n

        def unit_free(n, i):
            if n < SLOTS:
                b, j = EXPERT_JOB["y1"]
                return bank_full[b], i * EXPERT_USES[b] + bank_uses[b]
            kind, s, q = EXPERT_UNITS[n - SLOTS]
            if EXPERT_UNITS[n - SLOTS] in LAST_UNITS:
                b, m = expert_job(f"{kind}{s}", i)
                return bank_full[b], m
            return unit_read, i * READ_COUNT[-1] + READ_COUNT[n - SLOTS]

        def turned(n):
            for s in range(EXP_STEPS):
                after = UNIT_AT["gate", s + 1, 3] if s < EXP_STEPS - 1 else UNIT_AT["down", s - 1, 2]
                if n == after + SLOTS - 1:
                    return s
            return None

        block = ctx.enter_context(nc.Block())

        @block.sync
        def _(sp):
            sp.dma_start(x_meta[0:N_META, :], meta_tokens).then_inc(x_loaded, 16)
            sp.dma_start(x_rows, x[0].rearrange("(t p) d -> p t d", p=P)).then_inc(x_loaded, 16)

            def source(chunk):
                kind = chunk[0]
                if kind in ("in", "out", "gate", "up"):
                    w = {"in": w_in, "out": w_out, "gate": w_gate, "up": w_up}[kind]
                    l, c = chunk[1:] if len(chunk) == 3 else (0, chunk[1])
                    return w[l, :, c * CW:(c + 1) * CW].rearrange("(k p) n -> p k n", p=P)
                c, (k0, k1) = chunk[1], DOWN_PIECES[chunk[2]]
                return w_down[0, k0 * P:k1 * P, c * CW:(c + 1) * CW].rearrange("(k p) n -> p k n", p=P)

            def last_reader(chunk):
                kind = chunk[0]
                if kind == "in":
                    key = ("z", chunk[1], ["qa1", "qa3", "va0", "qb1", "kb1", "vb1", "uc1"][chunk[2]])
                elif kind == "out":
                    key = ("mix", chunk[1], 2 * chunk[2] + 1)
                elif kind in ("gate", "up"):
                    key = (kind[0], 2 * chunk[1] + 1)
                elif chunk[2] < 2:
                    return down_read, 2 * chunk[1] + chunk[2] + 1
                else:
                    key = ("down", 2 * chunk[1] + 1)
                b, n = bank_of[key]
                return bank_full[b], n

            for n, chunk in enumerate(chunks):
                if n >= RING:
                    sp.wait_ge(*last_reader(chunks[n - RING]))
                src = source(chunk)
                k = src.shape[1]
                dst = ring[:, n % RING, 0:k * CW].rearrange("p (k n) -> p k n", k=k)
                sp.dma_start(dst, src).then_inc(ring_full[n % RING], 16)

            def expert_source(n, e):
                kind, s, q = EXPERT_UNITS[2 * n]
                if kind == "down":
                    r = s * WIDE + q * P
                    return e_down[0, e, r:r + 2 * P, :].rearrange("(k p) n -> p k n", p=P)
                w = e_gate if kind == "gate" else e_up
                return w[0, e, 2 * q * P:(2 * q + 4) * P, s * WIDE:(s + 1) * WIDE].rearrange("(k p) n -> p k n", p=P)

            def stream_expert(i, e, first):
                for n in range(N_CHUNKS):
                    if n >= RING:
                        sp.wait_ge(unit_split, i * N_UNITS + 2 * (n - RING) + 2)
                    elif first:
                        sp.wait_ge(*last_reader(chunks[len(chunks) - RING + n]))
                    else:
                        sp.wait_ge(unit_split, i * N_UNITS + (2 * (n - RING) + 2))
                    src = expert_source(n, e)
                    dst = ring[:, n % RING, :].rearrange("p (k n) -> p k n", k=src.shape[1])
                    sp.dma_start(dst, src).then_inc(ring_full[n % RING], 16)

            stream_expert(0, 0, True)
            with sp.Fori(1, N_EXPERTS) as e:
                stream_expert(e, e, False)
            sp.wait_ge(count_ready, 1)
            count = sp.value_load(most[0:1, 0:1])
            with sp.If(count > CAP):
                with sp.Fori(1, PASSES) as p:
                    with sp.Fori(0, N_EXPERTS) as e:
                        stream_expert(p * N_EXPERTS + e, e, False)
                sp.wait_ge(*acc_done(ROUNDS - 1))
            sp.wait_ge(*acc_done(N_EXPERTS - 1))
            for t in range(2):
                sp.dma_start(out[0, t * P:(t + 1) * P, :], acc[:, t, :]).then_inc(out_stored, 16)
            sp.wait_ge(out_stored, 32)

        @block.tensor
        def _(pe):
            def open_job(key):
                b, n = bank_of[key]
                if n > 1:
                    pe.wait_ge(bank_drained[b], n - 1)
                return ps[b]

            def close(ins, key):
                ins.then_inc(bank_full[bank_of[key][0]], 1)

            def weights(chunk, n=CW):
                at = chunk_at[chunk]
                pe.wait_ge(ring_full[at % RING], 16 * (at // RING + 1))
                return ring[:, at % RING, :].rearrange("p (k n) -> p k n", n=n)

            ident = const("ident")
            pe.wait_ge(x_loaded, 32)
            pe.wait_ge(consts_loaded, 16)
            for k in range(KT):
                key = ("xt", k)
                o = open_job(key)
                cols = slice(k * P, (k + 1) * P)
                pe.transpose(o[:, 0:16], x_meta[0:N_META, cols], ident[0:N_META, 0:N_META])
                pe.transpose(o[:, 16:144], x_rows[:, 0, cols], ident)
                close(pe.transpose(o[:, 144:272], x_rows[:, 1, cols], ident), key)
            pe.wait_ge(dist_loaded, 48)
            key = ("dist",)
            o = open_job(key)
            close(pe.matmul(o[0:N_BIAS, 0:N_DIST], tab[0:N_BUCKETS, :], hot[0:N_BUCKETS, :], start=True, stop=True),
                  key)

            def mean_square(l, which):
                t0 = first_token(l) if which else 0
                key = ("ms", l, which)
                o = open_job(key)
                pe.wait_ge(squares_act, 2 * l + which + 1)
                for k in range(KT):
                    if k == KT // 2:
                        pe.wait_ge(squares_dve, 2 * l + which + 1)
                    ins = pe.matmul(o[:, t0:T], const("mean_d"), H[:, k, t0:T], start=k == 0, stop=k == KT - 1)
                close(ins, key)

            def h_ready_value(l, which, k):
                return (2 * l + which) * KT + k + 1

            def project(l, name):
                key = ("z", l, name)
                kind, j = name[:2], int(name[2])
                o = open_job(key)
                if kind in ("va", "vb"):
                    w = weights(("in", l, 2 if kind == "va" else 5))
                    if kind == "va":
                        places = [(META, 0), (REAL0, 128), (REAL1, 256)]
                        cols = slice(128, 256)
                    else:
                        places = [(META, 0), (REAL0, 256)] if j == 0 else [(REAL1, 0)]
                        cols = slice(0, 256)
                    for tile, at in places:
                        t0, t1 = TOKENS[tile]
                        for k in range(KT):
                            ins = pe.matmul(o[0:t1 - t0, at:at + cols.stop - cols.start], H[:, k, t0:t1],
                                            w[:, k, cols], start=k == 0, stop=k == KT - 1)
                else:
                    chunk, at = {"qa": (j // 2, j % 2), "ka": (2, 0), "qb": (3, j), "kb": (4, j), "uc": (6, j)}[kind]
                    w = weights(("in", l, chunk))
                    t0 = first_token(l) if kind[0] == "q" else 0
                    for k in range(KT):
                        if name == "qa0":
                            pe.wait_ge(h_ready, h_ready_value(l, 0, k))
                        ins = pe.matmul(o[:, t0:T], w[:, k, at * P:(at + 1) * P], H[:, k, t0:T],
                                        start=k == 0, stop=k == KT - 1)
                close(ins, key)

            def head_square(l, name):
                key = ("st", l, name)
                o = open_job(key)
                t0 = first_token(l) if name[0] == "q" else 0
                n = NORMED.index(name)
                pe.wait_ge(head_squares, l * len(NORMED) + n + 1)
                mean = const("mean64" if name[1] == "a" else "mean32")
                close(pe.matmul(o[:, t0:T], mean, square[:, n % 2, t0:T], start=True, stop=True), key)

            def scores_of(l, u):
                g, qt, h = u
                t0, t1 = TOKENS[qt]
                kts = key_tiles(g, qt)
                k0, k1 = TOKENS[kts[0]][0], TOKENS[kts[-1]][1]
                for i in range(1 + (g == "B")):
                    key = ("s", l, u, i)
                    o = open_job(key)
                    if g == "A":
                        r = slice(HD * (h % 2), HD * (h % 2) + HD)
                        ql, kr = q_a[r, h // 2, t0:t1], k_dup[r, h // 4, k0:k1]
                    else:
                        at = B_QK * (2 * (h % 2) + i)
                        r = slice(at, at + B_QK)
                        ql, kr = q_b[r, h // 2, t0:t1], k_b[r, h // 2, k0:k1]
                    close(pe.matmul(o[0:t1 - t0, 0:k1 - k0], ql, kr, start=True, stop=True), key)

            def output_of(l, u):
                g, qt, h = u
                nq = TOKENS[qt][1] - TOKENS[qt][0]
                kts = key_tiles(g, qt)
                key = ("pt", l, u)
                o = open_job(key)
                if g == "A":
                    pe.wait_ge(exp_ready, SCORE_NO[l, u, 0] + 1)
                else:
                    pe.wait_ge(probs_mixed, B_NO[l, u] + 1)
                pr = probs[:, SCORE_NO[l, u, 0] % PROB_SLOTS, :]
                at = 0
                for kt in kts:
                    k0, k1 = TOKENS[kt]
                    ins = pe.transpose(o[0:k1 - k0, kt * P:kt * P + nq], pr[0:nq, at:at + k1 - k0],
                                       ident[0:nq, 0:nq])
                    at += k1 - k0
                close(ins, key)

            def values_of(l, u, n):
                g, qt, h = u
                nq = TOKENS[qt][1] - TOKENS[qt][0]
                kts = key_tiles(g, qt)
                okey = ("o", l, u[:2])
                ob = ps[bank_of[okey][0]]
                if h == 0:
                    open_job(okey)
                drained(pe, ("pt", l, u))
                vcol = HD * (h // 4) if g == "A" else 2 * HD + B_V * h
                for m, kt in enumerate(kts):
                    rows = TOKENS[kt][1] - TOKENS[kt][0]
                    ins = pe.matmul(ob[0:nq, h * HD:(h + 1) * HD], probs_t[0:rows, n % 2, kt * P:kt * P + nq],
                                    v_all[0:rows, kt, vcol:vcol + HD], start=m == 0, stop=m == len(kts) - 1)
                if h == (A_HEADS if g == "A" else B_HEADS) - 1:
                    close(ins, okey)

            def transpose_heads(l, group):
                g, qt = group
                key = ("ot", l, group)
                nq = TOKENS[qt][1] - TOKENS[qt][0]
                o = open_job(key)
                m = groups(l).index(group)
                if g == "A":
                    drained(pe, ("o", l, group))
                else:
                    pe.wait_ge(heads_ready, B_GROUP_NO[l, group] + 1)
                for j in range(4 if g == "A" else 2):
                    ins = pe.transpose(o[:, j * P:j * P + nq], heads[0:nq, m % 2, j * P:(j + 1) * P],
                                       ident[0:nq, 0:nq])
                close(ins, key)

            for l in range(DEPTH):
                mean_square(l, 0)
                waiting = None
                for name in PROJECTIONS:
                    project(l, name)
                    if waiting:
                        head_square(l, waiting)
                    waiting = name if normed(name) else None
                drained(pe, ("z", l, "ka0"))
                for i in range(2):
                    key = ("kd", l, i)
                    o = open_job(key)
                    close(pe.matmul(o[:, 0:T], const("dup", i * P, P), k_a, start=True, stop=True), key)
                if l == 0:
                    pe.wait_ge(bias_loaded, 16)
                    for h in range(N_BIAS):
                        key = ("bias", h)
                        o = open_job(key)
                        close(pe.matmul(o[:, 0:T], const("flip"), bias_rev[:, h, :], start=True, stop=True), key)
                drained(pe, ("z", l, "kb1"))
                drained(pe, ("kd", l, 0))
                drained(pe, ("kd", l, 1))
                for name in ("va0", "vb0", "vb1"):
                    drained(pe, ("z", l, name))
                for n, s, c, o, v, fin, tr in unit_steps(l):
                    if s:
                        scores_of(l, s)
                    if o:
                        output_of(l, o)
                    if v:
                        values_of(l, v, n - 1)
                    if tr:
                        transpose_heads(l, tr)
                for j in range(2):
                    key = ("pool", l, j)
                    o = open_job(key)
                    pe.wait_ge(pool_ready, 2 * l + j + 1)
                    close(pe.matmul(o[:, 0:T], param("w_pool", (2 * l + j) * P, P), pool_d[:, j, :],
                                    start=True, stop=True), key)
                for group in groups(l):
                    drained(pe, ("ot", l, group))
                for j in range(2):
                    drained(pe, ("pool", l, j))
                t0 = first_token(l)
                for d in range(KT):
                    key = ("mix", l, d)
                    o = open_job(key)
                    w = weights(("out", l, d // 2))
                    for k in range(KT):
                        ins = pe.matmul(o[:, t0:T], w[:, k, (d % 2) * P:(d % 2 + 1) * P], mix[:, k, t0:T],
                                        start=k == 0, stop=k == KT - 1)
                    close(ins, key)
                mean_square(l, 1)
                if l < DEPTH - 1:
                    for f in range(FF_TILES):
                        for which in ("gate", "up"):
                            key = (which[0], f)
                            o = open_job(key)
                            w = weights((which, f // 2))
                            for k in range(KT):
                                if f == 0 and which == "gate":
                                    pe.wait_ge(h_ready, h_ready_value(l, 1, k))
                                ins = pe.matmul(o[:, 0:T], w[:, k, (f % 2) * P:(f % 2 + 1) * P], H[:, k, :],
                                                start=k == 0, stop=k == KT - 1)
                            close(ins, key)
                    for c in range(OUT_CHUNKS):
                        keys = [("down", 2 * c), ("down", 2 * c + 1)]
                        o = [open_job(key) for key in keys]
                        for p, (k0, k1) in enumerate(DOWN_PIECES):
                            w = weights(("down", c, p))
                            for j in range(2):
                                for k in range(k0, k1):
                                    if c == 0 and j == 0:
                                        drained(pe, ("u", k))
                                    ins = pe.matmul(o[j][:, 0:T], w[:, k - k0, j * P:(j + 1) * P], hidden[:, k, :],
                                                    start=k == 0, stop=k == FF_TILES - 1)
                                if p == len(DOWN_PIECES) - 1:
                                    close(ins, keys[j])
                            if p < len(DOWN_PIECES) - 1:
                                ins.then_inc(down_read, 1)

            pe.wait_ge(h_ready, h_ready_value(DEPTH - 1, 1, KT - 1))

            def rows_of(src, name):
                for i in range(4):
                    key = (name, i)
                    o = open_job(key)
                    for j in range(4):
                        k = 4 * (i % 2) + j
                        t0, t1 = TOKENS[1 + i // 2]
                        ins = pe.transpose(o[:, j * P:(j + 1) * P], src[:, k, t0:t1], ident)
                    close(ins, key)

            rows_of(H, "ht")
            key = ("logits",)
            o = open_job(key)
            for t in range(2):
                t0, t1 = TOKENS[1 + t]
                for k in range(KT):
                    ins = pe.matmul(o[:, t * N_EXPERTS:(t + 1) * N_EXPERTS], H[:, k, t0:t1],
                                    param("router", k * N_EXPERTS, N_EXPERTS), start=k == 0, stop=k == KT - 1)
            close(ins, key)
            key = ("rank",)
            o = open_job(key)
            pe.wait_ge(mask_ready, 1)
            mask = [route[:, 0, t * (ROUNDS + 1):t * (ROUNDS + 1) + N_EXPERTS] for t in range(2)]
            pe.matmul(o[:, 0:8], const("before"), mask[0], start=True, stop=True)
            pe.matmul(o[:, 8:16], const("ones"), mask[0], start=True, stop=False)
            pe.matmul(o[:, 8:16], const("before"), mask[1], start=False, stop=True)
            pe.matmul(o[:, 16:24], const("ones"), mask[0], start=True, stop=False)
            close(pe.matmul(o[:, 16:24], const("ones"), mask[1], start=False, stop=True), key)
            rows_of(X, "acc")
            for i in range(4):
                drained(pe, ("ht", i))

            def gather(half, o):
                for m in range(4):
                    d = 4 * half + m
                    for t in range(2):
                        ins = pe.matmul(o[:, m * CAP:(m + 1) * CAP], h_rows[:, t, d * P:(d + 1) * P],
                                        pick[:, t, :], start=t == 0, stop=t == 1)
                return ins

            pe.wait_ge(pick_ready, 1)
            for half in range(2):
                key = ("te", half)
                close(gather(half, open_job(key)), key)
            for half in range(2):
                drained(pe, ("te", half))

            def expert(i):
                def reopen(name):
                    b, n = expert_job(name, i, before=1)
                    pe.wait_ge(bank_drained[b], n)
                    return ps[b]

                def ends(ins, name):
                    ins.then_inc(bank_full[EXPERT_JOB[name][0]], 1)

                def read_out(name):
                    b, n = expert_job(name, i)
                    pe.wait_ge(bank_drained[b], n)

                def unit(u):
                    n = UNIT_AT[u]
                    pe.wait_ge(unit_split, i * N_UNITS + (n + 1))
                    return w_hi[:, n % SLOTS, :], w_lo[:, n % SLOTS, :]

                def into(kind, s):
                    o = reopen(f"{kind}{s}")
                    for q in range(4):
                        hi, lo = unit((kind, s, q))
                        for m in range(2):
                            k = 2 * q + m
                            cols = slice(m * WIDE, (m + 1) * WIDE)
                            pe.matmul(o[:, :], te_hi[:, k, :], hi[:, cols], start=k == 0, stop=False)
                            pe.matmul(o[:, :], te_hi[:, k, :], lo[:, cols], start=False, stop=False)
                            ins = pe.matmul(o[:, :], te_lo[:, k, :], hi[:, cols], start=False, stop=k == KT - 1)
                        if q < 3:
                            ins.then_inc(unit_read, 1)
                    ends(ins, f"{kind}{s}")

                def turn(s):
                    o = reopen(f"tr{s}")
                    read_out(f"up{s}")
                    for m in range(FF_PER_STEP):
                        ins = pe.transpose(o[:, m * CAP:(m + 1) * CAP], hid[:, m * P:(m + 1) * P], ident)
                    ends(ins, f"tr{s}")

                def down(s, q):
                    if s == 0 and q == 0:
                        reopen("y0")
                        reopen("y1")
                    if q == 0:
                        read_out(f"tr{s}")
                    hi, lo = unit(("down", s, q))
                    last = s == EXP_STEPS - 1 and q == 3
                    for half in range(2):
                        o = ps[EXPERT_JOB[f"y{half}"][0]]
                        cols = slice(half * WIDE, (half + 1) * WIDE)
                        h_hi, h_lo = hid_hi[:, s % 2, q, :], hid_lo[:, s % 2, q, :]
                        pe.matmul(o[:, :], h_hi, hi[:, cols], start=s == 0 and q == 0, stop=False)
                        pe.matmul(o[:, :], h_hi, lo[:, cols], start=False, stop=False)
                        ins = pe.matmul(o[:, :], h_lo, hi[:, cols], start=False, stop=last)
                        if last:
                            ends(ins, f"y{half}")
                    if not last:
                        ins.then_inc(unit_read, 1)

                for s in range(EXP_STEPS):
                    into("gate", s)
                    if s:
                        turn(s - 1)
                    into("up", s)
                    if s == 1:
                        o = reopen("gt")
                        pe.wait_ge(gates_picked, i + 1)
                        for t in range(2):
                            ins = pe.transpose(o[:, t * P:(t + 1) * P], gated_pick[:, t, :], ident)
                        ends(ins, "gt")
                    if s == EXP_STEPS - 1:
                        pe.wait_ge(pick_ready, i + 2)
                        for half in range(2):
                            ends(gather(half, reopen(f"te{half}")), f"te{half}")
                    if s:
                        for q in range(4):
                            if s == EXP_STEPS - 1 and q == 3:
                                turn(s)
                            down(s - 1, q)
                for q in range(4):
                    down(EXP_STEPS - 1, q)
                read_out("gt")
                for half in range(2):
                    read_out(f"y{half}")
                for t in range(2):
                    for half in range(2):
                        o = reopen(f"sc{t}{half}")
                        ends(pe.matmul(o[:, :], gate_t[:, t * P:(t + 1) * P], y[:, half * WIDE:(half + 1) * WIDE],
                                       start=True, stop=True), f"sc{t}{half}")
                for half in range(2):
                    read_out(f"te{half}")

            with pe.Fori(0, N_EXPERTS) as e:
                expert(e)
            pe.wait_ge(count_ready, 1)
            count = pe.value_load(most[0:1, 0:1])
            with pe.If(count > CAP):
                with pe.Fori(N_EXPERTS, ROUNDS) as i:
                    expert(i)

        @block.scalar
        def _(act):
            act.dma_start(cst[:, :], consts).then_inc(consts_loaded, 16)
            act.dma_start(tab[0:N_BUCKETS, :], bias_table).then_inc(dist_loaded, 16)
            act.dma_start(hot[0:N_BUCKETS, :], onehot).then_inc(dist_loaded, 16)
            act.dma_start(mrow[0:N_BIAS, :], mask_row).then_inc(dist_loaded, 16)
            act.dma_start(par[:, :], params).then_inc(params_loaded, 16)
            eps = const("eps")

            for k in range(KT // 2):
                o = full(act, ("xt", k))
                drain(nc.scalar.copy(X[:, k, :], o[:, 0:T]), ("xt", k))

            def norm(l, which):
                t0 = first_token(l) if which else 0
                if which:
                    drained(act, ("mix", l, KT // 2 - 1))
                elif l:
                    drained(act, ("down", KT // 2 - 1))
                else:
                    drained(act, ("xt", KT // 2 - 1))
                nc.scalar.activation(H[:, 0:KT // 2, t0:T], X[:, 0:KT // 2, t0:T], ACT.Square).then_inc(squares_act, 1)
                o = full(act, ("ms", l, which))
                drain(nc.scalar.activation(rstd[:, 0, t0:T], o[:, t0:T], ACT.Sqrt, bias=eps), ("ms", l, which))

            def head_std(l, name):
                n = NORMED.index(name)
                t0 = first_token(l) if name[0] == "q" else 0
                o = full(act, ("st", l, name))
                if n >= 2:
                    drained(act, ("z", l, NORMED[n - 2]))
                drain(nc.scalar.activation(rstd[:, n % 2, t0:T], o[:, t0:T], ACT.Sqrt, bias=eps),
                      ("st", l, name))

            for l in range(DEPTH):
                norm(l, 0)
                if l == 0:
                    act.wait_ge(lam_dot, 1)
                    nc.scalar.activation(lam_s[:, 0:2 * DEPTH], lam_s[:, 0:2 * DEPTH], ACT.Exp).then_inc(lam_exp, 1)
                waiting = None
                for name in PROJECTIONS:
                    key = ("z", l, name)
                    o = full(act, key)
                    if normed(name):
                        n = NORMED.index(name)
                        t0 = first_token(l) if name[0] == "q" else 0
                        if n >= 2:
                            full(act, ("st", l, NORMED[n - 2]))
                        nc.scalar.activation(square[:, n % 2, t0:T], o[:, t0:T], ACT.Square).then_inc(head_squares, 1)
                    elif name == "va0":
                        nc.scalar.copy(v_all[0:N_META, META, 0:128], o[0:N_META, 0:128])
                        drain(nc.scalar.copy(v_all[:, REAL0:REAL1 + 1, 0:128],
                                                    o[:, 128:384].rearrange("p (t n) -> p t n", t=2)), key)
                    elif name == "vb0":
                        nc.scalar.copy(v_all[0:N_META, META, 128:384], o[0:N_META, 0:256])
                        drain(nc.scalar.copy(v_all[:, REAL0, 128:384], o[:, 256:512]), key)
                    elif name == "vb1":
                        drain(nc.scalar.copy(v_all[:, REAL1, 128:384], o[:, 0:256]), key)
                    else:
                        drain(nc.scalar.copy(pool_u[:, int(name[2]), N_META:PADDED], o[:, 0:T]), key)
                    if waiting:
                        head_std(l, waiting)
                    waiting = name if normed(name) else None
                for i in range(2):
                    o = full(act, ("kd", l, i))
                    drain(nc.scalar.copy(k_dup[:, i, :], o[:, 0:T]), ("kd", l, i))
                if l == 0:
                    for h in range(0, N_BIAS, 2):
                        o = full(act, ("bias", h))
                        drain(nc.scalar.copy(bias[:, h, :], o[:, 0:T]), ("bias", h))
                gs = groups(l)
                for n, s, c, o_unit, v, fin, tr in unit_steps(l):
                    if s:
                        g, qt, h = s
                        nq = TOKENS[qt][1] - TOKENS[qt][0]
                        kts = key_tiles(g, qt)
                        nk = TOKENS[kts[-1]][1] - TOKENS[kts[0]][0]
                        m = gs.index(s[:2])
                        for i in range(1 + (g == "B")):
                            no = SCORE_NO[l, s, i]
                            col = h if g == "A" else 2 * h + i
                            drained(act, ("s", l, s, i))
                            if no >= PROB_SLOTS:
                                ol, ou = SCORE_OWNER[no - PROB_SLOTS]
                                full(act, ("pt", ol, ou))
                            nc.scalar.activation(probs[0:nq, no % PROB_SLOTS, 0:nk], scores[0:nq, no % SCORE_SLOTS, 0:nk],
                                                 ACT.Exp, bias=low[0:nq, m, col:col + 1], scale=-1.0,
                                                 accum_out=total[0:nq, m, col:col + 1]).then_inc(exp_ready, 1)
                        if g == "A" and h == A_HEADS - 1:
                            act.wait_ge(sink_gap, A_GROUP_NO[l, s[:2]] + 1)
                            nc.scalar.activation(gap[0:nq, m, :], gap[0:nq, m, :], ACT.Exp).then_inc(sink_exp, 1)
                    if o_unit and o_unit[0] == "B":
                        copy_probs(act, nc.scalar.copy, l, o_unit, n)
                    if fin and fin[0] == "B":
                        nq = TOKENS[fin[1]][1] - TOKENS[fin[1]][0]
                        m = gs.index(fin)
                        act.wait_ge(out_mean, B_GROUP_NO[l, fin] + 1)
                        nc.scalar.activation(std_o[0:nq, m, :], mean_o[0:nq, m, :], ACT.Sqrt, bias=eps[0:nq],
                                             scale=1.0 / B_V).then_inc(out_std, 1)
                    if tr:
                        g, qt = tr
                        t0, t1 = TOKENS[qt]
                        o = full(act, ("ot", l, tr))
                        j0, nj = (0, 4) if g == "A" else (4, 2)
                        drain(nc.scalar.copy(
                            mix[:, j0:j0 + nj, t0:t1],
                            o[:, 0:nj * P].rearrange("p (j t) -> p j t", j=nj)[:, :, 0:t1 - t0]), ("ot", l, tr))
                for j in range(2):
                    o = full(act, ("pool", l, j))
                    drain(nc.scalar.activation(mix[:, 6 + j, :], o[:, 0:T], ACT.Copy,
                                                      scale=param("pool_scale", 2 * l + j, 1)), ("pool", l, j))
                norm(l, 1)
                if l < DEPTH - 1:
                    for f in range(FF_TILES):
                        o = full(act, ("g", f))
                        if f >= 2:
                            drained(act, ("u", f - 2))
                        drain(nc.scalar.activation(probs[:, f % 2, :], o[:, 0:T], ACT.Silu), ("g", f))

            for i in (0, 2):
                o = full(act, ("ht", i))
                drain(nc.scalar.copy(h_rows[:, i // 2, 0:512], o[:, :]), ("ht", i))
            act.wait_ge(gap_ready, 1)
            nc.scalar.activation(rt[:, 2:4], rt[:, 0:2], ACT.Exp).then_inc(gap_exp, 1)
            for i in (0, 2):
                o = full(act, ("acc", i))
                drain(nc.scalar.copy(acc[:, i // 2, 0:512], o[:, :]), ("acc", i))

            def round_te(half, o):
                nc.scalar.copy(te_hi[:, 4 * half:4 * half + 4, :],
                               o[:, :].rearrange("p (d c) -> p d c", d=4)).then_inc(te_rounded, 1)

            for half in range(2):
                round_te(half, full(act, ("te", half)))

            def expert(i):
                def taken(name):
                    b, n = expert_job(name, i)
                    act.wait_ge(bank_full[b], n)
                    return ps[b]

                for n, u in enumerate(EXPERT_UNITS):
                    if n % 2 == 0:
                        c = n // 2
                        act.wait_ge(ring_full[c % RING], (i * ring_per + (ring_base + c // RING + 1)) * 16)
                    act.wait_ge(*unit_free(n, i))
                    nc.scalar.copy(w_hi[:, n % SLOTS, :], unit_weights(n)).then_inc(unit_rounded, 1)
                    kind, s, q = EXPERT_UNITS[n - SLOTS + 1]
                    if n < SLOTS - 1:
                        continue
                    if kind == "gate" and q == 3:
                        o = taken(f"gate{s}")
                        if s:
                            b, m = expert_job(f"up{s - 1}", i)
                            act.wait_ge(bank_drained[b], m)
                        nc.scalar.activation(silu[:, :], o[:, :], ACT.Silu).then_inc(
                            bank_drained[EXPERT_JOB[f"gate{s}"][0]], 1)
                    if turned(n) is not None:
                        round_hidden(i, turned(n), taken)
                    if (kind, s, q) == ("down", EXP_STEPS - 2, 1):
                        for half in range(2):
                            round_te(half, taken(f"te{half}"))
                b = EXPERT_JOB["y0"][0]
                nc.scalar.copy(y[:, 0:WIDE], taken("y0")[:, :]).then_inc(bank_drained[b], 1)

            def round_hidden(i, s, taken):
                o = taken(f"tr{s}")
                nc.scalar.copy(hid_hi[:, s % 2, :, :], o[:, :].rearrange("p (m c) -> p m c", m=FF_PER_STEP)).then_inc(
                    hid_rounded, 1)

            with act.Fori(0, N_EXPERTS) as e:
                expert(e)
            act.wait_ge(count_ready, 1)
            count = act.value_load(most[0:1, 0:1])
            with act.If(count > CAP):
                with act.Fori(N_EXPERTS, ROUNDS) as i:
                    expert(i)

        @block.vector
        def _(dve):
            V = nc.vector
            dve_steps = [0]

            def step(ins):
                dve_steps[0] += 1
                ins.then_inc(dve_step, 1)
                dve.wait_ge(dve_step, dve_steps[0])

            for k in range(KT // 2, KT):
                o = full(dve, ("xt", k))
                drain(V.tensor_copy(X[:, k, :], o[:, 0:T]), ("xt", k))
            drained(dve, ("xt", KT - 1))

            def squares(l, which):
                t0 = first_token(l) if which else 0
                V.tensor_tensor(H[:, KT // 2:KT, t0:T], X[:, KT // 2:KT, t0:T], X[:, KT // 2:KT, t0:T],
                                ALU.mult).then_inc(squares_dve, 1)

            def norm(l, which):
                t0 = first_token(l) if which else 0
                drained(dve, ("ms", l, which))
                step(V.reciprocal(rstd[:, 0, t0:T], rstd[:, 0, t0:T]))
                gain = param("g_ffn" if which else "g_mix", l * KT, KT)
                for k in range(KT):
                    V.scalar_tensor_tensor(H[:, k, t0:T], X[:, k, t0:T], gain[:, k:k + 1], rstd[:, 0, t0:T],
                                           ALU.mult, ALU.mult).then_inc(h_ready, 1)

            def normalise(l, name):
                n = NORMED.index(name)
                t0 = first_token(l) if name[0] == "q" else 0
                gain = gains[:, l, ["qa", "ka", "qb", "kb"].index(name[:2]):][:, 0:1]
                dst = {"qa": q_a[:, int(name[2]), t0:T], "ka": k_a[:, t0:T], "qb": q_b[:, int(name[2]) % 2, t0:T],
                       "kb": k_b[:, int(name[2]) % 2, t0:T]}[name[:2]]
                drained(dve, ("st", l, name))
                step(V.reciprocal(rstd[:, n % 2, t0:T], rstd[:, n % 2, t0:T]))
                o = full(dve, ("z", l, name))
                drain(V.scalar_tensor_tensor(dst, o[:, t0:T], gain, rstd[:, n % 2, t0:T], ALU.mult, ALU.mult),
                      ("z", l, name))

            squares(0, 0)
            dve.wait_ge(params_loaded, 16)
            lam_p = param("lam").rearrange("p (l a b n) -> p l a b n", l=DEPTH, a=2, b=2)
            for l in range(DEPTH):
                ins = V.tensor_tensor(lam_t[:, 2 * l:2 * l + 2, :], lam_p[:, l, :, 0, :], lam_p[:, l, :, 1, :], ALU.mult)
            step(ins)
            V.tensor_reduce(lam_s[:, 0:2 * DEPTH], lam_t[:, :, :], AX.X, ALU.add).then_inc(lam_dot, 1)
            V.tensor_scalar(neg_sink[:, :], param("sinks"), -1.0, None, ALU.mult)
            for l in range(DEPTH):
                V.tensor_scalar(gains[:, l, 0:1], param("gain_a", 2 * l, 1), -(HD ** -0.5), None, ALU.mult)
                V.tensor_copy(gains[:, l, 1:2], param("gain_a", 2 * l + 1, 1))
                V.tensor_scalar(gains[:, l, 2:3], param("gain_b", 2 * l, 1), -(B_QK ** -0.5), None, ALU.mult)
                V.tensor_copy(gains[:, l, 3:4], param("gain_b", 2 * l + 1, 1))
                step(V.tensor_scalar(g_out[:, l, :], param("g_out", l * B_V, B_V), 1.0 - lam_init(l), None, ALU.mult))
            o = full(dve, ("dist",))
            drain(V.tensor_tensor(dist[0:N_BIAS, :], mrow[0:N_BIAS, :], o[0:N_BIAS, 0:N_DIST], ALU.subtract),
                  ("dist",))

            for l in range(DEPTH):
                norm(l, 0)
                if l == 0:
                    dve.wait_ge(lam_exp, 1)
                    for m in range(DEPTH):
                        step(V.tensor_tensor(lam_s[:, 2 * m + 1:2 * m + 2], lam_s[:, 2 * m + 1:2 * m + 2],
                                             lam_s[:, 2 * m:2 * m + 1], ALU.subtract))
                        step(V.tensor_scalar(lam_s[:, 4 + m:5 + m], lam_s[:, 2 * m + 1:2 * m + 2], -lam_init(m), None,
                                             ALU.add))
                for name in NORMED:
                    normalise(l, name)
                if l == 0:
                    for h in range(1, N_BIAS, 2):
                        o = full(dve, ("bias", h))
                        drain(V.tensor_copy(bias[:, h, :], o[:, 0:T]), ("bias", h))
                    for h in range(N_BIAS):
                        drained(dve, ("bias", h))
                gs = groups(l)
                for n, s, c, o_unit, v, fin, tr in unit_steps(l):
                    if s:
                        g, qt, h = s
                        nq = TOKENS[qt][1] - TOKENS[qt][0]
                        kts = key_tiles(g, qt)
                        k0, k1 = TOKENS[kts[0]][0], TOKENS[kts[-1]][1]
                        m = gs.index(s[:2])
                        j0 = bias_column(qt) + k0
                        head = h if g == "A" else A_HEADS + h
                        for i in range(1 + (g == "B")):
                            no = SCORE_NO[l, s, i]
                            col = h if g == "A" else 2 * h + i
                            o = full(dve, ("s", l, s, i))
                            if no >= SCORE_SLOTS:
                                dve.wait_ge(exp_ready, no - SCORE_SLOTS + 1)
                            start = neg_sink[0:nq, l * A_HEADS + h:l * A_HEADS + h + 1] if g == "A" else 3.0e38
                            drain(V.tensor_tensor_reduce(
                                scores[0:nq, no % SCORE_SLOTS, 0:k1 - k0], o[0:nq, 0:k1 - k0],
                                bias[0:nq, head, j0:j0 + k1 - k0], 1.0, start, ALU.add, ALU.min,
                                low[0:nq, m, col:col + 1]), ("s", l, s, i))
                        if g == "A" and h == A_HEADS - 1:
                            drained(dve, ("s", l, s, 0))
                            V.tensor_tensor(gap[0:nq, m, :], low[0:nq, m, :],
                                            neg_sink[0:nq, l * A_HEADS:(l + 1) * A_HEADS],
                                            ALU.subtract).then_inc(sink_gap, 1)
                    if c and c[0] == "B":
                        g, qt, h = c
                        nq = TOKENS[qt][1] - TOKENS[qt][0]
                        kts = key_tiles(g, qt)
                        nk = TOKENS[kts[-1]][1] - TOKENS[kts[0]][0]
                        m = gs.index(c[:2])
                        dve.wait_ge(exp_ready, SCORE_NO[l, c, 1] + 1)
                        step(V.reciprocal(share[0:nq, m, 2 * h:2 * h + 2], total[0:nq, m, 2 * h:2 * h + 2]))
                        f = factor[0:nq, l, h:h + 1]
                        step(V.scalar_tensor_tensor(f, share[0:nq, m, 2 * h + 1:2 * h + 2], lam_s[0:nq, 4 + l:5 + l],
                                                    total[0:nq, m, 2 * h:2 * h + 1], ALU.mult, ALU.mult))
                        p0 = probs[0:nq, SCORE_NO[l, c, 0] % PROB_SLOTS, 0:nk]
                        p1 = probs[0:nq, SCORE_NO[l, c, 1] % PROB_SLOTS, 0:nk]
                        V.scalar_tensor_tensor(p0, p1, f, p0, ALU.mult, ALU.add).then_inc(probs_mixed, 1)
                    if o_unit and o_unit[0] == "A":
                        copy_probs(dve, V.tensor_copy, l, o_unit, n)
                    if fin:
                        g, qt = fin
                        nq = TOKENS[qt][1] - TOKENS[qt][0]
                        m = gs.index(fin)
                        nh = A_HEADS if g == "A" else B_HEADS
                        hv = heads[0:nq, m % 2, 0:nh * HD].rearrange("p (h d) -> p h d", h=nh)
                        if m >= 2:
                            full(dve, ("ot", l, gs[m - 2]))
                        if g == "A":
                            dve.wait_ge(sink_exp, A_GROUP_NO[l, fin] + 1)
                            step(V.tensor_tensor(share[0:nq, m, :], total[0:nq, m, :], gap[0:nq, m, :], ALU.add))
                            step(V.reciprocal(share[0:nq, m, :], share[0:nq, m, :]))
                            sh = share[0:nq, m, :]
                        else:
                            sh = share[0:nq, m, :].rearrange("p (h c) -> p h c", c=2)[:, :, 0]
                        o = full(dve, ("o", l, fin))
                        ov = o[0:nq, 0:nh * HD].rearrange("p (h d) -> p h d", h=nh)
                        drain(V.tensor_tensor(hv, ov, sh.unsqueeze(2).to_broadcast([nq, nh, HD]), ALU.mult),
                              ("o", l, fin))
                        if g == "B":
                            drained(dve, ("o", l, fin))
                            tmp = square[0:nq, 0, 0:nh * HD].rearrange("p (h d) -> p h d", h=nh)
                            step(V.tensor_tensor(tmp, hv, hv, ALU.mult))
                            V.tensor_reduce(mean_o[0:nq, m, :], tmp, AX.X, ALU.add).then_inc(out_mean, 1)
                            dve.wait_ge(out_std, B_GROUP_NO[l, fin] + 1)
                            step(V.reciprocal(std_o[0:nq, m, :], std_o[0:nq, m, :]))
                            step(V.tensor_tensor(hv, hv, std_o[0:nq, m, :].unsqueeze(2).to_broadcast([nq, nh, HD]),
                                                 ALU.mult))
                            V.tensor_tensor(hv, hv, g_out[0:nq, l, :].unsqueeze(1).to_broadcast([nq, nh, HD]),
                                            ALU.mult).then_inc(heads_ready, 1)

                t0 = first_token(l)

                def residual(name, d):
                    key = (name, l, d) if name == "mix" else (name, d)
                    o = full(dve, key)
                    drain(V.tensor_tensor(X[:, d, t0:T], X[:, d, t0:T], o[:, t0:T], ALU.add), key)

                for d in range(KT):
                    residual("mix", d)
                drained(dve, ("mix", l, KT - 1))
                squares(l, 1)
                norm(l, 1)
                if l < DEPTH - 1:
                    for f in range(FF_TILES):
                        drained(dve, ("g", f))
                        o = full(dve, ("u", f))
                        drain(V.tensor_tensor(hidden[:, f, :], probs[:, f % 2, :], o[:, 0:T], ALU.mult),
                              ("u", f))
                    for d in range(KT):
                        residual("down", d)
                    drained(dve, ("down", KT - 1))
                    squares(l + 1, 0)

            for i in (1, 3):
                o = full(dve, ("ht", i))
                drain(V.tensor_copy(h_rows[:, i // 2, 512:1024], o[:, :]), ("ht", i))
            step(V.memset(route[:, :, :], 0.0))
            o = full(dve, ("logits",))
            drain(V.tensor_copy(lg[:, :, :], o[:, 0:2 * N_EXPERTS].rearrange("p (t e) -> p t e", t=2)),
                  ("logits",))
            drained(dve, ("logits",))
            for t in range(2):
                step(V.max(top[:, t, :], lg[:, t, :]))
            V.tensor_tensor(rt[:, 0:2], top[:, :, 1], top[:, :, 0], ALU.subtract).then_inc(gap_ready, 1)
            for t in range(2):
                step(V.max_index(idx_u[:, t, :], top[:, t, :], lg[:, t, :]))
            step(V.tensor_copy(idx[:, :, :], idx_u[:, :, :]))
            for t in range(2):
                V.tensor_scalar(one[:, t, :], const("iota8"), idx[:, t, 0:1], None, ALU.is_equal)
                step(V.tensor_scalar(two[:, t, :], const("iota8"), idx[:, t, 1:2], None, ALU.is_equal))
            rv = route.rearrange("p a (t r) -> p a t r", t=2)
            first = slice(0, N_EXPERTS)
            V.tensor_tensor(rv[:, 0, :, first], one[:, :, :], two[:, :, :], ALU.add).then_inc(mask_ready, 1)
            dve.wait_ge(gap_exp, 1)
            step(V.tensor_scalar(rt[:, 4:6], rt[:, 2:4], 1.0, None, ALU.add))
            step(V.reciprocal(rt[:, 6:8], rt[:, 4:6]))
            step(V.tensor_tensor(rt[:, 8:10], rt[:, 6:8], rt[:, 2:4], ALU.mult))
            for t in range(2):
                step(V.tensor_scalar(rv[:, 2, t, first], one[:, t, :], rt[:, 6 + t:7 + t], None, ALU.mult))
                step(V.scalar_tensor_tensor(rv[:, 2, t, first], two[:, t, :], rt[:, 8 + t:9 + t], rv[:, 2, t, first],
                                            ALU.mult, ALU.add))
            o = full(dve, ("rank",))
            step(V.tensor_reduce(rt[:, 10:11], o[:, 16:24], AX.X, ALU.max))
            step(V.tensor_copy(most[:, 0:1], rt[:, 10:11]))
            drain(V.tensor_copy(rv[:, 1, :, first], o[:, 0:16].rearrange("p (t e) -> p t e", t=2)), ("rank",))
            drained(dve, ("rank",))
            for p in range(1, PASSES):
                cols = slice(p * N_EXPERTS, (p + 1) * N_EXPERTS)
                V.tensor_copy(rv[:, 0, :, cols], rv[:, 0, :, first])
                V.tensor_copy(rv[:, 2, :, cols], rv[:, 2, :, first])
                step(V.tensor_scalar(rv[:, 1, :, cols], rv[:, 1, :, first], -float(p * CAP), None, ALU.add))

            def pick_tokens(cols, done):
                V.tensor_copy(cur[:, :, :], cols).then_inc(dve_step, 1)
                dve.wait_ge(dve_step, done)
                for which, dst, ready in ((0, pick, pick_ready), (2, gated_pick, gates_picked)):
                    for t in range(2):
                        ins = V.tensor_scalar(dst[:, t, :], const("iota"), cur[:, 1, t:t + 1],
                                              cur[:, which, t:t + 1], ALU.is_equal, ALU.mult)
                    ins.then_inc(ready, 1)

            dve_steps[0] += 1
            pick_tokens(rv[:, :, :, 0], dve_steps[0])
            for i in (1, 3):
                o = full(dve, ("acc", i))
                drain(V.tensor_copy(acc[:, i // 2, 512:1024], o[:, :]), ("acc", i))
            V.tensor_copy(rt[:, 11:12], rt[:, 10:11]).then_inc(count_ready, 1)
            for i in (0, 2):
                drained(dve, ("acc", i))

            def split_te(half, o, b):
                V.tensor_tensor(te_lo[:, 4 * half:4 * half + 4, :], o[:, :].rearrange("p (d c) -> p d c", d=4),
                                te_hi[:, 4 * half:4 * half + 4, :].bitcast(F32),
                                ALU.subtract).then_inc(bank_drained[b], 1)

            for half in range(2):
                dve.wait_ge(te_rounded, half + 1)
                split_te(half, full(dve, ("te", half)), bank_of["te", half][0])

            steps_before = dve_steps[0]

            def expert(i):
                def taken(name):
                    b, n = expert_job(name, i)
                    dve.wait_ge(bank_full[b], n)
                    return ps[b]

                for n, u in enumerate(EXPERT_UNITS):
                    dve.wait_ge(unit_rounded, i * N_UNITS + (n + 1))
                    V.tensor_tensor(w_lo[:, n % SLOTS, :], unit_weights(n), w_hi[:, n % SLOTS, :].bitcast(F32),
                                    ALU.subtract).then_inc(unit_split, 1)
                    if n < SLOTS - 1:
                        continue
                    kind, s, q = EXPERT_UNITS[n - SLOTS + 1]
                    if kind == "up" and q == 3:
                        b, m = expert_job(f"gate{s}", i)
                        dve.wait_ge(bank_drained[b], m)
                        o = taken(f"up{s}")
                        V.tensor_tensor(hid[:, :], silu[:, :], o[:, :], ALU.mult).then_inc(
                            bank_drained[EXPERT_JOB[f"up{s}"][0]], 1)
                    t = turned(n) if turned(n) == EXP_STEPS - 1 else turned(n - 1)
                    if t is not None and (t < EXP_STEPS - 1 or turned(n) is not None):
                        o = taken(f"tr{t}")
                        dve.wait_ge(hid_rounded, i * EXP_STEPS + (t + 1))
                        V.tensor_tensor(hid_lo[:, t % 2, :, :], o[:, :].rearrange("p (m c) -> p m c", m=FF_PER_STEP),
                                        hid_hi[:, t % 2, :, :].bitcast(F32),
                                        ALU.subtract).then_inc(bank_drained[EXPERT_JOB[f"tr{t}"][0]], 1)
                    if (kind, s, q) == ("gate", 2, 3):
                        o = taken("gt")
                        V.tensor_copy(gate_t[:, :], o[:, 0:SEQ]).then_inc(bank_drained[EXPERT_JOB["gt"][0]], 1)
                    if (kind, s, q) == ("gate", EXP_STEPS - 1, 0):
                        pick_tokens(rv[:, :, :, bass.ds(i + 1, 1)].squeeze(3), i + (steps_before + 1))
                    if (kind, s, q) == ("down", EXP_STEPS - 2, 1):
                        for half in range(2):
                            o = taken(f"te{half}")
                            dve.wait_ge(te_rounded, i * 2 + (half + 3))
                            split_te(half, o, EXPERT_JOB[f"te{half}"][0])
                b = EXPERT_JOB["y1"][0]
                V.tensor_copy(y[:, WIDE:D], taken("y1")[:, :]).then_inc(bank_drained[b], 1)
                for t in range(2):
                    for half in range(2):
                        o = taken(f"sc{t}{half}")
                        a = acc[:, t, half * WIDE:(half + 1) * WIDE]
                        V.tensor_tensor(a, a, o[:, :], ALU.add).then_inc(
                            bank_drained[EXPERT_JOB[f"sc{t}{half}"][0]], 1)

            with dve.Fori(0, N_EXPERTS) as e:
                expert(e)
            count = dve.value_load(most[0:1, 0:1])
            with dve.If(count > CAP):
                with dve.Fori(N_EXPERTS, ROUNDS) as i:
                    expert(i)

        @block.gpsimd
        def _(pool):
            G = nc.gpsimd
            pool_steps = [0]
            drained(pool, ("dist",))
            pool.dma_start(dist_dram, dist[0:N_BIAS, :]).then_inc(dist_stored, 16)
            pool.wait_ge(dist_stored, 16)
            pool.dma_start(bias_rev, bass.AP(tensor=dist_dram.tensor, offset=0,
                                             ap=[[1, P], [N_DIST, N_BIAS], [1, T]])).then_inc(bias_loaded, 16)
            pool.wait_ge(bias_loaded, 16)

            def step(ins):
                pool_steps[0] += 1
                ins.then_inc(pool_step, 1)
                pool.wait_ge(pool_step, pool_steps[0])

            def later(dst, src, shift, rows=slice(0, P)):
                step(G.tensor_tensor(dst[rows, N_META:PADDED], src[rows, N_META:PADDED],
                                     src[rows, N_META - shift:PADDED - shift], ALU.add))

            low_half, high_half = slice(0, P // 2), slice(P // 2, P)
            for l in range(DEPTH):
                drained(pool, ("z", l, "uc1"))
                for buf in (pool_a, pool_b, pool_u[:, 0], pool_u[:, 1]):
                    ins = G.memset(buf[:, 0:N_META], 0.0)
                step(ins)
                for j in range(2):
                    u = pool_u[:, j, :]
                    inv = const("inv_count", j * T, T)
                    later(pool_a, u, 1)
                    if j == 0:
                        later(pool_b, pool_a, 2, high_half)
                    else:
                        later(pool_b, pool_a, 2)
                        later(pool_a, pool_b, 4)
                        later(pool_b, pool_a, 8, high_half)
                    G.tensor_tensor(pool_d[low_half, j, :], pool_a[low_half, N_META:PADDED], inv[low_half], ALU.mult)
                    step(G.tensor_tensor(pool_d[high_half, j, :], pool_b[high_half, N_META:PADDED], inv[high_half],
                                         ALU.mult))
                    G.tensor_tensor(pool_d[:, j, :], pool_d[:, j, :], u[:, N_META:PADDED],
                                    ALU.subtract).then_inc(pool_ready, 1)


def bucket(n):
    exact = N_BUCKETS // 2
    if n < exact:
        return n
    large = exact + int(np.log(np.float32(n) / exact) / math.log(MAX_DISTANCE / exact) * (N_BUCKETS - exact))
    return min(large, N_BUCKETS - 1)


def shape_constants():
    c = np.zeros((P, N_CONST), np.float32)

    def put(name, v):
        at, n = CONST_COLS[name]
        c[:, at:at + n] = v

    i = np.arange(P)
    put("ident", np.eye(P))
    put("mean_d", np.full((P, P), 1.0 / D))
    put("mean64", (i[:, None] // HD == i[None] // HD) / HD)
    put("mean32", (i[:, None] // B_QK == i[None] // B_QK) / B_QK)
    put("flip", np.eye(P)[::-1])
    put("before", i[:, None] < i[None])
    put("ones", np.ones((P, P)))
    put("dup", np.concatenate([i[:, None] == HD * j + i[None] % HD for j in range(2)], 1))
    put("iota", np.arange(CAP)[None])
    put("iota8", np.arange(N_EXPERTS)[None])
    t = np.arange(T)
    w = np.array(POOL_WINDOWS)[np.arange(2 * P) // 64].reshape(2, P).T
    put("inv_count", (np.float32(1) / np.minimum(t[None, None] + 1, w[:, :, None]).astype(np.float32)).reshape(P, -1))
    put("eps", EPS)
    n = T - 1 - np.arange(N_DIST)
    b = np.array([bucket(max(x, 0)) for x in n])
    hot = (np.arange(N_BUCKETS)[:, None] == b[None]).astype(np.float32)
    seen = np.stack([(n >= 0) & (n < WINDOW)] * A_HEADS + [n >= 0] * B_HEADS)
    return c, hot, np.where(seen, 0.0, MASKED).astype(np.float32)


def pack_params(v):
    p = np.zeros((P, N_PARAM), np.float32)

    def put(name, a):
        at, n = PARAM_COLS[name]
        p[:, at:at + n] = a

    put("g_mix", v["g_mix"].reshape(DEPTH * KT, P).T)
    put("g_ffn", v["g_ffn"].reshape(DEPTH * KT, P).T)
    put("gain_a", np.tile(v["qk_gain_a"].reshape(DEPTH * 2, HD), (1, P // HD)).T)
    put("gain_b", np.tile(v["qk_gain_b"].reshape(DEPTH * 2, B_QK), (1, P // B_QK)).T)
    put("pool_scale", v["pool_scale"].reshape(DEPTH * 2, P).T)
    put("sinks", v["sinks"].reshape(1, -1))
    put("lam", v["diff_lambda"].reshape(1, -1))
    put("g_out", v["g_diff_out"].reshape(1, -1))
    w = np.zeros((2, HD, DEPTH, 2, 2, HD), np.float32)
    for g in range(2):
        w[g, :, :, :, g, :] = v["w_pool"].reshape(DEPTH, 2, 2, HD, HD)[:, :, g].transpose(2, 0, 1, 3)
    put("w_pool", w.reshape(P, -1))
    put("router", v["w_router"][0].reshape(KT, P, N_EXPERTS).transpose(1, 0, 2).reshape(P, -1))
    return p


def kernel(**inputs):
    import concourse.bacc as bacc
    from concourse.bass_utils import run_bass_kernel_spmd

    nc = bacc.Bacc("TRN2", target_bir_lowering=False, num_devices=1)
    v = {name: np.ascontiguousarray(a) for name, a in inputs.items()}
    consts, hot, mask_row = shape_constants()
    arrays, args = {}, []
    for name, a in (("x", v["x"]), ("meta_tokens", v["meta_tokens"]), ("rel_bias_table", v["rel_bias_table"]),
                    ("onehot", hot), ("mask_row", mask_row), ("consts", consts), ("params", pack_params(v)),
                    ("w_in", v["w_in"]), ("w_out", v["w_out"]), ("w_ffn_gate", v["w_ffn_gate"]),
                    ("w_ffn_up", v["w_ffn_up"]), ("w_ffn_down", v["w_ffn_down"]), ("w_exp_gate", v["w_exp_gate"]),
                    ("w_exp_up", v["w_exp_up"]), ("w_exp_down", v["w_exp_down"])):
        arrays[f"in_{name}"] = a
        args.append(nc.dram_tensor(f"in_{name}", a.shape, mybir.dt.from_np(a.dtype), kind="ExternalInput").ap())
    out = nc.dram_tensor("out_0", (1, SEQ, D), F32, kind="ExternalOutput").ap()
    dist_dram = nc.dram_tensor("dist_scratch", (N_BIAS, N_DIST), F32, kind="Internal").ap()
    build(nc, *args, out, dist_dram)
    r = run_bass_kernel_spmd(nc, [arrays], core_ids=[0])
    return r.results[0]["out_0"]
```

```python
import math
from contextlib import ExitStack

import concourse.bass as bass
import numpy as np
from concourse import mybir

ALU = mybir.AluOpType
ACT = mybir.ActivationFunctionType
AX = mybir.AxisListType
F32 = mybir.dt.float32
F32R = mybir.dt.float32r
I32 = mybir.dt.int32
U32 = mybir.dt.uint32

P = 128
D = 1024
KT = D // P
N_META = 16
SEQ = 256
T = N_META + SEQ
DEPTH = 2
HD = 64
A_HEADS, A_KV = 8, 2
B_HEADS, B_QK, B_V = 4, 32, 64
WINDOW = 128
POOL_WINDOWS = (2, 4, 8, 16)
N_BUCKETS, MAX_DISTANCE = 32, 128
N_BIAS = A_HEADS + B_HEADS
D_FF = 2816
N_EXPERTS = 8
D_FF_EXPERT = 3584
EPS = 1e-6
MASKED = 1e30

META, REAL0, REAL1 = 0, 1, 2
TOKENS = [(0, 16), (16, 144), (144, 272)]
N_DIST = T + P - 1

CHUNK = 2048
CW = 256
RING = 14
FF_STEPS = D_FF // CW
FF_TILES = D_FF // P
DOWN_PIECES = [(0, 8), (8, 16), (16, FF_TILES)]
IN_CHUNKS = 7
OUT_CHUNKS = D // CW

CAP = 128
PASSES = -(-SEQ // CAP)
UNIT = CHUNK // 2
WIDE = 512
EXP_STEPS = D_FF_EXPERT // WIDE
FF_PER_STEP = WIDE // P
SLOTS = 4

CONST_COLS = {}
PARAM_COLS = {}


def _columns(table, items):
    at = 0
    for name, n in items:
        table[name] = (at, n)
        at += n
    return at


N_CONST = _columns(CONST_COLS, [
    ("ident", P), ("mean_d", P), ("eps", 1), ("mean64", P), ("mean32", P), ("flip", P), ("before", P), ("ones", P),
    ("dup", 2 * P), ("iota", CAP), ("iota8", N_EXPERTS), ("inv_count", 2 * T)])
N_PARAM = _columns(PARAM_COLS, [
    ("g_mix", DEPTH * KT), ("g_ffn", DEPTH * KT), ("gain_a", DEPTH * 2), ("gain_b", DEPTH * 2),
    ("pool_scale", DEPTH * 2), ("sinks", DEPTH * A_HEADS), ("lam", DEPTH * 4 * B_QK),
    ("g_out", DEPTH * B_V), ("w_pool", DEPTH * 2 * P), ("router", KT * N_EXPERTS)])


def lam_init(l):
    return 0.8 - 0.6 * math.exp(-0.3 * l)


def query_tiles(l):
    return [META, REAL0, REAL1] if l < DEPTH - 1 else [REAL0, REAL1]


def key_tiles(group, qt):
    if qt == META:
        return [META]
    if qt == REAL0:
        return [META, REAL0]
    return [REAL0, REAL1] if group == "A" else [META, REAL0, REAL1]


def bias_column(qt):
    return TOKENS[REAL1][0] - TOKENS[qt][0]


def units(l):
    return [(g, qt, h) for g, n in (("A", A_HEADS), ("B", B_HEADS)) for qt in query_tiles(l) for h in range(n)]


LAG = 3
WARM_STEPS, WARM_PRODUCTS = 4, 2
PROJECTIONS = ["qa0", "qa1", "qa2", "qa3", "ka0", "va0", "va1", "qb0", "qb1", "kb0", "kb1", "vb0", "vb1", "uc0",
               "uc1"]
CHUNK_ENDS = ["qa1", "qa3", "va1", "qb1", "kb1", "vb1", "uc1"]


def normed(name):
    return name[0] in "qk"


NORMED = [x for x in PROJECTIONS if normed(x)]


def first_token(l):
    return 0 if l < DEPTH - 1 else N_META


def unit_steps(l):
    u = units(l)

    def at(n):
        return u[n] if 0 <= n < len(u) else None

    def closed(n):
        x = at(n)
        return x[:2] if x and (n == len(u) - 1 or u[n + 1][:2] != x[:2]) else None

    for n in range(len(u) + LAG + 4):
        yield n, at(n), at(n - 2), at(n - LAG), at(n - LAG - 1), closed(n - LAG - 2), closed(n - LAG - 4)


def groups(l):
    return [(g, qt) for g in "AB" for qt in query_tiles(l)]


def pool_step_no(l):
    return len(units(l)) - 2


def mix_order(l):
    out = []
    for n, _, _, _, _, _, tr in unit_steps(l):
        if n == pool_step_no(l):
            out += [("pool", 0), ("pool", 1)]
        if tr:
            out.append(tr)
    return out


EARLY_OUT = 4
EARLY_K, LATE_K = [0, 1, 2, 3, 6, 7], [4, 5]


SCORE_NO, B_NO, A_GROUP_NO, B_GROUP_NO = {}, {}, {}, {}
SCORE_OWNER = []
for _l in range(DEPTH):
    for _u in units(_l):
        for _i in range(1 + (_u[0] == "B")):
            SCORE_NO[_l, _u, _i] = len(SCORE_OWNER)
            SCORE_OWNER.append((_l, _u))
        if _u[0] == "B":
            B_NO[_l, _u] = len(B_NO)
    for _g in groups(_l):
        _no = A_GROUP_NO if _g[0] == "A" else B_GROUP_NO
        _no[_l, _g] = len(_no)
SCORE_SLOTS = 4
PROB_SLOTS = 8


def plan_banks():
    of, used, turn = {}, [0] * 8, [0, 0]

    def add(key):
        held = key[0] in ("o", "ms")
        b = 6 + turn[1] % 2 if held else turn[0] % 6
        turn[held] += 1
        used[b] += 1
        of[key] = (b, used[b])

    for k in range(KT):
        add(("xt", k))
    add(("dist",))
    for l in range(DEPTH):
        add(("ms", l, 0))
        waiting = None
        for name in PROJECTIONS:
            add(("z", l, name))
            if waiting:
                add(("st", l, waiting))
            waiting = name if normed(name) else None
        add(("kd", l, 0))
        add(("kd", l, 1))
        if l == 0:
            for h in range(N_BIAS):
                add(("bias", h))
        for n, s, c, o, v, fin, tr in unit_steps(l):
            if n == pool_step_no(l):
                add(("pool", l, 0))
                add(("pool", l, 1))
            if s:
                for i in range(1 + (s[0] == "B")):
                    add(("s", l, s, i))
            if o:
                add(("pt", l, o))
            if v and v[2] == 0:
                add(("o", l, v[:2]))
            if tr == groups(l)[-1]:
                for d in range(EARLY_OUT):
                    add(("mix", l, d))
            if tr:
                add(("ot", l, tr))
        for d in range(EARLY_OUT, KT):
            add(("mix", l, d))
        add(("ms", l, 1))
        if l < DEPTH - 1:
            for s in range(FF_STEPS):
                for which, f in (("g", 2 * s), ("g", 2 * s + 1), ("u", 2 * s), ("u", 2 * s + 1)):
                    add((which, f))
            for d in range(KT):
                add(("down", d))
    for i in range(4):
        add(("acc", i))
    add(("lt",))
    add(("logits",))
    for i in range(4):
        add(("ht", i))
    add(("rank",))
    add(("count",))
    add(("te", 0))
    add(("te", 1))
    return of, used


def plan_chunks():
    out = []
    for l in range(DEPTH):
        out += [("in", l, c) for c in range(IN_CHUNKS)]
        out += [("out", l, c) for c in range(OUT_CHUNKS)]
        if l < DEPTH - 1:
            out += [x for s in range(FF_STEPS) for x in (("gate", s), ("up", s))]
            out += [("down", c, p) for c in range(OUT_CHUNKS) for p in range(len(DOWN_PIECES))]
    return out


CHUNKS = plan_chunks()
CHUNK_NO = {c: n for n, c in enumerate(CHUNKS)}
TRUNK_RING = RING // 2
TRUNK_UNITS = [(c, q) for c in CHUNKS for q in range(2)]
N_TRUNK = len(TRUNK_UNITS)


def ends_job(u):
    chunk, q = u
    return q == 1 and (chunk[0] != "down" or chunk[2] == len(DOWN_PIECES) - 1)


FFN_UNITS = range(2 * CHUNK_NO["gate", 0], 2 * CHUNK_NO["in", 1, 0])
TRUNK_READ = [sum(not ends_job(u) for u in TRUNK_UNITS[:n + 1]) for n in range(N_TRUNK)]


def unit_width(n):
    (chunk, q) = TRUNK_UNITS[n]
    tiles = KT if chunk[0] != "down" else DOWN_PIECES[chunk[2]][1] - DOWN_PIECES[chunk[2]][0]
    return min(tiles * CW - q * UNIT, UNIT)


EXPERT_UNITS = []
for _s in range(EXP_STEPS):
    EXPERT_UNITS += [("gate", _s, _q) for _q in range(4)] + [("up", _s, _q) for _q in range(4)]
    if _s:
        EXPERT_UNITS += [("down", _s - 1, _q) for _q in range(4)]
EXPERT_UNITS += [("down", EXP_STEPS - 1, _q) for _q in range(4)]
N_UNITS = len(EXPERT_UNITS)
UNIT_AT = {u: n for n, u in enumerate(EXPERT_UNITS)}
N_CHUNKS = N_UNITS // 2
LAST_UNITS = [("down", EXP_STEPS - 1, 3)] + [(w, _s, 3) for w in ("gate", "up") for _s in range(EXP_STEPS)]
READ_COUNT = [sum(u not in LAST_UNITS for u in EXPERT_UNITS[:n + 1]) for n in range(N_UNITS)]

_last = EXP_STEPS - 1
EXPERT_JOBS = []
for _s in range(EXP_STEPS):
    EXPERT_JOBS.append((f"gate{_s}", _s % 2))
    if _s:
        EXPERT_JOBS.append((f"tr{_s - 1}", 6))
    EXPERT_JOBS.append((f"up{_s}", 2 + _s % 2))
    if _s == 1:
        EXPERT_JOBS += [("pt", 7), ("y0", 4), ("y1", 5)]
EXPERT_JOBS += [("te0", 7), ("te1", 6), (f"tr{_last}", 7), ("sc00", 1), ("sc01", 3), ("sc10", 6), ("sc11", 4)]
EXPERT_USES = [sum(b == x for _, x in EXPERT_JOBS) for b in range(8)]
EXPERT_JOB = {name: (b, sum(x == b for _, x in EXPERT_JOBS[:n])) for n, (name, b) in enumerate(EXPERT_JOBS)}
ROUNDS = PASSES * N_EXPERTS


def build(nc, x, meta_tokens, bias_table, onehot, mask_row, consts, params, w_in, w_out, w_gate, w_up, w_down,
          e_gate, e_up, e_down, out, dist_dram):
    bank_of, bank_uses = plan_banks()
    assert len(CHUNKS) % TRUNK_RING == 0 and N_CHUNKS % RING == 0 and N_UNITS % SLOTS == 0
    ring_per = N_CHUNKS // RING

    with ExitStack() as ctx:
        def sb(name, shape, dt=F32):
            return ctx.enter_context(nc.sbuf_tensor(name, shape, dt))

        def sem(name):
            return ctx.enter_context(nc.semaphore(name))

        cst = sb("cst", [P, N_CONST])
        par = sb("par", [P, N_PARAM])

        WORK = (SCORE_SLOTS + PROB_SLOTS) * T + 2 * 3 * P
        ARENA = 9184
        sizes = [N_BIAS * T, WORK, KT * T, KT * T, ARENA]
        ring_at = sum(sizes)
        region = -(-nc.sbuf_base // 32) * 32
        sb("region", [P, ring_at + RING * CHUNK])

        def place(name, shape, at, dt=F32):
            return nc.alloc_sbuf_tensor_at(name, shape, dt, offset=region + 4 * at)

        bias = place("bias", [P, N_BIAS, T], 0)
        work = place("work", [P, WORK], sizes[0])
        X = place("X", [P, KT, T], sum(sizes[:2]))
        H = place("H", [P, KT, T], sum(sizes[:3]))
        arena_base = sum(sizes[:4])
        arena = place("arena", [P, ARENA], arena_base)
        ring = place("ring", [P, RING, CHUNK], ring_at)
        split_at = ring_at + TRUNK_RING * CHUNK
        t_hi = place("t_hi", [P, SLOTS, UNIT], split_at, F32R)
        t_lo = place("t_lo", [P, SLOTS, UNIT], split_at + SLOTS * UNIT, F32R)
        h_hi = [place("h_hi_mix", [P, KT, T], split_at + 2 * SLOTS * UNIT, F32R),
                place("h_hi_ffn", [P, KT, T], arena_base + FF_TILES * T, F32R)]
        h_lo = place("h_lo", [P, KT, T], sum(sizes[:3]), F32R)
        mix_hi = place("mix_hi", [P, KT, T], split_at + 2 * SLOTS * UNIT, F32R)
        hidden_hi = place("hidden_hi", [P, FF_TILES, T], split_at + 2 * SLOTS * UNIT, F32R)
        hidden_lo = place("hidden_lo", [P, FF_TILES, T], arena_base, F32R)
        assert 2 * SLOTS * UNIT + FF_TILES * T <= (RING - TRUNK_RING) * CHUNK
        w_hi = place("w_hi", [P, SLOTS, UNIT], 0, F32R)
        w_lo = place("w_lo", [P, SLOTS, UNIT], SLOTS * UNIT, F32R)
        te_hi = place("te_hi", [P, KT, CAP], sum(sizes[:3]), F32R)
        te_lo = place("te_lo", [P, KT, CAP], sum(sizes[:3]) + KT * CAP, F32R)
        hid_end = sum(sizes) - 4 * FF_PER_STEP * CAP
        hid_hi = place("hid_hi", [P, 2, FF_PER_STEP, CAP], hid_end, F32R)
        hid_lo = place("hid_lo", [P, 2, FF_PER_STEP, CAP], hid_end + 2 * FF_PER_STEP * CAP, F32R)
        scores = work[:, 0:SCORE_SLOTS * T].rearrange("p (s t) -> p s t", s=SCORE_SLOTS)
        probs = work[:, SCORE_SLOTS * T:(SCORE_SLOTS + PROB_SLOTS) * T].rearrange("p (s t) -> p s t", s=PROB_SLOTS)
        probs_t = work[:, (SCORE_SLOTS + PROB_SLOTS) * T:].rearrange("p (s t) -> p s t", s=2)
        bias_rev = work[:, 0:N_BIAS * T].rearrange("p (h t) -> p h t", h=N_BIAS)
        rstd = sb("rstd", [P, 2, T])
        neg_sink = sb("neg_sink", [P, DEPTH * A_HEADS])
        gains = sb("gains", [P, DEPTH, 4])
        g_out = sb("g_out", [P, DEPTH, B_V])
        lam_s = sb("lam_s", [P, DEPTH * 4])
        arena_at = [0]

        def part(shape):
            n = int(np.prod(shape[1:]))
            at = arena_at[0]
            arena_at[0] += n
            assert arena_at[0] <= ARENA, arena_at
            v = arena[:, at:at + n]
            if len(shape) == 3:
                v = v.rearrange("p (a b) -> p a b", a=shape[1])
            return v

        q_a = part([P, 4, T])
        k_a = part([P, T])
        k_dup = part([P, 2, T])
        q_b = part([P, 2, T])
        k_b = part([P, 2, T])
        v_all = part([P, 3, 2 * HD + B_HEADS * B_V])
        mix_lo = place("mix_lo", [P, KT, T], arena_base + arena_at[0], F32R)
        arena_at[0] += KT * T
        square = part([P, 2, T])
        PADDED = N_META + T
        pool_u = part([P, 2, PADDED])
        attention_end = arena_at[0]
        arena_at[0] = 0
        x_rows = part([P, 2, D])
        x_meta = part([P, D])
        arena_at[0] = attention_end
        hot = part([P, N_DIST])
        mrow = part([P, N_DIST])
        dist = part([P, N_DIST])
        tab = part([P, N_BIAS])
        prologue_end = arena_at[0]
        arena_at[0] = ARENA - 6 * 4 * 8 - 2 * 6 * 4 - DEPTH * B_HEADS - DEPTH * 2 * B_QK
        assert arena_at[0] >= max(prologue_end, (FF_TILES + KT) * T)
        low = part([P, 6, 8])
        total = part([P, 6, 8])
        gap = part([P, 6, 8])
        share = part([P, 6, 8])
        mean_o = part([P, 6, 4])
        std_o = part([P, 6, 4])
        factor = part([P, DEPTH, B_HEADS])
        lam_t = part([P, DEPTH * 2, B_QK])
        arena_at[0] = 0
        hidden = part([P, FF_TILES, T])
        arena_at[0] = 0
        h_rows = part([P, 2, D])
        acc = part([P, 2, D])
        pick = part([P, 2, CAP])
        logits_t = part([P, SEQ])
        pick_t = place("pick_t", [P, SEQ], arena_base + arena_at[0], F32R)
        arena_at[0] += SEQ
        silu = part([P, WIDE])
        hid = part([P, WIDE])
        y_hi = place("y_hi", [P, D], arena_base + arena_at[0], F32R)
        arena_at[0] += D
        y_lo = place("y_lo", [P, D], 2 * SLOTS * UNIT, F32R)
        assert 2 * SLOTS * UNIT + D <= sum(sizes[:3])
        route = part([P, 3, 2 * (ROUNDS + 1)])
        cur = part([P, 2, 2])
        gate_now = part([P, 2])
        lg = part([P, 2, N_EXPERTS])
        top = part([P, 2, N_EXPERTS])
        idx = part([P, 2, N_EXPERTS])
        one = part([P, 2, N_EXPERTS])
        two = part([P, 2, N_EXPERTS])
        rt = part([P, 16])
        assert sum(sizes[:4]) + arena_at[0] <= hid_end
        h_flat = H[:, :, :].rearrange("p k t -> p (k t)")
        pool_a = h_flat[:, 0:PADDED]
        pool_b = h_flat[:, PADDED:2 * PADDED]
        pool_d = h_flat[:, 2 * PADDED:2 * PADDED + 2 * T].rearrange("p (j t) -> p j t", j=2)
        heads = h_flat[:, 2 * PADDED + 2 * T:2 * PADDED + 2 * T + 2 * A_HEADS * HD].rearrange("p (m n) -> p m n", m=2)
        idx_u = sb("idx_u", [P, 2, N_EXPERTS], U32)
        most = sb("most", [P, 2], I32)

        ps = [ctx.enter_context(nc.psum_tensor(f"bank{b}", [P, 512], F32)) for b in range(8)]

        bank_full = [sem(f"bank_full{b}") for b in range(8)]
        bank_drained = [sem(f"bank_drained{b}") for b in range(8)]
        ring_full = [sem(f"ring_full{r}") for r in range(RING)]
        x_loaded = sem("x_loaded")
        consts_loaded = sem("consts_loaded")
        all_consts_loaded = sem("all_consts_loaded")
        params_loaded = sem("params_loaded")
        dist_loaded = sem("dist_loaded")
        dist_stored = sem("dist_stored")
        bias_loaded = sem("bias_loaded")
        squared = sem("squared")
        head_squares = sem("head_squares")
        dve_step = sem("dve_step")
        pool_step = sem("pool_step")
        h_ready = sem("h_ready")
        h_rounded = sem("h_rounded")
        h_split = sem("h_split")
        mix_rounded = sem("mix_rounded")
        hidden_rounded = sem("hidden_rounded")
        hidden_split = sem("hidden_split")
        exp_ready = sem("exp_ready")
        sink_gap = sem("sink_gap")
        sink_exp = sem("sink_exp")
        probs_mixed = sem("probs_mixed")
        out_mean = sem("out_mean")
        out_std = sem("out_std")
        heads_ready = sem("heads_ready")
        pool_ready = sem("pool_ready")
        lam_dot = sem("lam_dot")
        lam_exp = sem("lam_exp")
        gap_ready = sem("gap_ready")
        gap_exp = sem("gap_exp")
        mask_ready = sem("mask_ready")
        count_ready = sem("count_ready")
        pick_ready = sem("pick_ready")
        gates_taken = sem("gates_taken")
        y_rounded = sem("y_rounded")
        unit_rounded = sem("unit_rounded")
        unit_split = sem("unit_split")
        unit_read = sem("unit_read")
        te_rounded = sem("te_rounded")
        hid_rounded = sem("hid_rounded")
        out_stored = sem("out_stored")

        def const(name, a=0, n=None):
            at, size = CONST_COLS[name]
            return cst[:, at + a:at + (size if n is None else a + n)]

        def param(name, a=0, n=None):
            at, size = PARAM_COLS[name]
            return par[:, at + a:at + (size if n is None else a + n)]

        def full(eng, key):
            b, n = bank_of[key]
            eng.wait_ge(bank_full[b], n)
            return ps[b]

        def drained(eng, key):
            b, n = bank_of[key]
            eng.wait_ge(bank_drained[b], n)

        def drain(ins, key):
            ins.then_inc(bank_drained[bank_of[key][0]], 1)

        def copy_probs(eng, copy, l, u, n):
            g, qt, h = u
            nq = TOKENS[qt][1] - TOKENS[qt][0]
            kts = key_tiles(g, qt)
            o = full(eng, ("pt", l, u))
            slot = probs_t[:, n % 2, :]
            ins = None
            if META in kts:
                ins = copy(slot[0:N_META, 0:nq], o[0:N_META, 0:nq])
            if kts[-1] != META:
                first = max(kts[0], REAL0)
                ins = copy(slot[:, first * P:(kts[-1] + 1) * P], o[:, first * P:(kts[-1] + 1) * P])
            drain(ins, ("pt", l, u))

        def expert_job(name, i, before=0):
            b, j = EXPERT_JOB[name]
            return b, i * EXPERT_USES[b] + (bank_uses[b] + j + 1 - before)

        def trunk_unit_free(n):
            chunk, q = TRUNK_UNITS[n - SLOTS]
            if not ends_job((chunk, q)):
                return unit_read, TRUNK_READ[n - SLOTS]
            kind = chunk[0]
            if kind == "in":
                key = ("z", chunk[1], CHUNK_ENDS[chunk[2]])
            elif kind == "out":
                key = ("mix", chunk[1], 2 * chunk[2] + 1)
            else:
                key = (kind[0] if kind != "down" else kind, 2 * chunk[1] + 1)
            b, m = bank_of[key]
            return bank_full[b], m

        def trunk_weights(n):
            at = (n % 2) * UNIT
            return ring[:, (n // 2) % TRUNK_RING, at:at + unit_width(n)]

        def mix_count(l, part_):
            return l * len(mix_order(0)) + mix_order(l).index(part_) + 1

        def unit_weights(n):
            return ring[:, (n // 2) % RING, (n % 2) * UNIT:(n % 2 + 1) * UNIT]

        def acc_done(i):
            b, n = expert_job("sc11", i)
            return bank_drained[b], n

        def unit_free(n, i):
            if n == SLOTS - 1:
                b, j = EXPERT_JOB["y1"]
                return bank_full[b], i * EXPERT_USES[b] + bank_uses[b]
            if n < SLOTS:
                return unit_read, i * READ_COUNT[-1] + (TRUNK_READ[-1] + READ_COUNT[n - SLOTS] - READ_COUNT[-1])
            kind, s, q = EXPERT_UNITS[n - SLOTS]
            if EXPERT_UNITS[n - SLOTS] in LAST_UNITS:
                b, m = expert_job(f"{kind}{s}", i)
                return bank_full[b], m
            return unit_read, i * READ_COUNT[-1] + (TRUNK_READ[-1] + READ_COUNT[n - SLOTS])

        def turned(n):
            for s in range(EXP_STEPS):
                after = UNIT_AT["gate", s + 1, 3] if s < EXP_STEPS - 1 else UNIT_AT["down", s - 1, 2]
                if n == after + SLOTS - 1:
                    return s
            return None

        block = ctx.enter_context(nc.Block())

        @block.sync
        def _(sp):
            sp.dma_start(x_meta[0:N_META, :], meta_tokens).then_inc(x_loaded, 16)
            sp.dma_start(x_rows, x[0].rearrange("(t p) d -> p t d", p=P)).then_inc(x_loaded, 16)

            def source(chunk):
                kind = chunk[0]
                if kind in ("in", "out", "gate", "up"):
                    w = {"in": w_in, "out": w_out, "gate": w_gate, "up": w_up}[kind]
                    l, c = chunk[1:] if len(chunk) == 3 else (0, chunk[1])
                    return w[l, :, c * CW:(c + 1) * CW].rearrange("(k p) n -> p k n", p=P)
                c, (k0, k1) = chunk[1], DOWN_PIECES[chunk[2]]
                return w_down[0, k0 * P:k1 * P, c * CW:(c + 1) * CW].rearrange("(k p) n -> p k n", p=P)

            for n, chunk in enumerate(CHUNKS):
                if n >= TRUNK_RING:
                    sp.wait_ge(unit_split, 2 * (n - TRUNK_RING) + 2)
                src = source(chunk)
                k = src.shape[1]
                dst = ring[:, n % TRUNK_RING, 0:k * CW].rearrange("p (k n) -> p k n", k=k)
                sp.dma_start(dst, src).then_inc(ring_full[n % TRUNK_RING], 16)

            def expert_source(n, e):
                kind, s, q = EXPERT_UNITS[2 * n]
                if kind == "down":
                    r = s * WIDE + q * P
                    return e_down[0, e, r:r + 2 * P, :].rearrange("(k p) n -> p k n", p=P)
                w = e_gate if kind == "gate" else e_up
                return w[0, e, 2 * q * P:(2 * q + 4) * P, s * WIDE:(s + 1) * WIDE].rearrange("(k p) n -> p k n", p=P)

            def stream_expert(i, e, first):
                for n in range(N_CHUNKS):
                    if n >= RING or not first:
                        sp.wait_ge(unit_split, i * N_UNITS + (N_TRUNK + 2 * (n - RING) + 2))
                    elif n < TRUNK_RING:
                        sp.wait_ge(unit_split, N_TRUNK + 2 * (n - TRUNK_RING) + 2)
                    elif n == TRUNK_RING:
                        full(sp, ("mix", DEPTH - 1, KT - 1))
                    src = expert_source(n, e)
                    dst = ring[:, n % RING, :].rearrange("p (k n) -> p k n", k=src.shape[1])
                    sp.dma_start(dst, src).then_inc(ring_full[n % RING], 16)

            stream_expert(0, 0, True)
            with sp.Fori(1, N_EXPERTS) as e:
                stream_expert(e, e, False)
            sp.wait_ge(count_ready, 1)
            count = sp.value_load(most[0:1, 0:1])
            with sp.If(count > CAP):
                with sp.Fori(1, PASSES) as p:
                    with sp.Fori(0, N_EXPERTS) as e:
                        stream_expert(p * N_EXPERTS + e, e, False)
                sp.wait_ge(*acc_done(ROUNDS - 1))
            sp.wait_ge(*acc_done(N_EXPERTS - 1))
            for t in range(2):
                sp.dma_start(out[0, t * P:(t + 1) * P, :], acc[:, t, :]).then_inc(out_stored, 16)
            sp.wait_ge(out_stored, 32)

        @block.tensor
        def _(pe):
            def open_job(key):
                b, n = bank_of[key]
                if n > 1:
                    pe.wait_ge(bank_drained[b], n - 1)
                return ps[b]

            def close(ins, key):
                ins.then_inc(bank_full[bank_of[key][0]], 1)

            def unit(chunk, q):
                n = 2 * CHUNK_NO[chunk] + q
                pe.wait_ge(unit_split, n + 1)
                return [w[:, n % SLOTS, :].rearrange("p (k n) -> p k n", n=CW) for w in (t_hi, t_lo)]

            def products(o, chunk, j, k0, k1, hi, lo, t0, first, last, ready=None):
                for k in range(k0, k1):
                    q, m = divmod(k - k0, SLOTS)
                    if m == 0:
                        w_h, w_l = unit(chunk, q)
                    if ready:
                        ready(k)
                    cols = slice(j * P, (j + 1) * P)
                    pe.matmul(o[:, t0:T], w_h[:, m, cols], hi[:, k, t0:T], start=first and k == k0, stop=False)
                    pe.matmul(o[:, t0:T], w_l[:, m, cols], hi[:, k, t0:T], start=False, stop=False)
                    ins = pe.matmul(o[:, t0:T], w_h[:, m, cols], lo[:, k, t0:T], start=False,
                                    stop=last and k == k1 - 1)
                    if j == 1 and q == 0 and m == SLOTS - 1:
                        ins.then_inc(unit_read, 1)
                return ins

            def first_products(o, chunk, hi, lo, t0, norm_no):
                w = []
                for k in range(KT):
                    q, m = divmod(k, SLOTS)
                    if m == 0:
                        w.append(unit(chunk, q))
                    pe.wait_ge(h_rounded, norm_no * KT + k + 1)
                    for part_ in range(2):
                        pe.matmul(o[:, t0:T], w[q][part_][:, m, 0:P], hi[:, k, t0:T],
                                  start=k == 0 and part_ == 0, stop=False)
                for k in range(KT):
                    q, m = divmod(k, SLOTS)
                    pe.wait_ge(h_split, norm_no * KT + k + 1)
                    ins = pe.matmul(o[:, t0:T], w[q][0][:, m, 0:P], lo[:, k, t0:T], start=False, stop=k == KT - 1)
                return ins

            def mean_square(l, which, k):
                t0 = first_token(l) if which else 0
                key = ("ms", l, which)
                o = open_job(key) if k == 0 else ps[bank_of[key][0]]
                pe.wait_ge(squared, (2 * l + which) * KT + k + 1)
                ins = pe.matmul(o[:, t0:T], const("mean_d"), H[:, k, t0:T], start=k == 0, stop=k == KT - 1)
                if k == KT - 1:
                    close(ins, key)

            ident = const("ident")
            pe.wait_ge(x_loaded, 32)
            pe.wait_ge(consts_loaded, 16)
            for k in range(KT):
                key = ("xt", k)
                o = open_job(key)
                cols = slice(k * P, (k + 1) * P)
                pe.transpose(o[:, 0:16], x_meta[0:N_META, cols], ident[0:N_META, 0:N_META])
                pe.transpose(o[:, 16:144], x_rows[:, 0, cols], ident)
                close(pe.transpose(o[:, 144:272], x_rows[:, 1, cols], ident), key)
                if k >= 2:
                    mean_square(0, 0, k - 2)
            for k in range(KT - 2, KT):
                mean_square(0, 0, k)
            pe.wait_ge(dist_loaded, 48)
            key = ("dist",)
            o = open_job(key)
            close(pe.matmul(o[0:N_BIAS, 0:N_DIST], tab[0:N_BUCKETS, :], hot[0:N_BUCKETS, :], start=True, stop=True),
                  key)
            pe.wait_ge(all_consts_loaded, 16)

            def project(l, name):
                key = ("z", l, name)
                kind, j = name[:2], int(name[2])
                o = open_job(key)
                if kind in ("va", "vb"):
                    chunk = ("in", l, 2 if kind == "va" else 5)
                    for tile, at in [(META, 0), (REAL0, 256)] if j == 0 else [(REAL1, 0)]:
                        t0, t1 = TOKENS[tile]
                        for k in range(KT):
                            q, m = divmod(k, SLOTS)
                            if m == 0:
                                w_h, w_l = unit(chunk, q)
                            dst = o[0:t1 - t0, at:at + CW]
                            pe.matmul(dst, h_hi[0][:, k, t0:t1], w_h[:, m, :], start=k == 0, stop=False)
                            pe.matmul(dst, h_hi[0][:, k, t0:t1], w_l[:, m, :], start=False, stop=False)
                            ins = pe.matmul(dst, h_lo[:, k, t0:t1], w_h[:, m, :], start=False, stop=k == KT - 1)
                            if j == 1 and k == SLOTS - 1:
                                ins.then_inc(unit_read, 1)
                else:
                    chunk, at = {"qa": (j // 2, j % 2), "ka": (2, 0), "qb": (3, j), "kb": (4, j), "uc": (6, j)}[kind]
                    t0 = first_token(l) if kind[0] == "q" else 0
                    if name == "qa0":
                        ins = first_products(o, ("in", l, 0), h_hi[0], h_lo, t0, 2 * l)
                    else:
                        ins = products(o, ("in", l, chunk), at, 0, KT, h_hi[0], h_lo, t0, True, True)
                close(ins, key)

            def head_square(l, name):
                key = ("st", l, name)
                o = open_job(key)
                t0 = first_token(l) if name[0] == "q" else 0
                n = NORMED.index(name)
                pe.wait_ge(head_squares, l * len(NORMED) + n + 1)
                mean = const("mean64" if name[1] == "a" else "mean32")
                close(pe.matmul(o[:, t0:T], mean, square[:, n % 2, t0:T], start=True, stop=True), key)

            def scores_of(l, u):
                g, qt, h = u
                t0, t1 = TOKENS[qt]
                kts = key_tiles(g, qt)
                k0, k1 = TOKENS[kts[0]][0], TOKENS[kts[-1]][1]
                for i in range(1 + (g == "B")):
                    key = ("s", l, u, i)
                    o = open_job(key)
                    if g == "A":
                        r = slice(HD * (h % 2), HD * (h % 2) + HD)
                        ql, kr = q_a[r, h // 2, t0:t1], k_dup[r, h // 4, k0:k1]
                    else:
                        at = B_QK * (2 * (h % 2) + i)
                        r = slice(at, at + B_QK)
                        ql, kr = q_b[r, h // 2, t0:t1], k_b[r, h // 2, k0:k1]
                    close(pe.matmul(o[0:t1 - t0, 0:k1 - k0], ql, kr, start=True, stop=True), key)

            def output_of(l, u):
                g, qt, h = u
                nq = TOKENS[qt][1] - TOKENS[qt][0]
                kts = key_tiles(g, qt)
                key = ("pt", l, u)
                o = open_job(key)
                if g == "A":
                    pe.wait_ge(exp_ready, SCORE_NO[l, u, 0] + 1)
                else:
                    pe.wait_ge(probs_mixed, B_NO[l, u] + 1)
                pr = probs[:, SCORE_NO[l, u, 0] % PROB_SLOTS, :]
                at = 0
                for kt in kts:
                    k0, k1 = TOKENS[kt]
                    ins = pe.transpose(o[0:k1 - k0, kt * P:kt * P + nq], pr[0:nq, at:at + k1 - k0],
                                       ident[0:nq, 0:nq])
                    at += k1 - k0
                close(ins, key)

            def values_of(l, u, n):
                g, qt, h = u
                nq = TOKENS[qt][1] - TOKENS[qt][0]
                kts = key_tiles(g, qt)
                okey = ("o", l, u[:2])
                ob = ps[bank_of[okey][0]]
                if h == 0:
                    open_job(okey)
                drained(pe, ("pt", l, u))
                vcol = HD * (h // 4) if g == "A" else 2 * HD + B_V * h
                for m, kt in enumerate(kts):
                    rows = TOKENS[kt][1] - TOKENS[kt][0]
                    ins = pe.matmul(ob[0:nq, h * HD:(h + 1) * HD], probs_t[0:rows, n % 2, kt * P:kt * P + nq],
                                    v_all[0:rows, kt, vcol:vcol + HD], start=m == 0, stop=m == len(kts) - 1)
                if h == (A_HEADS if g == "A" else B_HEADS) - 1:
                    close(ins, okey)

            def transpose_heads(l, group):
                g, qt = group
                key = ("ot", l, group)
                nq = TOKENS[qt][1] - TOKENS[qt][0]
                o = open_job(key)
                m = groups(l).index(group)
                if g == "A":
                    drained(pe, ("o", l, group))
                else:
                    pe.wait_ge(heads_ready, B_GROUP_NO[l, group] + 1)
                for j in range(4 if g == "A" else 2):
                    ins = pe.transpose(o[:, j * P:j * P + nq], heads[0:nq, m % 2, j * P:(j + 1) * P],
                                       ident[0:nq, 0:nq])
                close(ins, key)

            for l in range(DEPTH):
                waiting = None
                for name in PROJECTIONS:
                    project(l, name)
                    if waiting:
                        head_square(l, waiting)
                    waiting = name if normed(name) else None
                drained(pe, ("z", l, "ka0"))
                for i in range(2):
                    key = ("kd", l, i)
                    o = open_job(key)
                    close(pe.matmul(o[:, 0:T], const("dup", i * P, P), k_a, start=True, stop=True), key)
                if l == 0:
                    pe.wait_ge(bias_loaded, 16)
                    for h in range(N_BIAS):
                        key = ("bias", h)
                        o = open_job(key)
                        close(pe.matmul(o[:, 0:T], const("flip"), bias_rev[:, h, :], start=True, stop=True), key)
                drained(pe, ("z", l, "kb1"))
                drained(pe, ("kd", l, 0))
                drained(pe, ("kd", l, 1))
                for name in ("va0", "va1", "vb0", "vb1"):
                    drained(pe, ("z", l, name))
                def keep_warm(l):
                    b, n = bank_of["o", l, groups(l)[0]]
                    pe.wait_ge(bank_drained[b], n - 1)
                    for _ in range(WARM_PRODUCTS):
                        pe.matmul(ps[b][:, 0:T], ident, k_dup[:, 0, :], start=True, stop=True)

                def early_outputs():
                    for part_ in mix_order(l):
                        if part_[0] == "A":
                            drained(pe, ("ot", l, part_))
                    for j in range(2):
                        drained(pe, ("pool", l, j))
                    for d in range(EARLY_OUT):
                        o = open_job(("mix", l, d))
                        out_products(o, d, EARLY_K, True, False)

                def out_products(o, d, ks, first, last):
                    chunk, j = ("out", l, d // 2), d % 2
                    cols, t0 = slice(j * P, (j + 1) * P), first_token(l)
                    w = [unit(chunk, q) for q in range(2)]
                    for k in ks:
                        q, m = divmod(k, SLOTS)
                        (w_h, w_l) = w[q]
                        pe.matmul(o[:, t0:T], w_h[:, m, cols], mix_hi[:, k, t0:T], start=first and k == ks[0],
                                  stop=False)
                        pe.matmul(o[:, t0:T], w_l[:, m, cols], mix_hi[:, k, t0:T], start=False, stop=False)
                        ins = pe.matmul(o[:, t0:T], w_h[:, m, cols], mix_lo[:, k, t0:T], start=False,
                                        stop=last and k == ks[-1])
                        if j == 1 and k == SLOTS - 1:
                            ins.then_inc(unit_read, 1)
                    return ins

                for n, s, c, o, v, fin, tr in unit_steps(l):
                    if n == pool_step_no(l):
                        for j in range(2):
                            key = ("pool", l, j)
                            o_pool = open_job(key)
                            pe.wait_ge(pool_ready, 2 * l + j + 1)
                            close(pe.matmul(o_pool[:, 0:T], param("w_pool", (2 * l + j) * P, P), pool_d[:, j, :],
                                            start=True, stop=True), key)
                    if s:
                        scores_of(l, s)
                    if n < WARM_STEPS:
                        keep_warm(l)
                    if o:
                        output_of(l, o)
                    if v:
                        values_of(l, v, n - 1)
                    if tr == groups(l)[-1]:
                        early_outputs()
                    if tr:
                        transpose_heads(l, tr)
                for group in groups(l):
                    drained(pe, ("ot", l, group))
                for d in range(KT):
                    key = ("mix", l, d)
                    if d < EARLY_OUT:
                        close(out_products(ps[bank_of[key][0]], d, LATE_K, False, True), key)
                    else:
                        close(out_products(open_job(key), d, range(KT), True, True), key)
                    if d >= 2:
                        mean_square(l, 1, d - 2)
                for k in range(KT - 2, KT):
                    mean_square(l, 1, k)
                if l < DEPTH - 1:
                    for s in range(FF_STEPS):
                        for which in ("gate", "up"):
                            for j in range(2):
                                key = (which[0], 2 * s + j)
                                o = open_job(key)
                                if key == ("g", 0):
                                    ins = first_products(o, (which, s), h_hi[1], h_lo, 0, 2 * l + 1)
                                else:
                                    ins = products(o, (which, s), j, 0, KT, h_hi[1], h_lo, 0, True, True)
                                close(ins, key)

                    def hidden_ready(k):
                        pe.wait_ge(hidden_split, k + 1)

                    for c in range(OUT_CHUNKS):
                        keys = [("down", 2 * c), ("down", 2 * c + 1)]
                        o = [open_job(key) for key in keys]
                        for p, (k0, k1) in enumerate(DOWN_PIECES):
                            last = p == len(DOWN_PIECES) - 1
                            for j in range(2):
                                ins = products(o[j], ("down", c, p), j, k0, k1, hidden_hi, hidden_lo, 0, p == 0,
                                               last, hidden_ready if c == 0 and j == 0 else None)
                                if last:
                                    close(ins, keys[j])
                            if not last:
                                ins.then_inc(unit_read, 1)
                        if c:
                            for k in (2 * c - 2, 2 * c - 1):
                                mean_square(l + 1, 0, k)
                    for k in range(KT - 2, KT):
                        mean_square(l + 1, 0, k)


            def rows_of(src, name):
                for i in range(4):
                    key = (name, i)
                    o = open_job(key)
                    for j in range(4):
                        k = 4 * (i % 2) + j
                        t0, t1 = TOKENS[1 + i // 2]
                        ins = pe.transpose(o[:, j * P:(j + 1) * P], src[:, k, t0:t1], ident)
                    close(ins, key)

            for d in range(KT):
                drained(pe, ("mix", DEPTH - 1, d))
            rows_of(X, "acc")
            key = ("lt",)
            o = open_job(key)
            for k in range(KT):
                pe.wait_ge(h_ready, (2 * DEPTH - 1) * KT + k + 1)
                ins = pe.matmul(o[0:N_EXPERTS, 0:SEQ], param("router", k * N_EXPERTS, N_EXPERTS), H[:, k, N_META:T],
                                start=k == 0, stop=k == KT - 1)
            close(ins, key)
            drained(pe, ("lt",))
            key = ("logits",)
            o = open_job(key)
            for t in range(2):
                ins = pe.transpose(o[:, t * N_EXPERTS:(t + 1) * N_EXPERTS], logits_t[0:N_EXPERTS, t * P:(t + 1) * P],
                                   ident[0:N_EXPERTS, 0:N_EXPERTS])
            close(ins, key)
            rows_of(H, "ht")
            key = ("rank",)
            o = open_job(key)
            pe.wait_ge(mask_ready, 1)
            mask = [route[:, 0, t * (ROUNDS + 1):t * (ROUNDS + 1) + N_EXPERTS] for t in range(2)]
            pe.matmul(o[:, 0:8], const("before"), mask[0], start=True, stop=True)
            pe.matmul(o[:, 8:16], const("ones"), mask[0], start=True, stop=False)
            close(pe.matmul(o[:, 8:16], const("before"), mask[1], start=False, stop=True), key)
            key = ("count",)
            o = open_job(key)
            pe.matmul(o[:, 0:8], const("ones"), mask[0], start=True, stop=False)
            close(pe.matmul(o[:, 0:8], const("ones"), mask[1], start=False, stop=True), key)
            for i in range(4):
                drained(pe, ("ht", i))

            def gather(half, o):
                for m in range(4):
                    d = 4 * half + m
                    for t in range(2):
                        ins = pe.matmul(o[:, m * CAP:(m + 1) * CAP], h_rows[:, t, d * P:(d + 1) * P],
                                        pick[:, t, :], start=t == 0, stop=t == 1)
                return ins

            pe.wait_ge(pick_ready, 1)
            for half in range(2):
                key = ("te", half)
                close(gather(half, open_job(key)), key)
            for half in range(2):
                drained(pe, ("te", half))

            def scatter(i, ago=0):
                for name in ("pt", "y0", "y1"):
                    b, n = expert_job(name, i, before=ago * EXPERT_USES[EXPERT_JOB[name][0]])
                    pe.wait_ge(bank_drained[b], n)
                for t in range(2):
                    for half in range(2):
                        name = f"sc{t}{half}"
                        b = EXPERT_JOB[name][0]
                        _, n = expert_job(name, i, before=ago * EXPERT_USES[b] + 1)
                        pe.wait_ge(bank_drained[b], n)
                        slots, cols = pick_t[:, t * P:(t + 1) * P], slice(half * WIDE, (half + 1) * WIDE)
                        pe.matmul(ps[b][:, :], slots, y_hi[:, cols], start=True, stop=False)
                        pe.matmul(ps[b][:, :], slots, y_lo[:, cols], start=False, stop=True).then_inc(
                            bank_full[b], 1)

            def expert(i, scatter_last):
                def reopen(name):
                    b, n = expert_job(name, i, before=1)
                    pe.wait_ge(bank_drained[b], n)
                    return ps[b]

                def ends(ins, name):
                    ins.then_inc(bank_full[EXPERT_JOB[name][0]], 1)

                def read_out(name):
                    b, n = expert_job(name, i)
                    pe.wait_ge(bank_drained[b], n)

                def unit(u):
                    n = UNIT_AT[u]
                    pe.wait_ge(unit_split, i * N_UNITS + (N_TRUNK + n + 1))
                    return w_hi[:, n % SLOTS, :], w_lo[:, n % SLOTS, :]

                def into(kind, s):
                    o = reopen(f"{kind}{s}")
                    for q in range(4):
                        hi, lo = unit((kind, s, q))
                        for m in range(2):
                            k = 2 * q + m
                            cols = slice(m * WIDE, (m + 1) * WIDE)
                            pe.matmul(o[:, :], te_hi[:, k, :], hi[:, cols], start=k == 0, stop=False)
                            pe.matmul(o[:, :], te_hi[:, k, :], lo[:, cols], start=False, stop=False)
                            ins = pe.matmul(o[:, :], te_lo[:, k, :], hi[:, cols], start=False, stop=k == KT - 1)
                        if q < 3:
                            ins.then_inc(unit_read, 1)
                    ends(ins, f"{kind}{s}")

                def turn(s):
                    o = reopen(f"tr{s}")
                    read_out(f"up{s}")
                    for m in range(FF_PER_STEP):
                        ins = pe.transpose(o[:, m * CAP:(m + 1) * CAP], hid[:, m * P:(m + 1) * P], ident)
                    ends(ins, f"tr{s}")

                def down(s, q):
                    if s == 0 and q == 0:
                        reopen("y0")
                        reopen("y1")
                    if q == 0:
                        read_out(f"tr{s}")
                    hi, lo = unit(("down", s, q))
                    last = s == EXP_STEPS - 1 and q == 3
                    for half in range(2):
                        o = ps[EXPERT_JOB[f"y{half}"][0]]
                        cols = slice(half * WIDE, (half + 1) * WIDE)
                        h_hi, h_lo = hid_hi[:, s % 2, q, :], hid_lo[:, s % 2, q, :]
                        pe.matmul(o[:, :], h_hi, hi[:, cols], start=s == 0 and q == 0, stop=False)
                        pe.matmul(o[:, :], h_hi, lo[:, cols], start=False, stop=False)
                        ins = pe.matmul(o[:, :], h_lo, hi[:, cols], start=False, stop=last)
                        if last:
                            ends(ins, f"y{half}")
                    if not last:
                        ins.then_inc(unit_read, 1)

                for s in range(EXP_STEPS):
                    into("gate", s)
                    if s == 0 and scatter_last:
                        scatter(i, 1)
                    if s:
                        turn(s - 1)
                    into("up", s)
                    if s == 1:
                        o = reopen("pt")
                        for t in range(2):
                            ins = pe.transpose(o[:, t * P:(t + 1) * P], pick[:, t, :], ident)
                        ends(ins, "pt")
                    if s == EXP_STEPS - 1:
                        pe.wait_ge(pick_ready, i + 2)
                        for half in range(2):
                            ends(gather(half, reopen(f"te{half}")), f"te{half}")
                    if s:
                        for q in range(4):
                            if s == EXP_STEPS - 1 and q == 3:
                                turn(s)
                            down(s - 1, q)
                for q in range(4):
                    down(EXP_STEPS - 1, q)
                for half in range(2):
                    read_out(f"te{half}")

            expert(0, False)
            with pe.Fori(1, N_EXPERTS) as e:
                expert(e, True)
            scatter(N_EXPERTS - 1)
            pe.wait_ge(count_ready, 1)
            count = pe.value_load(most[0:1, 0:1])
            with pe.If(count > CAP):
                with pe.Fori(N_EXPERTS, ROUNDS) as i:
                    expert(i, False)
                    scatter(i)

        @block.scalar
        def _(act):
            n_first = CONST_COLS["eps"][0] + 1
            act.dma_start(cst[:, 0:n_first], consts[:, 0:n_first]).then_inc(consts_loaded, 16)
            act.dma_start(par[:, :], params).then_inc(params_loaded, 16)
            act.dma_start(tab[0:N_BUCKETS, :], bias_table).then_inc(dist_loaded, 16)
            act.dma_start(hot[0:N_BUCKETS, :], onehot).then_inc(dist_loaded, 16)
            act.dma_start(mrow[0:N_BIAS, :], mask_row).then_inc(dist_loaded, 16)
            act.dma_start(cst[:, n_first:N_CONST], consts[:, n_first:N_CONST]).then_inc(all_consts_loaded, 16)
            eps = const("eps")

            def square_of(l, which, k):
                t0 = first_token(l) if which else 0
                drained(act, ("mix", l, k) if which else ("down", k) if l else ("xt", k))
                nc.scalar.activation(H[:, k, t0:T], X[:, k, t0:T], ACT.Square).then_inc(squared, 1)

            def load_table(f):
                nc.scalar.activation(lam_s[:, 4 * DEPTH - 1:4 * DEPTH], eps, f)

            def round_unit(n):
                c = n // 2
                act.wait_ge(ring_full[c % TRUNK_RING], 16 * (c // TRUNK_RING + 1))
                if n >= SLOTS:
                    act.wait_ge(*trunk_unit_free(n))
                nc.scalar.copy(t_hi[:, n % SLOTS, 0:unit_width(n)], trunk_weights(n)).then_inc(unit_rounded, 1)

            act.wait_ge(consts_loaded, 16)
            load_table(ACT.Sqrt)
            for k in range(KT):
                square_of(0, 0, k)

            def norm(l, which):
                t0 = first_token(l) if which else 0
                split = (l, which) != (DEPTH - 1, 1)
                n = 2 * CHUNK_NO["gate", 0] if which else 2 * CHUNK_NO["in", l, 0]
                o = full(act, ("ms", l, which))
                drain(nc.scalar.activation(rstd[:, 0, t0:T], o[:, t0:T], ACT.Sqrt, bias=eps), ("ms", l, which))
                if (l, which) == (0, 0):
                    round_unit(0)
                    round_unit(1)
                if split:
                    for k in range(KT):
                        act.wait_ge(h_ready, (2 * l + which) * KT + k + 1)
                        nc.scalar.copy(h_hi[which][:, k, t0:T], H[:, k, t0:T]).then_inc(h_rounded, 1)
                    round_unit(n + 2)
                    round_unit(n + 3)

            def head_std(l, name):
                n = NORMED.index(name)
                t0 = first_token(l) if name[0] == "q" else 0
                o = full(act, ("st", l, name))
                if n >= 2:
                    drained(act, ("z", l, NORMED[n - 2]))
                drain(nc.scalar.activation(rstd[:, n % 2, t0:T], o[:, t0:T], ACT.Sqrt, bias=eps),
                      ("st", l, name))

            for l in range(DEPTH):
                norm(l, 0)
                waiting = None
                for name in PROJECTIONS:
                    key = ("z", l, name)
                    o = full(act, key)
                    if normed(name):
                        n = NORMED.index(name)
                        t0 = first_token(l) if name[0] == "q" else 0
                        if n >= 2:
                            full(act, ("st", l, NORMED[n - 2]))
                        nc.scalar.activation(square[:, n % 2, t0:T], o[:, t0:T], ACT.Square).then_inc(head_squares, 1)
                    elif name == "va0":
                        nc.scalar.copy(v_all[0:N_META, META, 0:128], o[0:N_META, 128:256])
                        drain(nc.scalar.copy(v_all[:, REAL0, 0:128], o[:, 384:512]), key)
                    elif name == "va1":
                        drain(nc.scalar.copy(v_all[:, REAL1, 0:128], o[:, 128:256]), key)
                    elif name == "vb0":
                        nc.scalar.copy(v_all[0:N_META, META, 128:384], o[0:N_META, 0:256])
                        drain(nc.scalar.copy(v_all[:, REAL0, 128:384], o[:, 256:512]), key)
                    elif name == "vb1":
                        drain(nc.scalar.copy(v_all[:, REAL1, 128:384], o[:, 0:256]), key)
                    else:
                        drain(nc.scalar.copy(pool_u[:, int(name[2]), N_META:PADDED], o[:, 0:T]), key)
                    if waiting:
                        head_std(l, waiting)
                    waiting = name if normed(name) else None
                    if name == "vb1":
                        load_table(ACT.Exp)
                        if l == 0:
                            act.wait_ge(lam_dot, 1)
                            nc.scalar.activation(lam_s[:, 0:2 * DEPTH], lam_s[:, 0:2 * DEPTH], ACT.Exp).then_inc(
                                lam_exp, 1)
                    if name in CHUNK_ENDS[:-2]:
                        for q in range(2):
                            round_unit(2 * (CHUNK_NO["in", l, 0] + CHUNK_ENDS.index(name) + 2) + q)
                for i in range(2):
                    o = full(act, ("kd", l, i))
                    drain(nc.scalar.copy(k_dup[:, i, :], o[:, 0:T]), ("kd", l, i))
                if l == 0:
                    for h in range(0, N_BIAS, 2):
                        o = full(act, ("bias", h))
                        drain(nc.scalar.copy(bias[:, h, :], o[:, 0:T]), ("bias", h))
                gs = groups(l)
                for n, s, c, o_unit, v, fin, tr in unit_steps(l):
                    if n == pool_step_no(l):
                        for j in range(2):
                            o = full(act, ("pool", l, j))
                            nc.scalar.activation(mix_hi[:, 6 + j, :], o[:, 0:T], ACT.Copy,
                                                 scale=param("pool_scale", 2 * l + j, 1)).then_inc(mix_rounded, 1)
                    if s:
                        g, qt, h = s
                        nq = TOKENS[qt][1] - TOKENS[qt][0]
                        kts = key_tiles(g, qt)
                        nk = TOKENS[kts[-1]][1] - TOKENS[kts[0]][0]
                        m = gs.index(s[:2])
                        for i in range(1 + (g == "B")):
                            no = SCORE_NO[l, s, i]
                            col = h if g == "A" else 2 * h + i
                            drained(act, ("s", l, s, i))
                            if no >= PROB_SLOTS:
                                ol, ou = SCORE_OWNER[no - PROB_SLOTS]
                                full(act, ("pt", ol, ou))
                            nc.scalar.activation(probs[0:nq, no % PROB_SLOTS, 0:nk], scores[0:nq, no % SCORE_SLOTS, 0:nk],
                                                 ACT.Exp, bias=low[0:nq, m, col:col + 1], scale=-1.0,
                                                 accum_out=total[0:nq, m, col:col + 1]).then_inc(exp_ready, 1)
                        if g == "A" and h == A_HEADS - 1:
                            act.wait_ge(sink_gap, A_GROUP_NO[l, s[:2]] + 1)
                            nc.scalar.activation(gap[0:nq, m, :], gap[0:nq, m, :], ACT.Exp).then_inc(sink_exp, 1)
                    if o_unit and o_unit[0] == "B":
                        copy_probs(act, nc.scalar.copy, l, o_unit, n)
                    if fin and fin[0] == "B":
                        nq = TOKENS[fin[1]][1] - TOKENS[fin[1]][0]
                        m = gs.index(fin)
                        act.wait_ge(out_mean, B_GROUP_NO[l, fin] + 1)
                        nc.scalar.activation(std_o[0:nq, m, :], mean_o[0:nq, m, :], ACT.Sqrt, bias=eps[0:nq],
                                             scale=1.0 / B_V).then_inc(out_std, 1)
                    if tr:
                        g, qt = tr
                        t0, t1 = TOKENS[qt]
                        o = full(act, ("ot", l, tr))
                        j0, nj = (0, 4) if g == "A" else (4, 2)
                        nc.scalar.copy(mix_hi[:, j0:j0 + nj, t0:t1],
                                       o[:, 0:nj * P].rearrange("p (j t) -> p j t", j=nj)[:, :, 0:t1 - t0]).then_inc(
                                           mix_rounded, 1)
                load_table(ACT.Sqrt)
                for d in range(KT):
                    square_of(l, 1, d)
                    if d in (1, 3) or (d == 5 and l < DEPTH - 1):
                        for q in range(2):
                            round_unit(2 * CHUNK_NO["out", l, 0] + SLOTS + d - 1 + q)
                norm(l, 1)
                if l < DEPTH - 1:
                    for n in FFN_UNITS:
                        if n + SLOTS < FFN_UNITS.stop + 2:
                            round_unit(n + SLOTS)
                        (kind, s, *piece), q = TRUNK_UNITS[n]
                        f = 2 * s + q
                        if kind == "gate":
                            o = full(act, ("g", f))
                            if f >= 2:
                                drained(act, ("u", f - 2))
                            drain(nc.scalar.activation(probs[:, f % 2, :], o[:, 0:T], ACT.Silu), ("g", f))
                        if kind == "up":
                            drained(act, ("u", f))
                            nc.scalar.copy(hidden_hi[:, f, :], hidden[:, f, :]).then_inc(hidden_rounded, 1)
                        if kind == "down" and piece == [len(DOWN_PIECES) - 1] and q == 1:
                            square_of(l + 1, 0, 2 * s)
                            square_of(l + 1, 0, 2 * s + 1)

            def round_y(i, ago=0):
                for half in range(2):
                    b, n = expert_job(f"y{half}", i, before=ago * EXPERT_USES[EXPERT_JOB[f"y{half}"][0]])
                    act.wait_ge(bank_full[b], n)
                    nc.scalar.copy(y_hi[:, half * WIDE:(half + 1) * WIDE], ps[b][:, :]).then_inc(y_rounded, 1)

            def round_expert_unit(n, i, slot_used=True):
                if n % 2 == 0:
                    c = n // 2
                    before = len(CHUNKS) // TRUNK_RING if c % RING < TRUNK_RING else 0
                    act.wait_ge(ring_full[c % RING], (i * ring_per + (before + c // RING + 1)) * 16)
                if slot_used:
                    act.wait_ge(*unit_free(n, i))
                nc.scalar.copy(w_hi[:, n % SLOTS, :], unit_weights(n)).then_inc(unit_rounded, 1)

            for name, rows in (("acc", acc), ("ht", h_rows)):
                for i in range(4):
                    o = full(act, (name, i))
                    at = (i % 2) * WIDE
                    drain(nc.scalar.copy(rows[:, i // 2, at:at + WIDE], o[:, :]), (name, i))
                if name == "acc":
                    for n in range(SLOTS):
                        round_expert_unit(n, 0, False)
            def round_te(half, o):
                nc.scalar.copy(te_hi[:, 4 * half:4 * half + 4, :],
                               o[:, :].rearrange("p (d c) -> p d c", d=4)).then_inc(te_rounded, 1)

            for half in range(2):
                round_te(half, full(act, ("te", half)))
            act.wait_ge(gap_ready, 1)
            nc.scalar.activation(rt[:, 2:4], rt[:, 0:2], ACT.Exp).then_inc(gap_exp, 1)

            load_table(ACT.Silu)

            def expert(i, first, copy_last):
                def taken(name):
                    b, n = expert_job(name, i)
                    act.wait_ge(bank_full[b], n)
                    return ps[b]

                for n, u in enumerate(EXPERT_UNITS):
                    if n >= first:
                        round_expert_unit(n, i)
                    if n == SLOTS - 1 and copy_last:
                        round_y(i, 1)
                    kind, s, q = EXPERT_UNITS[n - SLOTS + 1]
                    if n < SLOTS - 1:
                        continue
                    if kind == "gate" and q == 3:
                        o = taken(f"gate{s}")
                        if s:
                            b, m = expert_job(f"up{s - 1}", i)
                            act.wait_ge(bank_drained[b], m)
                        nc.scalar.activation(silu[:, :], o[:, :], ACT.Silu).then_inc(
                            bank_drained[EXPERT_JOB[f"gate{s}"][0]], 1)
                    if turned(n) is not None:
                        round_hidden(i, turned(n), taken)
                    if (kind, s, q) == ("down", EXP_STEPS - 2, 1):
                        for half in range(2):
                            round_te(half, taken(f"te{half}"))

            def round_hidden(i, s, taken):
                o = taken(f"tr{s}")
                nc.scalar.copy(hid_hi[:, s % 2, :, :], o[:, :].rearrange("p (m c) -> p m c", m=FF_PER_STEP)).then_inc(
                    hid_rounded, 1)

            expert(0, SLOTS, False)
            with act.Fori(1, N_EXPERTS) as e:
                expert(e, 0, True)
            round_y(N_EXPERTS - 1)
            act.wait_ge(count_ready, 1)
            count = act.value_load(most[0:1, 0:1])
            with act.If(count > CAP):
                with act.Fori(N_EXPERTS, ROUNDS) as i:
                    expert(i, 0, False)
                    round_y(i)

        @block.vector
        def _(dve):
            V = nc.vector
            dve_steps = [0]

            def step(ins):
                dve_steps[0] += 1
                ins.then_inc(dve_step, 1)
                dve.wait_ge(dve_step, dve_steps[0])

            for k in range(KT):
                o = full(dve, ("xt", k))
                drain(V.tensor_copy(X[:, k, :], o[:, 0:T]), ("xt", k))

            def split_unit(n):
                dve.wait_ge(unit_rounded, n + 1)
                w = unit_width(n)
                V.tensor_tensor(t_lo[:, n % SLOTS, 0:w], trunk_weights(n), t_hi[:, n % SLOTS, 0:w].bitcast(F32),
                                ALU.subtract).then_inc(unit_split, 1)

            def norm(l, which):
                t0 = first_token(l) if which else 0
                split = (l, which) != (DEPTH - 1, 1)
                n = 2 * CHUNK_NO["gate", 0] if which else 2 * CHUNK_NO["in", l, 0]
                drained(dve, ("ms", l, which))
                step(V.reciprocal(rstd[:, 0, t0:T], rstd[:, 0, t0:T]))
                gain = param("g_ffn" if which else "g_mix", l * KT, KT)
                for k in range(KT):
                    if (l, which) == (0, 0) and k == KT // 2:
                        dve.wait_ge(unit_split, 1)
                        split_unit(1)
                    V.scalar_tensor_tensor(H[:, k, t0:T], X[:, k, t0:T], gain[:, k:k + 1], rstd[:, 0, t0:T],
                                           ALU.mult, ALU.mult).then_inc(h_ready, 1)
                if split:
                    for k in range(KT):
                        dve.wait_ge(h_rounded, (2 * l + which) * KT + k + 1)
                        V.tensor_tensor(h_lo[:, k, t0:T], H[:, k, t0:T], h_hi[which][:, k, t0:T].bitcast(F32),
                                        ALU.subtract).then_inc(h_split, 1)
                    split_unit(n + 2)
                    split_unit(n + 3)

            def normalise(l, name):
                n = NORMED.index(name)
                t0 = first_token(l) if name[0] == "q" else 0
                gain = gains[:, l, ["qa", "ka", "qb", "kb"].index(name[:2]):][:, 0:1]
                dst = {"qa": q_a[:, int(name[2]), t0:T], "ka": k_a[:, t0:T], "qb": q_b[:, int(name[2]) % 2, t0:T],
                       "kb": k_b[:, int(name[2]) % 2, t0:T]}[name[:2]]
                drained(dve, ("st", l, name))
                step(V.reciprocal(rstd[:, n % 2, t0:T], rstd[:, n % 2, t0:T]))
                o = full(dve, ("z", l, name))
                drain(V.scalar_tensor_tensor(dst, o[:, t0:T], gain, rstd[:, n % 2, t0:T], ALU.mult, ALU.mult),
                      ("z", l, name))

            def derive_parameters():
                dve.wait_ge(params_loaded, 16)
                lam_p = param("lam").rearrange("p (l a b n) -> p l a b n", l=DEPTH, a=2, b=2)
                for l in range(DEPTH):
                    ins = V.tensor_tensor(lam_t[:, 2 * l:2 * l + 2, :], lam_p[:, l, :, 0, :], lam_p[:, l, :, 1, :], ALU.mult)
                step(ins)
                V.tensor_reduce(lam_s[:, 0:2 * DEPTH], lam_t[:, :, :], AX.X, ALU.add).then_inc(lam_dot, 1)
                V.tensor_scalar(neg_sink[:, :], param("sinks"), -1.0, None, ALU.mult)
                for l in range(DEPTH):
                    V.tensor_scalar(gains[:, l, 0:1], param("gain_a", 2 * l, 1), -(HD ** -0.5), None, ALU.mult)
                    V.tensor_copy(gains[:, l, 1:2], param("gain_a", 2 * l + 1, 1))
                    V.tensor_scalar(gains[:, l, 2:3], param("gain_b", 2 * l, 1), -(B_QK ** -0.5), None, ALU.mult)
                    V.tensor_copy(gains[:, l, 3:4], param("gain_b", 2 * l + 1, 1))
                    step(V.tensor_scalar(g_out[:, l, :], param("g_out", l * B_V, B_V), 1.0 - lam_init(l), None, ALU.mult))
                o = full(dve, ("dist",))
                drain(V.tensor_tensor(dist[0:N_BIAS, :], mrow[0:N_BIAS, :], o[0:N_BIAS, 0:N_DIST], ALU.subtract),
                      ("dist",))

            for l in range(DEPTH):
                if l == 0:
                    dve.wait_ge(params_loaded, 16)
                norm(l, 0)
                if l == 0:
                    derive_parameters()
                waiting = None
                for name in PROJECTIONS:
                    if waiting:
                        normalise(l, waiting)
                    waiting = name if normed(name) else None
                    if name in CHUNK_ENDS[:-2]:
                        for q in range(2):
                            split_unit(2 * (CHUNK_NO["in", l, 0] + CHUNK_ENDS.index(name) + 2) + q)
                if l == 0:
                    dve.wait_ge(lam_exp, 1)
                    for m in range(DEPTH):
                        step(V.tensor_tensor(lam_s[:, 2 * m + 1:2 * m + 2], lam_s[:, 2 * m + 1:2 * m + 2],
                                             lam_s[:, 2 * m:2 * m + 1], ALU.subtract))
                        step(V.tensor_scalar(lam_s[:, 4 + m:5 + m], lam_s[:, 2 * m + 1:2 * m + 2], -lam_init(m), None,
                                             ALU.add))
                    for h in range(1, N_BIAS, 2):
                        o = full(dve, ("bias", h))
                        drain(V.tensor_copy(bias[:, h, :], o[:, 0:T]), ("bias", h))
                    for h in range(N_BIAS):
                        drained(dve, ("bias", h))
                gs = groups(l)
                for n, s, c, o_unit, v, fin, tr in unit_steps(l):
                    if n == pool_step_no(l):
                        for j in range(2):
                            o = full(dve, ("pool", l, j))
                            dve.wait_ge(mix_rounded, mix_count(l, ("pool", j)))
                            drain(V.scalar_tensor_tensor(
                                mix_lo[:, 6 + j, :], o[:, 0:T], param("pool_scale", 2 * l + j, 1),
                                mix_hi[:, 6 + j, :].bitcast(F32), ALU.mult, ALU.subtract), ("pool", l, j))
                    if s:
                        g, qt, h = s
                        nq = TOKENS[qt][1] - TOKENS[qt][0]
                        kts = key_tiles(g, qt)
                        k0, k1 = TOKENS[kts[0]][0], TOKENS[kts[-1]][1]
                        m = gs.index(s[:2])
                        j0 = bias_column(qt) + k0
                        head = h if g == "A" else A_HEADS + h
                        for i in range(1 + (g == "B")):
                            no = SCORE_NO[l, s, i]
                            col = h if g == "A" else 2 * h + i
                            o = full(dve, ("s", l, s, i))
                            if no >= SCORE_SLOTS:
                                dve.wait_ge(exp_ready, no - SCORE_SLOTS + 1)
                            start = neg_sink[0:nq, l * A_HEADS + h:l * A_HEADS + h + 1] if g == "A" else 3.0e38
                            drain(V.tensor_tensor_reduce(
                                scores[0:nq, no % SCORE_SLOTS, 0:k1 - k0], o[0:nq, 0:k1 - k0],
                                bias[0:nq, head, j0:j0 + k1 - k0], 1.0, start, ALU.add, ALU.min,
                                low[0:nq, m, col:col + 1]), ("s", l, s, i))
                        if g == "A" and h == A_HEADS - 1:
                            drained(dve, ("s", l, s, 0))
                            V.tensor_tensor(gap[0:nq, m, :], low[0:nq, m, :],
                                            neg_sink[0:nq, l * A_HEADS:(l + 1) * A_HEADS],
                                            ALU.subtract).then_inc(sink_gap, 1)
                    if c and c[0] == "B":
                        g, qt, h = c
                        nq = TOKENS[qt][1] - TOKENS[qt][0]
                        kts = key_tiles(g, qt)
                        nk = TOKENS[kts[-1]][1] - TOKENS[kts[0]][0]
                        m = gs.index(c[:2])
                        dve.wait_ge(exp_ready, SCORE_NO[l, c, 1] + 1)
                        step(V.reciprocal(share[0:nq, m, 2 * h:2 * h + 2], total[0:nq, m, 2 * h:2 * h + 2]))
                        f = factor[0:nq, l, h:h + 1]
                        step(V.scalar_tensor_tensor(f, share[0:nq, m, 2 * h + 1:2 * h + 2], lam_s[0:nq, 4 + l:5 + l],
                                                    total[0:nq, m, 2 * h:2 * h + 1], ALU.mult, ALU.mult))
                        p0 = probs[0:nq, SCORE_NO[l, c, 0] % PROB_SLOTS, 0:nk]
                        p1 = probs[0:nq, SCORE_NO[l, c, 1] % PROB_SLOTS, 0:nk]
                        V.scalar_tensor_tensor(p0, p1, f, p0, ALU.mult, ALU.add).then_inc(probs_mixed, 1)
                    if o_unit and o_unit[0] == "A":
                        copy_probs(dve, V.tensor_copy, l, o_unit, n)
                    if fin:
                        g, qt = fin
                        nq = TOKENS[qt][1] - TOKENS[qt][0]
                        m = gs.index(fin)
                        nh = A_HEADS if g == "A" else B_HEADS
                        hv = heads[0:nq, m % 2, 0:nh * HD].rearrange("p (h d) -> p h d", h=nh)
                        if m >= 2:
                            full(dve, ("ot", l, gs[m - 2]))
                        if g == "A":
                            dve.wait_ge(sink_exp, A_GROUP_NO[l, fin] + 1)
                            step(V.tensor_tensor(share[0:nq, m, :], total[0:nq, m, :], gap[0:nq, m, :], ALU.add))
                            step(V.reciprocal(share[0:nq, m, :], share[0:nq, m, :]))
                            sh = share[0:nq, m, :]
                        else:
                            sh = share[0:nq, m, :].rearrange("p (h c) -> p h c", c=2)[:, :, 0]
                        o = full(dve, ("o", l, fin))
                        ov = o[0:nq, 0:nh * HD].rearrange("p (h d) -> p h d", h=nh)
                        drain(V.tensor_tensor(hv, ov, sh.unsqueeze(2).to_broadcast([nq, nh, HD]), ALU.mult),
                              ("o", l, fin))
                        if g == "B":
                            drained(dve, ("o", l, fin))
                            tmp = square[0:nq, 0, 0:nh * HD].rearrange("p (h d) -> p h d", h=nh)
                            step(V.tensor_tensor(tmp, hv, hv, ALU.mult))
                            V.tensor_reduce(mean_o[0:nq, m, :], tmp, AX.X, ALU.add).then_inc(out_mean, 1)
                            dve.wait_ge(out_std, B_GROUP_NO[l, fin] + 1)
                            step(V.reciprocal(std_o[0:nq, m, :], std_o[0:nq, m, :]))
                            step(V.tensor_tensor(hv, hv, std_o[0:nq, m, :].unsqueeze(2).to_broadcast([nq, nh, HD]),
                                                 ALU.mult))
                            V.tensor_tensor(hv, hv, g_out[0:nq, l, :].unsqueeze(1).to_broadcast([nq, nh, HD]),
                                            ALU.mult).then_inc(heads_ready, 1)
                    if tr:
                        g, qt = tr
                        t0, t1 = TOKENS[qt]
                        o = full(dve, ("ot", l, tr))
                        j0, nj = (0, 4) if g == "A" else (4, 2)
                        dve.wait_ge(mix_rounded, mix_count(l, tr))
                        drain(V.tensor_tensor(mix_lo[:, j0:j0 + nj, t0:t1],
                                              o[:, 0:nj * P].rearrange("p (j t) -> p j t", j=nj)[:, :, 0:t1 - t0],
                                              mix_hi[:, j0:j0 + nj, t0:t1].bitcast(F32), ALU.subtract),
                              ("ot", l, tr))

                t0 = first_token(l)

                def residual(name, d):
                    key = (name, l, d) if name == "mix" else (name, d)
                    o = full(dve, key)
                    drain(V.tensor_tensor(X[:, d, t0:T], X[:, d, t0:T], o[:, t0:T], ALU.add), key)

                for d in range(KT):
                    residual("mix", d)
                    if d in (1, 3) or (d == 5 and l < DEPTH - 1):
                        for q in range(2):
                            split_unit(2 * CHUNK_NO["out", l, 0] + SLOTS + d - 1 + q)
                norm(l, 1)
                if l < DEPTH - 1:
                    def split_hidden(f):
                        dve.wait_ge(hidden_rounded, f + 1)
                        V.tensor_tensor(hidden_lo[:, f, :], hidden[:, f, :], hidden_hi[:, f, :].bitcast(F32),
                                        ALU.subtract).then_inc(hidden_split, 1)

                    for n in FFN_UNITS:
                        if n + SLOTS < FFN_UNITS.stop + 2:
                            split_unit(n + SLOTS)
                        (kind, s, *piece), q = TRUNK_UNITS[n]
                        f = 2 * s + q
                        if kind == "up":
                            drained(dve, ("g", f))
                            o = full(dve, ("u", f))
                            drain(V.tensor_tensor(hidden[:, f, :], probs[:, f % 2, :], o[:, 0:T], ALU.mult),
                                  ("u", f))
                            if f:
                                split_hidden(f - 1)
                        elif kind == "down" and s == 0 and piece == [0] and q == 0:
                            split_hidden(FF_TILES - 1)
                        elif kind == "down" and piece == [len(DOWN_PIECES) - 1] and q == 1:
                            residual("down", 2 * s)
                            residual("down", 2 * s + 1)

            step(V.memset(route[:, :, :], 0.0))
            o = full(dve, ("lt",))
            drain(V.tensor_copy(logits_t[0:N_EXPERTS, :], o[0:N_EXPERTS, 0:SEQ]), ("lt",))
            def split_expert_unit(n, i):
                dve.wait_ge(unit_rounded, i * N_UNITS + (N_TRUNK + n + 1))
                V.tensor_tensor(w_lo[:, n % SLOTS, :], unit_weights(n), w_hi[:, n % SLOTS, :].bitcast(F32),
                                ALU.subtract).then_inc(unit_split, 1)

            o = full(dve, ("logits",))
            drain(V.tensor_copy(lg[:, :, :], o[:, 0:2 * N_EXPERTS].rearrange("p (t e) -> p t e", t=2)),
                  ("logits",))
            drained(dve, ("logits",))
            for t in range(2):
                step(V.max(top[:, t, :], lg[:, t, :]))
            V.tensor_tensor(rt[:, 0:2], top[:, :, 1], top[:, :, 0], ALU.subtract).then_inc(gap_ready, 1)
            for t in range(2):
                step(V.max_index(idx_u[:, t, :], top[:, t, :], lg[:, t, :]))
            step(V.tensor_copy(idx[:, :, :], idx_u[:, :, :]))
            for t in range(2):
                V.tensor_scalar(one[:, t, :], const("iota8"), idx[:, t, 0:1], None, ALU.is_equal)
                step(V.tensor_scalar(two[:, t, :], const("iota8"), idx[:, t, 1:2], None, ALU.is_equal))
            rv = route.rearrange("p a (t r) -> p a t r", t=2)
            first = slice(0, N_EXPERTS)
            V.tensor_tensor(rv[:, 0, :, first], one[:, :, :], two[:, :, :], ALU.add).then_inc(mask_ready, 1)
            full(dve, ("acc", 3))
            split_expert_unit(0, 0)
            o = full(dve, ("rank",))
            drain(V.tensor_copy(rv[:, 1, :, first], o[:, 0:16].rearrange("p (t e) -> p t e", t=2)), ("rank",))
            drained(dve, ("rank",))
            step(V.tensor_copy(cur[:, :, :], rv[:, 0:2, :, 0]))
            for t in range(2):
                ins = V.tensor_scalar(pick[:, t, :], const("iota"), cur[:, 1, t:t + 1], cur[:, 0, t:t + 1],
                                      ALU.is_equal, ALU.mult)
            ins.then_inc(pick_ready, 1)
            for n in range(1, SLOTS):
                split_expert_unit(n, 0)
            for i in range(4):
                drained(dve, ("acc", i))

            def split_te(half, o, b):
                V.tensor_tensor(te_lo[:, 4 * half:4 * half + 4, :], o[:, :].rearrange("p (d c) -> p d c", d=4),
                                te_hi[:, 4 * half:4 * half + 4, :].bitcast(F32),
                                ALU.subtract).then_inc(bank_drained[b], 1)

            for half in range(2):
                dve.wait_ge(te_rounded, half + 1)
                split_te(half, full(dve, ("te", half)), bank_of["te", half][0])
            drain(V.tensor_reduce(rt[:, 10:11], full(dve, ("count",))[:, 0:8], AX.X, ALU.max), ("count",))
            drained(dve, ("count",))
            V.tensor_copy(most[:, 0:1], rt[:, 10:11]).then_inc(count_ready, 1)
            dve.wait_ge(gap_exp, 1)
            step(V.tensor_scalar(rt[:, 4:6], rt[:, 2:4], 1.0, None, ALU.add))
            step(V.reciprocal(rt[:, 6:8], rt[:, 4:6]))
            step(V.tensor_tensor(rt[:, 8:10], rt[:, 6:8], rt[:, 2:4], ALU.mult))
            for t in range(2):
                step(V.tensor_scalar(rv[:, 2, t, first], one[:, t, :], rt[:, 6 + t:7 + t], None, ALU.mult))
                step(V.scalar_tensor_tensor(rv[:, 2, t, first], two[:, t, :], rt[:, 8 + t:9 + t], rv[:, 2, t, first],
                                            ALU.mult, ALU.add))
            for p in range(1, PASSES):
                cols = slice(p * N_EXPERTS, (p + 1) * N_EXPERTS)
                V.tensor_copy(rv[:, 0, :, cols], rv[:, 0, :, first])
                V.tensor_copy(rv[:, 2, :, cols], rv[:, 2, :, first])
                step(V.tensor_scalar(rv[:, 1, :, cols], rv[:, 1, :, first], -float(p * CAP), None, ALU.add))

            def pick_tokens(cols, done):
                V.tensor_copy(cur[:, :, :], cols).then_inc(dve_step, 1)
                dve.wait_ge(dve_step, done)
                for t in range(2):
                    ins = V.tensor_scalar(pick[:, t, :], const("iota"), cur[:, 1, t:t + 1], cur[:, 0, t:t + 1],
                                          ALU.is_equal, ALU.mult)
                ins.then_inc(pick_ready, 1)


            steps_before = dve_steps[0]

            def split_y(i, ago=0):
                for half in range(2):
                    b = EXPERT_JOB[f"y{half}"][0]
                    dve.wait_ge(y_rounded, i * 2 + (half + 1 - 2 * ago))
                    cols = slice(half * WIDE, (half + 1) * WIDE)
                    V.tensor_tensor(y_lo[:, cols], ps[b][:, :], y_hi[:, cols].bitcast(F32),
                                    ALU.subtract).then_inc(bank_drained[b], 1)

            def add_outputs(i, ago=0):
                dve.wait_ge(gates_taken, i + (1 - ago))
                for t in range(2):
                    for half in range(2):
                        name = f"sc{t}{half}"
                        b, n = expert_job(name, i, before=ago * EXPERT_USES[EXPERT_JOB[name][0]])
                        dve.wait_ge(bank_full[b], n)
                        a = acc[:, t, half * WIDE:(half + 1) * WIDE]
                        V.scalar_tensor_tensor(a, ps[b][:, :], gate_now[:, t:t + 1], a, ALU.mult,
                                               ALU.add).then_inc(bank_drained[b], 1)

            def expert(i, first_unit, add_last):
                def taken(name):
                    b, n = expert_job(name, i)
                    dve.wait_ge(bank_full[b], n)
                    return ps[b]

                for n, u in enumerate(EXPERT_UNITS):
                    if n >= first_unit:
                        split_expert_unit(n, i)
                    if n == SLOTS and add_last:
                        split_y(i, 1)
                    if n == 2 * SLOTS - 1 and add_last:
                        add_outputs(i, 1)
                    if n < SLOTS - 1:
                        continue
                    kind, s, q = EXPERT_UNITS[n - SLOTS + 1]
                    if kind == "up" and q == 3:
                        b, m = expert_job(f"gate{s}", i)
                        dve.wait_ge(bank_drained[b], m)
                        o = taken(f"up{s}")
                        V.tensor_tensor(hid[:, :], silu[:, :], o[:, :], ALU.mult).then_inc(
                            bank_drained[EXPERT_JOB[f"up{s}"][0]], 1)
                    t = turned(n) if turned(n) == EXP_STEPS - 1 else turned(n - 1)
                    if t is not None and (t < EXP_STEPS - 1 or turned(n) is not None):
                        o = taken(f"tr{t}")
                        dve.wait_ge(hid_rounded, i * EXP_STEPS + (t + 1))
                        V.tensor_tensor(hid_lo[:, t % 2, :, :], o[:, :].rearrange("p (m c) -> p m c", m=FF_PER_STEP),
                                        hid_hi[:, t % 2, :, :].bitcast(F32),
                                        ALU.subtract).then_inc(bank_drained[EXPERT_JOB[f"tr{t}"][0]], 1)
                    if (kind, s, q) == ("gate", 2, 3):
                        o = taken("pt")
                        V.tensor_copy(pick_t[:, :], o[:, 0:SEQ]).then_inc(bank_drained[EXPERT_JOB["pt"][0]], 1)
                        V.tensor_copy(gate_now[:, :], rv[:, 2, :, bass.ds(i, 1)].squeeze(2)).then_inc(gates_taken, 1)
                    if (kind, s, q) == ("gate", EXP_STEPS - 1, 0):
                        pick_tokens(rv[:, 0:2, :, bass.ds(i + 1, 1)].squeeze(3), i + (steps_before + 1))
                    if (kind, s, q) == ("down", EXP_STEPS - 2, 1):
                        for half in range(2):
                            o = taken(f"te{half}")
                            dve.wait_ge(te_rounded, i * 2 + (half + 3))
                            split_te(half, o, EXPERT_JOB[f"te{half}"][0])

            expert(0, SLOTS, False)
            with dve.Fori(1, N_EXPERTS) as e:
                expert(e, 0, True)
            split_y(N_EXPERTS - 1)
            add_outputs(N_EXPERTS - 1)
            count = dve.value_load(most[0:1, 0:1])
            with dve.If(count > CAP):
                with dve.Fori(N_EXPERTS, ROUNDS) as i:
                    expert(i, 0, False)
                    split_y(i)
                    add_outputs(i)

        @block.gpsimd
        def _(pool):
            G = nc.gpsimd
            pool_steps = [0]

            def split_unit(n):
                pool.wait_ge(unit_rounded, n + 1)
                G.tensor_tensor(t_lo[:, n % SLOTS, :], trunk_weights(n), t_hi[:, n % SLOTS, :].bitcast(F32),
                                ALU.subtract).then_inc(unit_split, 1)

            split_unit(0)
            drained(pool, ("dist",))
            pool.dma_start(dist_dram, dist[0:N_BIAS, :]).then_inc(dist_stored, 16)
            pool.wait_ge(dist_stored, 16)
            pool.dma_start(bias_rev, bass.AP(tensor=dist_dram.tensor, offset=0,
                                             ap=[[1, P], [N_DIST, N_BIAS], [1, T]])).then_inc(bias_loaded, 16)
            pool.wait_ge(bias_loaded, 16)

            def step(ins):
                pool_steps[0] += 1
                ins.then_inc(pool_step, 1)
                pool.wait_ge(pool_step, pool_steps[0])

            def later(dst, src, shift, rows=slice(0, P)):
                step(G.tensor_tensor(dst[rows, N_META:PADDED], src[rows, N_META:PADDED],
                                     src[rows, N_META - shift:PADDED - shift], ALU.add))

            low_half, high_half = slice(0, P // 2), slice(P // 2, P)
            for l in range(DEPTH):
                drained(pool, ("z", l, "uc1"))
                for buf in (pool_a, pool_b, pool_u[:, 0], pool_u[:, 1]):
                    ins = G.memset(buf[:, 0:N_META], 0.0)
                step(ins)
                for j in range(2):
                    u = pool_u[:, j, :]
                    inv = const("inv_count", j * T, T)
                    later(pool_a, u, 1)
                    if j == 0:
                        later(pool_b, pool_a, 2, high_half)
                    else:
                        later(pool_b, pool_a, 2)
                        later(pool_a, pool_b, 4)
                        later(pool_b, pool_a, 8, high_half)
                    G.tensor_tensor(pool_d[low_half, j, :], pool_a[low_half, N_META:PADDED], inv[low_half], ALU.mult)
                    step(G.tensor_tensor(pool_d[high_half, j, :], pool_b[high_half, N_META:PADDED], inv[high_half],
                                         ALU.mult))
                    G.tensor_tensor(pool_d[:, j, :], pool_d[:, j, :], u[:, N_META:PADDED],
                                    ALU.subtract).then_inc(pool_ready, 1)
                for n in range(2 * CHUNK_NO["out", l, 0], 2 * CHUNK_NO["out", l, 0] + SLOTS):
                    c = n // 2
                    pool.wait_ge(ring_full[c % TRUNK_RING], 16 * (c // TRUNK_RING + 1))
                    G.tensor_copy(t_hi[:, n % SLOTS, :], trunk_weights(n)).then_inc(unit_rounded, 1)
                    split_unit(n)


def bucket(n):
    exact = N_BUCKETS // 2
    if n < exact:
        return n
    large = exact + int(np.log(np.float32(n) / exact) / math.log(MAX_DISTANCE / exact) * (N_BUCKETS - exact))
    return min(large, N_BUCKETS - 1)


def shape_constants():
    c = np.zeros((P, N_CONST), np.float32)

    def put(name, v):
        at, n = CONST_COLS[name]
        c[:, at:at + n] = v

    i = np.arange(P)
    put("ident", np.eye(P))
    put("mean_d", np.full((P, P), 1.0 / D))
    put("mean64", (i[:, None] // HD == i[None] // HD) / HD)
    put("mean32", (i[:, None] // B_QK == i[None] // B_QK) / B_QK)
    put("flip", np.eye(P)[::-1])
    put("before", i[:, None] < i[None])
    put("ones", np.ones((P, P)))
    put("dup", np.concatenate([i[:, None] == HD * j + i[None] % HD for j in range(2)], 1))
    put("iota", np.arange(CAP)[None])
    put("iota8", np.arange(N_EXPERTS)[None])
    t = np.arange(T)
    w = np.array(POOL_WINDOWS)[np.arange(2 * P) // 64].reshape(2, P).T
    put("inv_count", (np.float32(1) / np.minimum(t[None, None] + 1, w[:, :, None]).astype(np.float32)).reshape(P, -1))
    put("eps", EPS)
    n = T - 1 - np.arange(N_DIST)
    b = np.array([bucket(max(x, 0)) for x in n])
    hot = (np.arange(N_BUCKETS)[:, None] == b[None]).astype(np.float32)
    seen = np.stack([(n >= 0) & (n < WINDOW)] * A_HEADS + [n >= 0] * B_HEADS)
    return c, hot, np.where(seen, 0.0, MASKED).astype(np.float32)


def pack_params(v):
    p = np.zeros((P, N_PARAM), np.float32)

    def put(name, a):
        at, n = PARAM_COLS[name]
        p[:, at:at + n] = a

    put("g_mix", v["g_mix"].reshape(DEPTH * KT, P).T)
    put("g_ffn", v["g_ffn"].reshape(DEPTH * KT, P).T)
    put("gain_a", np.tile(v["qk_gain_a"].reshape(DEPTH * 2, HD), (1, P // HD)).T)
    put("gain_b", np.tile(v["qk_gain_b"].reshape(DEPTH * 2, B_QK), (1, P // B_QK)).T)
    put("pool_scale", v["pool_scale"].reshape(DEPTH * 2, P).T)
    put("sinks", v["sinks"].reshape(1, -1))
    put("lam", v["diff_lambda"].reshape(1, -1))
    put("g_out", v["g_diff_out"].reshape(1, -1))
    w = np.zeros((2, HD, DEPTH, 2, 2, HD), np.float32)
    for g in range(2):
        w[g, :, :, :, g, :] = v["w_pool"].reshape(DEPTH, 2, 2, HD, HD)[:, :, g].transpose(2, 0, 1, 3)
    put("w_pool", w.reshape(P, -1))
    put("router", v["w_router"][0].reshape(KT, P, N_EXPERTS).transpose(1, 0, 2).reshape(P, -1))
    return p


def kernel(**inputs):
    import concourse.bacc as bacc
    from concourse.bass_utils import run_bass_kernel_spmd

    nc = bacc.Bacc("TRN2", target_bir_lowering=False, num_devices=1)
    v = {name: np.ascontiguousarray(a) for name, a in inputs.items()}
    consts, hot, mask_row = shape_constants()
    arrays, args = {}, []
    for name, a in (("x", v["x"]), ("meta_tokens", v["meta_tokens"]), ("rel_bias_table", v["rel_bias_table"]),
                    ("onehot", hot), ("mask_row", mask_row), ("consts", consts), ("params", pack_params(v)),
                    ("w_in", v["w_in"]), ("w_out", v["w_out"]), ("w_ffn_gate", v["w_ffn_gate"]),
                    ("w_ffn_up", v["w_ffn_up"]), ("w_ffn_down", v["w_ffn_down"]), ("w_exp_gate", v["w_exp_gate"]),
                    ("w_exp_up", v["w_exp_up"]), ("w_exp_down", v["w_exp_down"])):
        arrays[f"in_{name}"] = a
        args.append(nc.dram_tensor(f"in_{name}", a.shape, mybir.dt.from_np(a.dtype), kind="ExternalInput").ap())
    out = nc.dram_tensor("out_0", (1, SEQ, D), F32, kind="ExternalOutput").ap()
    dist_dram = nc.dram_tensor("dist_scratch", (N_BIAS, N_DIST), F32, kind="Internal").ap()
    build(nc, *args, out, dist_dram)
    r = run_bass_kernel_spmd(nc, [arrays], core_ids=[0])
    return r.results[0]["out_0"]
```
